# Optimizing a Trainium2 kernel written in Bass

```python
import math
import jax, jax.numpy as jnp
from jax import lax
import numpy as np

D_MODEL = 1024
BATCH = 1
SEQ = 512
DEPTH = 1

MIX_WIDTH = D_MODEL
ATT_WIDTH = MIX_WIDTH // 2
RWKV_WIDTH = MIX_WIDTH - ATT_WIDTH
HD_ATT = 64
H_ATT = ATT_WIDTH // HD_ATT
HD_RWKV = 64
H_RWKV = RWKV_WIDTH // HD_RWKV
Q_LORA = 256
KV_LATENT = 128
IDX_HEADS = 8
IDX_DIM = 64
TOPK_MAX = 256
Q_BLOCK = 128
NUM_BUCKETS = 32
MAX_DISTANCE = 128
DECAY_LORA = 64
AAA_LORA = 64
GATE_LORA = 160
GN_EPS = 64e-5
ATT_COLS = Q_LORA + KV_LATENT + IDX_DIM + IDX_HEADS
RWKV_COLS = 3 * RWKV_WIDTH + DECAY_LORA + AAA_LORA + GATE_LORA
IN_COLS = ATT_COLS + RWKV_COLS
D_FF = -(-8 * D_MODEL // 768) * 256
NORM_EPS = 1e-6


def rms_norm(x, gain):
    xf = x.astype(jnp.float32)
    y = xf * lax.rsqrt(jnp.mean(xf * xf, axis=-1, keepdims=True) + NORM_EPS)
    return (y * gain.astype(jnp.float32)).astype(x.dtype)

def t5_bucket(rel):
    max_exact = NUM_BUCKETS // 2
    nf = jnp.maximum(rel, 1).astype(jnp.float32)
    large = max_exact + (jnp.log(nf / max_exact) / math.log(MAX_DISTANCE / max_exact)
                         * (NUM_BUCKETS - max_exact)).astype(jnp.int32)
    large = jnp.minimum(large, NUM_BUCKETS - 1)
    return jnp.where(rel < max_exact, rel, large)

def dsa_attention(c_q, c_kv, idx_k_raw, idx_w_raw, q_norm, w_uq, w_idx_q, kv_norm, idx_k_norm, w_uk, w_uv, rel_bias):
    B, T, _ = c_q.shape
    topk = min(TOPK_MAX, T // 4)
    cq = rms_norm(c_q, q_norm)
    q = jnp.einsum('btr,rhd->bthd', cq, w_uq)
    q_abs = jnp.einsum('bthd,hcd->bthc', q, w_uk) * (HD_ATT ** -0.5)
    ckv = rms_norm(c_kv, kv_norm)
    iq = jnp.einsum('btr,rhd->bthd', cq, w_idx_q).astype(jnp.float32)
    ik = rms_norm(idx_k_raw, idx_k_norm).astype(jnp.float32)
    iw = idx_w_raw.astype(jnp.float32) * (IDX_HEADS ** -0.5 * IDX_DIM ** -0.5)
    s_pos = jnp.arange(T)

    def block(i):
        t0 = i * Q_BLOCK
        qi = lax.dynamic_slice_in_dim(iq, t0, Q_BLOCK, axis=1)
        wi = lax.dynamic_slice_in_dim(iw, t0, Q_BLOCK, axis=1)
        qa = lax.dynamic_slice_in_dim(q_abs, t0, Q_BLOCK, axis=1)
        t_pos = t0 + jnp.arange(Q_BLOCK)
        score = jnp.einsum('bth,bths->bts', wi, jax.nn.relu(jnp.einsum('bthd,bsd->bths', qi, ik)))
        causal = s_pos[None, :] <= t_pos[:, None]
        score = jnp.where(causal[None], score, -jnp.inf)
        _, sel = lax.top_k(score, topk)
        kv_sel = jax.vmap(lambda m, j: m[j])(ckv, sel)
        rel = t_pos[None, :, None] - sel
        bias = rel_bias[t5_bucket(jnp.maximum(rel, 0))]
        logits = (jnp.einsum('bthc,btkc->bthk', qa, kv_sel).astype(jnp.float32)
                  + jnp.moveaxis(bias, -1, 2).astype(jnp.float32))
        logits = jnp.where((rel >= 0)[:, :, None, :], logits, -jnp.inf)
        p = jax.nn.softmax(logits, axis=-1).astype(kv_sel.dtype)
        return jnp.einsum('bthk,btkc->bthc', p, kv_sel)

    o = lax.map(block, jnp.arange(T // Q_BLOCK))
    o = jnp.moveaxis(o, 0, 1).reshape(B, T, H_ATT, KV_LATENT)
    return jnp.einsum('bthc,hcd->bthd', o, w_uv).reshape(B, T, ATT_WIDTH)

def rwkv7_scan(r, w, k, v, a_vec, b_vec):
    B, T, H, N = r.shape

    def step(S, inp):
        r_t, w_t, k_t, v_t, a_t, b_t = inp
        sa = jnp.einsum('bhij,bhj->bhi', S, a_t)
        S = S * w_t[:, :, None, :] + sa[..., None] * b_t[:, :, None, :] + v_t[..., None] * k_t[:, :, None, :]
        return S, jnp.einsum('bhij,bhj->bhi', S, r_t)

    xs = tuple(jnp.moveaxis(z, 1, 0) for z in (r, w, k, v, a_vec, b_vec))
    _, y = lax.scan(step, jnp.zeros((B, H, N, N), jnp.float32), xs)
    return jnp.moveaxis(y, 0, 1)

def rwkv7_group(p, mu_shift, w0, w_decay_up, a0, w_aaa_up, w_gate_up, k_k, k_a, r_k, ln_x_gain, ln_x_bias):
    B, T, _ = p.shape
    dt = p.dtype
    p_prev = jnp.pad(p, ((0, 0), (1, 0), (0, 0)))[:, :T]
    p = p + mu_shift * (p_prev - p)
    splits = [RWKV_WIDTH, 2 * RWKV_WIDTH, 3 * RWKV_WIDTH, 3 * RWKV_WIDTH + DECAY_LORA, 3 * RWKV_WIDTH + DECAY_LORA + AAA_LORA]
    r, k, v, wd, ad, gd = jnp.split(p, splits, axis=-1)
    w_log = -jax.nn.softplus(-(w0 + jnp.tanh(wd) @ w_decay_up)) - 0.5
    decay = jnp.exp(-jnp.exp(w_log.astype(jnp.float32)))
    a = jax.nn.sigmoid(a0 + ad @ w_aaa_up)
    g = jax.nn.sigmoid(gd) @ w_gate_up
    hs = (B, T, H_RWKV, HD_RWKV)
    kk = (k * k_k).astype(jnp.float32).reshape(hs)
    kk = kk / jnp.maximum(jnp.linalg.norm(kk, axis=-1, keepdims=True), 1e-12)
    k = k * (1 + (a - 1) * k_a)
    rf = r.astype(jnp.float32).reshape(hs)
    kf = k.astype(jnp.float32).reshape(hs)
    vf = v.astype(jnp.float32).reshape(hs)
    af = a.astype(jnp.float32).reshape(hs)
    y = rwkv7_scan(rf, decay.reshape(hs), kf, vf, -kk, kk * af)
    mean = jnp.mean(y, axis=-1, keepdims=True)
    var = jnp.mean(jnp.square(y - mean), axis=-1, keepdims=True)
    y = ((y - mean) * lax.rsqrt(var + GN_EPS)).reshape(B, T, RWKV_WIDTH)
    y = y * ln_x_gain.astype(jnp.float32) + ln_x_bias.astype(jnp.float32)
    bonus = jnp.sum(rf * kf * r_k.astype(jnp.float32), axis=-1, keepdims=True) * vf
    y = (y + bonus.reshape(B, T, RWKV_WIDTH)) * g.astype(jnp.float32)
    return y.astype(dt)

def hybrid_layer(x, c, rel_bias, ada_w, ada_b, mix_pre_norm, mix_post_norm, ffn_pre_norm, ffn_post_norm,
                 w_in, q_norm, w_uq, w_idx_q, kv_norm, idx_k_norm, w_uk, w_uv,
                 mu_shift, w0, w_decay_up, a0, w_aaa_up, w_gate_up, k_k, k_a, r_k, ln_x_gain, ln_x_bias,
                 w_out, w_ffn_gate, w_ffn_up, w_ffn_down):
    mod = jax.nn.silu(c) @ ada_w + ada_b
    sh_m, sc_m, g_m, sh_f, sc_f, g_f = [m[:, None, :] for m in jnp.split(mod, 6, axis=-1)]
    h = rms_norm(x, mix_pre_norm) * (1 + sc_m) + sh_m
    proj = h @ w_in
    att_p, rwkv_p = proj[..., :ATT_COLS], proj[..., ATT_COLS:]
    c_q, c_kv, idx_k_raw, idx_w_raw = jnp.split(att_p, [Q_LORA, Q_LORA + KV_LATENT, Q_LORA + KV_LATENT + IDX_DIM], axis=-1)
    y_att = dsa_attention(c_q, c_kv, idx_k_raw, idx_w_raw, q_norm, w_uq, w_idx_q, kv_norm, idx_k_norm, w_uk, w_uv, rel_bias)
    y_rwkv = rwkv7_group(rwkv_p, mu_shift, w0, w_decay_up, a0, w_aaa_up, w_gate_up, k_k, k_a, r_k, ln_x_gain, ln_x_bias)
    mix = jnp.concatenate([y_att, y_rwkv], axis=-1) @ w_out
    x = x + g_m * rms_norm(mix, mix_post_norm)
    hf = rms_norm(x, ffn_pre_norm) * (1 + sc_f) + sh_f
    f = (jax.nn.silu(hf @ w_ffn_gate) * (hf @ w_ffn_up)) @ w_ffn_down
    return x + g_f * rms_norm(f, ffn_post_norm)

def first_inputs(seed: int = 0) -> dict:
    key = jax.random.key(seed)
    ks = jax.random.split(key, 40)
    f32 = jnp.float32
    L = DEPTH

    def nrm(k, shape, scale):
        return jax.random.normal(k, shape, f32) * scale

    def gain(k, n):
        return 1.0 + 0.05 * jax.random.normal(k, (L, n), f32)

    return {
        "x": jax.random.normal(ks[0], (BATCH, SEQ, D_MODEL), f32),
        "c": jax.random.normal(ks[1], (BATCH, D_MODEL), f32),
        "rel_bias": nrm(ks[2], (NUM_BUCKETS, H_ATT), 0.5),
        "ada_w": nrm(ks[3], (L, D_MODEL, 6 * D_MODEL), 0.5 * D_MODEL ** -0.5),
        "ada_b": nrm(ks[4], (L, 6 * D_MODEL), 0.02),
        "mix_pre_norm": gain(ks[5], D_MODEL),
        "mix_post_norm": gain(ks[6], D_MODEL),
        "ffn_pre_norm": gain(ks[7], D_MODEL),
        "ffn_post_norm": gain(ks[8], D_MODEL),
        "w_in": nrm(ks[9], (L, D_MODEL, IN_COLS), D_MODEL ** -0.5),
        "q_norm": gain(ks[10], Q_LORA),
        "w_uq": nrm(ks[11], (L, Q_LORA, H_ATT, HD_ATT), Q_LORA ** -0.5),
        "w_idx_q": nrm(ks[12], (L, Q_LORA, IDX_HEADS, IDX_DIM), Q_LORA ** -0.5),
        "kv_norm": gain(ks[13], KV_LATENT),
        "idx_k_norm": gain(ks[14], IDX_DIM),
        "w_uk": nrm(ks[15], (L, H_ATT, KV_LATENT, HD_ATT), KV_LATENT ** -0.5),
        "w_uv": nrm(ks[16], (L, H_ATT, KV_LATENT, HD_ATT), KV_LATENT ** -0.5),
        "mu_shift": jax.random.uniform(ks[17], (L, RWKV_COLS), f32),
        "w0": nrm(ks[18], (L, RWKV_WIDTH), 0.5),
        "w_decay_up": nrm(ks[19], (L, DECAY_LORA, RWKV_WIDTH), 0.1 * DECAY_LORA ** -0.5),
        "a0": nrm(ks[20], (L, RWKV_WIDTH), 0.1),
        "w_aaa_up": nrm(ks[21], (L, AAA_LORA, RWKV_WIDTH), 0.5 * AAA_LORA ** -0.5),
        "w_gate_up": nrm(ks[22], (L, GATE_LORA, RWKV_WIDTH), GATE_LORA ** -0.5),
        "k_k": 0.85 + 0.05 * jax.random.normal(ks[23], (L, RWKV_WIDTH), f32),
        "k_a": 1.0 + 0.05 * jax.random.normal(ks[24], (L, RWKV_WIDTH), f32),
        "r_k": nrm(ks[25], (L, H_RWKV, HD_RWKV), 0.1),
        "ln_x_gain": gain(ks[26], RWKV_WIDTH),
        "ln_x_bias": nrm(ks[27], (L, RWKV_WIDTH), 0.02),
        "w_out": nrm(ks[28], (L, MIX_WIDTH, D_MODEL), MIX_WIDTH ** -0.5),
        "w_ffn_gate": nrm(ks[29], (L, D_MODEL, D_FF), D_MODEL ** -0.5),
        "w_ffn_up": nrm(ks[30], (L, D_MODEL, D_FF), D_MODEL ** -0.5),
        "w_ffn_down": nrm(ks[31], (L, D_FF, D_MODEL), D_FF ** -0.5),
    }

def first_block(x, c, rel_bias, ada_w, ada_b, mix_pre_norm, mix_post_norm, ffn_pre_norm, ffn_post_norm,
              w_in, q_norm, w_uq, w_idx_q, kv_norm, idx_k_norm, w_uk, w_uv,
              mu_shift, w0, w_decay_up, a0, w_aaa_up, w_gate_up, k_k, k_a, r_k, ln_x_gain, ln_x_bias,
              w_out, w_ffn_gate, w_ffn_up, w_ffn_down):
    layer_params = (ada_w, ada_b, mix_pre_norm, mix_post_norm, ffn_pre_norm, ffn_post_norm,
                    w_in, q_norm, w_uq, w_idx_q, kv_norm, idx_k_norm, w_uk, w_uv,
                    mu_shift, w0, w_decay_up, a0, w_aaa_up, w_gate_up, k_k, k_a, r_k, ln_x_gain, ln_x_bias,
                    w_out, w_ffn_gate, w_ffn_up, w_ffn_down)
    for l in range(DEPTH):
        x = hybrid_layer(x, c, rel_bias, *[p[l] for p in layer_params])
    return x


DEPTH_2 = 2

CHUNK = 64
RMS_EPS = 1e-6
D_FF_2 = 2816
POOL_WINDOWS = (2, 4, 8, 16)
POOL_GROUP = D_MODEL // 8
POOL_WIDTH = POOL_GROUP * len(POOL_WINDOWS)
FOX_HEADS = 8
FOX_HEAD_DIM = D_MODEL // (2 * FOX_HEADS)
FOX_WIDTH = FOX_HEADS * FOX_HEAD_DIM
AB_IN = POOL_WIDTH + 3 * FOX_WIDTH + FOX_HEADS
AB_MIX = POOL_WIDTH + FOX_WIDTH
MLA_HEADS = 16
MLA_NOPE = 64
MLA_ROPE = 32
MLA_V = 64
MLA_Q_LORA = 256
MLA_KV_LORA = 128
MLA_IN = MLA_Q_LORA + MLA_KV_LORA + MLA_ROPE
ROPE_THETA = 10000.0
N_EVEN = (DEPTH_2 + 1) // 2
N_ODD = DEPTH_2 // 2


def rms_norm_2(x, g):
    xf = x.astype(jnp.float32)
    y = xf * lax.rsqrt(jnp.mean(xf * xf, axis=-1, keepdims=True) + RMS_EPS)
    return (y * g.astype(jnp.float32)).astype(x.dtype)

def swiglu(x, w_gate, w_up, w_down):
    return (jax.nn.silu(x @ w_gate) * (x @ w_up)) @ w_down

def rope_tables(positions):
    inv_freq = ROPE_THETA ** (-jnp.arange(0, MLA_ROPE, 2, dtype=jnp.float32) / MLA_ROPE)
    ang = positions.astype(jnp.float32)[..., None] * inv_freq
    return jnp.cos(ang), jnp.sin(ang)

def apply_rope(x, cos, sin):
    xf = x.astype(jnp.float32)
    half = xf.shape[-1] // 2
    x1, x2 = xf[..., :half], xf[..., half:]
    return jnp.concatenate([x1 * cos - x2 * sin, x2 * cos + x1 * sin], axis=-1).astype(x.dtype)

def blocked_attention(q, k, v, scale, chunk, log_decay=None):
    b, s, h, dk = q.shape
    dv = v.shape[-1]
    nb = s // Q_BLOCK
    q = q * scale
    qb = q.reshape(b, nb, Q_BLOCK, h, dk).transpose(1, 0, 2, 3, 4)
    k_chunk = jnp.arange(s) // chunk
    xs = (qb, jnp.arange(nb))
    if log_decay is not None:
        fk = log_decay.transpose(0, 2, 1)
        fqb = log_decay.reshape(b, nb, Q_BLOCK, h).transpose(1, 0, 3, 2)
        xs = xs + (fqb,)

    def attend(args):
        q_blk, blk = args[0], args[1]
        logits = jnp.einsum('bqhd,bkhd->bhqk', q_blk, k).astype(jnp.float32)
        if log_decay is not None:
            logits = logits + (args[2][..., None] - fk[:, :, None, :])
        t_pos = blk * Q_BLOCK + jnp.arange(Q_BLOCK)
        allowed = k_chunk[None, :] <= (t_pos // chunk)[:, None]
        logits = jnp.where(allowed, logits, -jnp.inf)
        p = jax.nn.softmax(logits, axis=-1)
        return jnp.einsum('bhqk,bkhd->bqhd', p.astype(v.dtype), v)

    out = lax.map(attend, xs)
    return out.transpose(1, 0, 2, 3, 4).reshape(b, s, h, dv)

def pool_mixer(u, w_pool, pool_scale):
    s = u.shape[1]
    cs = jnp.cumsum(u.astype(jnp.float32), axis=1)
    t_count = jnp.arange(s) + 1
    outs = []
    for g, w in enumerate(POOL_WINDOWS):
        lo, hi = g * POOL_GROUP, (g + 1) * POOL_GROUP
        cs_g = cs[..., lo:hi]
        lagged = jnp.pad(cs_g, ((0, 0), (w, 0), (0, 0)))[:, :s]
        count = jnp.minimum(t_count, w).astype(jnp.float32)[None, :, None]
        diff = (cs_g - lagged) / count - u[..., lo:hi].astype(jnp.float32)
        outs.append(diff.astype(u.dtype) @ w_pool[g])
    return jnp.concatenate(outs, axis=-1) * pool_scale

def pool_fox_mixer(h, w_in, b_forget, w_pool, pool_scale, w_out):
    b, s, _ = h.shape
    proj = h @ w_in
    o1 = POOL_WIDTH
    o2 = o1 + FOX_WIDTH
    o3 = o2 + FOX_WIDTH
    o4 = o3 + FOX_WIDTH
    u = proj[..., :o1]
    q = proj[..., o1:o2].reshape(b, s, FOX_HEADS, FOX_HEAD_DIM)
    k = proj[..., o2:o3].reshape(b, s, FOX_HEADS, FOX_HEAD_DIM)
    v = proj[..., o3:o4].reshape(b, s, FOX_HEADS, FOX_HEAD_DIM)
    f_logit = proj[..., o4:] + b_forget
    y_pool = pool_mixer(u, w_pool, pool_scale)
    log_f = jax.nn.log_sigmoid(f_logit.astype(jnp.float32))
    cum_log_f = jnp.cumsum(log_f, axis=1)
    y_fox = blocked_attention(q, k, v, FOX_HEAD_DIM ** -0.5, 1, cum_log_f)
    y = jnp.concatenate([y_pool, y_fox.reshape(b, s, FOX_WIDTH)], axis=-1)
    return y @ w_out

def mla_mixer(h, cos, sin, w_in, q_norm, kv_norm, w_q_b, w_kv_b, w_out):
    b, s, _ = h.shape
    proj = h @ w_in
    c_q = proj[..., :MLA_Q_LORA]
    c_kv = proj[..., MLA_Q_LORA:MLA_Q_LORA + MLA_KV_LORA]
    k_rope = apply_rope(proj[..., MLA_Q_LORA + MLA_KV_LORA:], cos, sin)
    q = (rms_norm_2(c_q, q_norm) @ w_q_b).reshape(b, s, MLA_HEADS, MLA_NOPE + MLA_ROPE)
    q_rope = apply_rope(q[..., MLA_NOPE:], cos[:, :, None, :], sin[:, :, None, :])
    qk = jnp.concatenate([q[..., :MLA_NOPE], q_rope], axis=-1)
    kv = (rms_norm_2(c_kv, kv_norm) @ w_kv_b).reshape(b, s, MLA_HEADS, MLA_NOPE + MLA_V)
    k = jnp.concatenate(
        [kv[..., :MLA_NOPE], jnp.broadcast_to(k_rope[:, :, None, :], (b, s, MLA_HEADS, MLA_ROPE))],
        axis=-1)
    v = kv[..., MLA_NOPE:]
    y = blocked_attention(qk, k, v, (MLA_NOPE + MLA_ROPE) ** -0.5, CHUNK)
    return y.reshape(b, s, MLA_HEADS * MLA_V) @ w_out

def second_inputs(seed: int = 0) -> dict:
    key = jax.random.key(seed)
    ks = jax.random.split(key, 20)

    def normal(k, shape, scale):
        return scale * jax.random.normal(k, shape, jnp.float32)

    x = normal(ks[0], (BATCH, SEQ, D_MODEL), 1.0)
    start = jax.random.randint(ks[1], (BATCH, 1), 0, 64, dtype=jnp.int32) * CHUNK
    positions = (start + jnp.arange(SEQ, dtype=jnp.int32)[None, :]).astype(jnp.int32)
    norm_ffn = 1.0 + normal(ks[2], (DEPTH_2, 2, D_MODEL), 0.05)
    norm_mix = 1.0 + normal(ks[3], (DEPTH_2, D_MODEL), 0.05)
    norm_final = 1.0 + normal(ks[4], (D_MODEL,), 0.05)
    ffn_w_gate = normal(ks[5], (DEPTH_2, 2, D_MODEL, D_FF_2), D_MODEL ** -0.5)
    ffn_w_up = normal(ks[6], (DEPTH_2, 2, D_MODEL, D_FF_2), D_MODEL ** -0.5)
    ffn_w_down = normal(ks[7], (DEPTH_2, 2, D_FF_2, D_MODEL), D_FF_2 ** -0.5)
    ab_w_in = normal(ks[8], (N_EVEN, D_MODEL, AB_IN), D_MODEL ** -0.5)
    ab_b_forget = jax.random.uniform(ks[9], (N_EVEN, FOX_HEADS), jnp.float32, 1.0, 6.0)
    pool_w = normal(ks[10], (N_EVEN, len(POOL_WINDOWS), POOL_GROUP, POOL_GROUP), POOL_GROUP ** -0.5)
    pool_scale = 1.0 + normal(ks[11], (N_EVEN, POOL_WIDTH), 0.1)
    ab_w_out = normal(ks[12], (N_EVEN, AB_MIX, D_MODEL), AB_MIX ** -0.5)
    mla_w_in = normal(ks[13], (N_ODD, D_MODEL, MLA_IN), D_MODEL ** -0.5)
    mla_q_norm = 1.0 + normal(ks[14], (N_ODD, MLA_Q_LORA), 0.05)
    mla_kv_norm = 1.0 + normal(ks[15], (N_ODD, MLA_KV_LORA), 0.05)
    mla_w_q_b = normal(ks[16], (N_ODD, MLA_Q_LORA, MLA_HEADS * (MLA_NOPE + MLA_ROPE)), MLA_Q_LORA ** -0.5)
    mla_w_kv_b = normal(ks[17], (N_ODD, MLA_KV_LORA, MLA_HEADS * (MLA_NOPE + MLA_V)), MLA_KV_LORA ** -0.5)
    mla_w_out = normal(ks[18], (N_ODD, MLA_HEADS * MLA_V, D_MODEL), (MLA_HEADS * MLA_V) ** -0.5)
    return {'x': x, 'positions': positions, 'norm_ffn': norm_ffn, 'norm_mix': norm_mix,
            'norm_final': norm_final, 'ffn_w_gate': ffn_w_gate, 'ffn_w_up': ffn_w_up,
            'ffn_w_down': ffn_w_down, 'ab_w_in': ab_w_in, 'ab_b_forget': ab_b_forget,
            'pool_w': pool_w, 'pool_scale': pool_scale, 'ab_w_out': ab_w_out,
            'mla_w_in': mla_w_in, 'mla_q_norm': mla_q_norm, 'mla_kv_norm': mla_kv_norm,
            'mla_w_q_b': mla_w_q_b, 'mla_w_kv_b': mla_w_kv_b, 'mla_w_out': mla_w_out}

def second_block(x, positions, norm_ffn, norm_mix, norm_final, ffn_w_gate, ffn_w_up, ffn_w_down,
              ab_w_in, ab_b_forget, pool_w, pool_scale, ab_w_out,
              mla_w_in, mla_q_norm, mla_kv_norm, mla_w_q_b, mla_w_kv_b, mla_w_out):
    cos, sin = rope_tables(positions)
    h = x
    for layer in range(DEPTH_2):
        h = h + 0.5 * swiglu(rms_norm_2(h, norm_ffn[layer, 0]), ffn_w_gate[layer, 0],
                             ffn_w_up[layer, 0], ffn_w_down[layer, 0])
        hn = rms_norm_2(h, norm_mix[layer])
        i = layer // 2
        if layer % 2 == 0:
            h = h + pool_fox_mixer(hn, ab_w_in[i], ab_b_forget[i], pool_w[i], pool_scale[i], ab_w_out[i])
        else:
            h = h + mla_mixer(hn, cos, sin, mla_w_in[i], mla_q_norm[i], mla_kv_norm[i],
                              mla_w_q_b[i], mla_w_kv_b[i], mla_w_out[i])
        h = h + 0.5 * swiglu(rms_norm_2(h, norm_ffn[layer, 1]), ffn_w_gate[layer, 1],
                             ffn_w_up[layer, 1], ffn_w_down[layer, 1])
    return rms_norm_2(h, norm_final)


def setup_inputs(seed=0):
    out = dict(first_inputs(seed))
    for name, value in second_inputs(seed + 1).items():
        if name != "x":
            out[name + "_2"] = value
    return out


def reference(
    x, c, rel_bias, ada_w, ada_b, mix_pre_norm, mix_post_norm, ffn_pre_norm, ffn_post_norm,
    w_in, q_norm, w_uq, w_idx_q, kv_norm, idx_k_norm, w_uk, w_uv, mu_shift, w0, w_decay_up, a0,
    w_aaa_up, w_gate_up, k_k, k_a, r_k, ln_x_gain, ln_x_bias, w_out, w_ffn_gate, w_ffn_up,
    w_ffn_down, positions_2, norm_ffn_2, norm_mix_2, norm_final_2, ffn_w_gate_2, ffn_w_up_2,
    ffn_w_down_2, ab_w_in_2, ab_b_forget_2, pool_w_2, pool_scale_2, ab_w_out_2, mla_w_in_2,
    mla_q_norm_2, mla_kv_norm_2, mla_w_q_b_2, mla_w_kv_b_2, mla_w_out_2,
):
    x = first_block(
        x, c, rel_bias, ada_w, ada_b, mix_pre_norm, mix_post_norm, ffn_pre_norm, ffn_post_norm,
        w_in, q_norm, w_uq, w_idx_q, kv_norm, idx_k_norm, w_uk, w_uv, mu_shift, w0, w_decay_up,
        a0, w_aaa_up, w_gate_up, k_k, k_a, r_k, ln_x_gain, ln_x_bias, w_out, w_ffn_gate,
        w_ffn_up, w_ffn_down,
    )
    return second_block(
        x, positions_2, norm_ffn_2, norm_mix_2, norm_final_2, ffn_w_gate_2, ffn_w_up_2,
        ffn_w_down_2, ab_w_in_2, ab_b_forget_2, pool_w_2, pool_scale_2, ab_w_out_2, mla_w_in_2,
        mla_q_norm_2, mla_kv_norm_2, mla_w_q_b_2, mla_w_kv_b_2, mla_w_out_2,
    )


_drawn_inputs = setup_inputs


def setup_inputs(seed=0):
    import zlib

    import numpy as np

    out = dict(_drawn_inputs(seed))
    spreads = {}
    factors = {'mix_post_norm': 2.98,
     'ffn_post_norm': 3.696,
     'q_norm': 4.289,
     'kv_norm': 4.446,
     'idx_k_norm': 4.831,
     'w_decay_up': 8.0,
     'a0': 3.581,
     'k_k': 8.0,
     'k_a': 3.007,
     'ln_x_gain': 4.314,
     'ln_x_bias': 8.0,
     'mla_q_norm_2': 8.0,
     'mla_kv_norm_2': 8.0}
    for name, (base, spread) in spreads.items():
        noise = np.random.default_rng([zlib.crc32(name.encode()), seed]).standard_normal(out[name].shape)
        drawn = base * np.exp(spread * noise) if base else spread * noise
        out[name] = __import__('jax').numpy.asarray(drawn.astype(out[name].dtype))
    for name, factor in factors.items():
        out[name] = (out[name] * factor).astype(out[name].dtype)
    return out
```

```python
import math
from contextlib import ExitStack

import numpy as np

import concourse.bass as bass
from concourse import mybir

F32 = mybir.dt.float32
I32 = mybir.dt.int32
ALU = mybir.AluOpType
ACT = mybir.ActivationFunctionType
AX = mybir.AxisListType

P = 128
T = 512
D = 1024
KD = D // P
F = 2816
KF = F // P
HD = 64
TB = T // P
C = 64
NCH = T // C
EPS = 1e-6
GN_EPS = 64e-5
BIG = 1e30
CAUSAL_FILL = -3.0e38
TAKEN = -3.3e38
TOPK = min(256, T // 4)
RING = 4
SLOT = 11 * 256
WC = 256

LEVELS = (1, 2, 4, 8, 16, 32)
CONST = {}
_at = 0
for _name, _n in (("ident", P), ("flip", P), ("ones", P), ("heads", P), ("first", P), ("first_t", P)) + tuple(
        (f"low{s}", P) for s in LEVELS[1:]) + (("strict", P), ("upto", C), ("causal", T),
                                           ("chunked", T), ("reset", T), ("eps", 4), ("freq", 2)):
    CONST[_name] = (_at, _at + _n)
    _at += _n
CONST_W = _at

ROWS_A = (("ada_b", 48), ("mix_pre_norm", 8), ("mix_post_norm", 8), ("ffn_pre_norm", 8), ("ffn_post_norm", 8),
          ("c", 8), ("q_norm", 2), ("kv_norm", 1), ("w0", 4), ("a0", 4), ("k_k", 4), ("k_a", 4), ("r_k", 4),
          ("ln_x_gain", 4), ("ln_x_bias", 4))
ROWS_B = (("norm_ffn_2", 32), ("norm_mix_2", 16), ("norm_final_2", 8), ("mla_q_norm_2", 2), ("mla_kv_norm_2", 1),
          ("pool_scale_2", 4), ("mu_rkv", 12), ("mu_wa", 1), ("mu_g", 1), ("mu_g2", 1), ("idx_k_norm", 1),
          ("ab_b_forget_2", 1))


def columns(rows, base):
    at, out = base, {}
    for name, n in rows:
        out[name] = at
        at += n
    return out, at


COL, _end = columns(ROWS_A, 0)
_colb, PAR_W = columns(ROWS_B, P)
COL.update(_colb)
N_A, N_B = sum(n for _, n in ROWS_A), sum(n for _, n in ROWS_B)

O_KV, O_IK, O_IW, O_R = 256, 384, 448, 456
O_WA = O_R + 3 * 512
O_G = O_WA + 128
IN_COLS = O_G + 160
AB_F = 2048
NEG_SQRT_E = -math.exp(-0.5)


class Plan:

    def __init__(self):
        self.segments, self.n, self.mark = {}, 0, 0
        self.order = []

    def add(self, name, count, src, marks=(2,)):
        per = [marks[r % len(marks)] for r in range(4)]
        s = {"name": name, "n0": self.n, "count": count, "src": src, "per": per, "mark0": self.mark}
        self.segments[name] = s
        self.order.append(s)
        self.n += count
        self.mark += sum(per[j % 4] for j in range(count))

    def used(self, n, q=0):
        s = [x for x in self.order if x["n0"] <= n][-1]
        j = n - s["n0"]
        return s["mark0"] + sum(s["per"][k % 4] for k in range(j + 1)) + sum(s["per"]) * q

    def tile(self, name, j, k, q=0):
        s = self.segments[name]
        return s["mark0"] + sum(s["per"][i % 4] for i in range(j)) + k + 1 + sum(s["per"]) * q


class Core:

    def __init__(self, nc, ctx, io, plan):
        self.nc, self.ctx, self.io, self.plan = nc, ctx, io, plan
        sb = lambda name, shape, dt=F32: ctx.enter_context(nc.sbuf_tensor(name, shape, dt))
        self.const = sb("const", [P, CONST_W])
        self.par = sb("par", [P, PAR_W])
        self.mod = sb("mod", [P, 48])
        self.coef = sb("coef", [P, 64])
        self.x = sb("x", [P, KD, T])
        self.h = sb("h", [P, KD, T])
        self.ring = sb("ring", [P, RING, SLOT])
        self.rstd = sb("rstd", [P, T])
        self.bank = [ctx.enter_context(nc.psum_tensor(f"bank{i}", [P, 512], F32)) for i in range(8)]
        self.loaded = [ctx.enter_context(nc.semaphore(f"chunk_loaded{i}")) for i in range(RING)]
        self.tiles_done = ctx.enter_context(nc.semaphore("tiles_done"))
        self.side_loaded = ctx.enter_context(nc.semaphore("side_loaded"))
        self.issued = 0

    def k(self, name):
        a, b = CONST[name]
        return self.const[:, a:b]

    def p(self, name, i=0):
        return self.par[:, COL[name] + i:COL[name] + i + 1]

    def stream(self, sp, upto):
        plan = self.plan
        upto = min(upto, plan.n)
        while self.issued < upto:
            n = self.issued
            s = [x for x in plan.order if x["n0"] <= n][-1]
            j, end = n - s["n0"], min(upto, s["n0"] + s["count"])
            rounds = (end - n) // RING
            if j % RING == 0 and rounds >= 2 and n >= RING:
                lag = [plan.used(n + r - RING) for r in range(RING)]
                steady = j >= RING
                if steady:
                    with sp.Fori(0, rounds) as i:
                        for r in range(RING):
                            sp.wait_ge(self.tiles_done, lag[r] + sum(s["per"]) * i)
                            self.load(sp, s, n + r, j // RING + i, r)
                    self.issued = n + RING * rounds
                    continue
            for m in range(n, min(n + RING - j % RING, end)):
                if m >= RING:
                    sp.wait_ge(self.tiles_done, plan.used(m - RING))
                self.load(sp, s, m, (m - s["n0"]) // RING, (m - s["n0"]) % RING)
                self.issued = m + 1

    def load(self, sp, s, n, q, r):
        src = s["src"](q, r)
        a, b = src.shape[1], src.shape[2]
        dst = self.ring[:, n % RING, 0:a * b].rearrange("p (a b) -> p a b", a=a)
        sp.dma_start(dst, src).then_inc(self.loaded[n % RING], 16)

    def chunk(self, pe, name, j, width, q=0):
        n = self.plan.segments[name]["n0"] + j
        pe.wait_ge(self.loaded[n % RING], 16 * (n // RING + 1) + 16 * q)
        k = SLOT // width
        return self.ring[:, n % RING, 0:k * width].rearrange("p (k n) -> p k n", n=width)

    def end_of(self, name):
        s = self.plan.segments[name]
        return s["n0"] + s["count"]


def product(pe, out, pairs, start=True, stop=True):
    for n, (a, b) in enumerate(pairs):
        last = pe.matmul(out, a, b, start=start and n == 0, stop=stop and n == len(pairs) - 1)
    return last


def stage(K, name):
    st = ExitStack()
    nc = K.nc
    mine = []

    def sem(n):
        mine.append(nc.alloc_semaphore(f"{name}_{n}"))
        return mine[-1]

    def give_back():
        for x in mine:
            nc.gpsimd.sem_clear(x)
            nc.release_semaphore(x)

    st.callback(give_back)
    st.sem = sem
    st.sb = lambda n, shape, dt=F32: st.enter_context(nc.sbuf_tensor(f"{name}_{n}", shape, dt))
    st.sems = lambda *ns: [sem(n) for n in ns]
    return st


def start_stage(K, xin_rows):
    nc, io = K.nc, K.io
    with stage(K, "start") as st:
        rows = st.sb("rows", [P, 2, P])
        xin = st.sb("xin", [P, TB, D])
        s_const, s_rows, s_x, s_zero, s_turned, s_copied = st.sems("const", "rows", "x", "zero", "turned", "copied")
        with nc.Block() as block:
            @block.sync
            def _(sp):
                sp.dma_start(K.const[:, :], io["const"]).then_inc(s_const, 16)
                for t in range(TB):
                    sp.dma_start(xin[:, t, :], io["x"][0, t * P:(t + 1) * P, :]).then_inc(s_x, 16)
                K.stream(sp, RING)

            @block.gpsimd
            def _(pool):
                pass

            @block.scalar
            def _(act):
                act.wait_ge(s_zero, 1)
                n = 0
                for which, group in enumerate((ROWS_A, ROWS_B)):
                    at = 0
                    for name, cnt in group:
                        for dst, src in param_rows(io, name, cnt, rows, which, at):
                            act.dma_start(dst, src).then_inc(s_rows, 16)
                            n += 1
                        at += cnt
                st.n_rows = n
                for k in range(1, KD, 2):
                    act.wait_ge(s_turned, 2 + k + 1)
                    nc.scalar.copy(K.x[:, k, :], K.bank[k][:, :])

            @block.vector
            def _(dve):
                nc.vector.memset(rows[:, :, :], 0.0).then_inc(s_zero, 1)
                dve.wait_ge(s_turned, 2)
                nc.vector.tensor_copy(K.par[:, 0:N_A], K.bank[0][:, 0:N_A])
                nc.vector.tensor_copy(K.par[:, P:P + N_B], K.bank[1][:, 0:N_B]).then_inc(s_copied, 1)
                for k in range(0, KD, 2):
                    dve.wait_ge(s_turned, 2 + k + 1)
                    nc.vector.tensor_copy(K.x[:, k, :], K.bank[k][:, :])

            @block.tensor
            def _(pe):
                pe.wait_ge(s_const, 16)
                pe.wait_ge(s_rows, 16 * st.n_rows)
                pe.transpose(K.bank[0][:, 0:N_A], rows[0:N_A, 0, :], K.k("ident")[0:N_A, 0:N_A]).then_inc(s_turned, 1)
                pe.transpose(K.bank[1][:, 0:N_B], rows[0:N_B, 1, :], K.k("ident")[0:N_B, 0:N_B]).then_inc(s_turned, 1)
                pe.wait_ge(s_x, 16 * TB)
                for k in range(KD):
                    if k == 0:
                        pe.wait_ge(s_copied, 1)
                    for t in range(TB):
                        last = pe.transpose(K.bank[k][:, t * P:(t + 1) * P], xin[:, t, k * P:(k + 1) * P], K.k("ident"))
                    last.then_inc(s_turned, 1)


def param_rows(io, name, cnt, rows, which, at):
    dst = rows[at:at + cnt, which, :]
    mu = io["mu_shift"]
    if name == "mu_rkv":
        return [(dst, mu[0:1, 0:1536].rearrange("a (n p) -> (a n) p", p=P))]
    if name == "mu_wa":
        return [(dst, mu[0:1, 1536:1664])]
    if name == "mu_g":
        return [(dst, mu[0:1, 1664:1792])]
    if name == "mu_g2":
        return [(dst[:, 0:32], mu[0:1, 1792:1824])]
    if name == "idx_k_norm":
        return [(dst[:, 0:64], io[name]), (dst[:, 64:128], io[name])]
    if name == "ab_b_forget_2":
        return [(dst[:, 0:8], io[name])]
    ap = io[name]
    if name == "norm_ffn_2":
        return [(dst, ap.rearrange("a b (n p) -> (a b n) p", p=P))]
    if name == "r_k":
        return [(dst, ap.rearrange("a (n h) d -> (a n) (h d)", h=2))]
    if len(ap.shape) == 1:
        return [(dst, ap.rearrange("(n p) -> n p", p=P))]
    return [(dst, ap.rearrange("a (n p) -> (a n) p", p=P))]


def mod_stage(K, name, first, n_chunks):
    nc = K.nc
    with stage(K, name) as st:
        s_silu, s_out = st.sems("silu", "out")
        with nc.Block() as block:
            @block.sync
            def _(sp):
                K.stream(sp, K.end_of(name) + RING)

            @block.scalar
            def _(act):
                if first == 0:
                    nc.scalar.activation(K.coef[:, 0:8], K.par[:, COL["c"]:COL["c"] + 8], ACT.Silu).then_inc(s_silu, 1)

            @block.vector
            def _(dve):
                dve.wait_ge(K.tiles_done, K.plan.used(K.end_of(name) - 1))
                a, b = first, first + 2 * n_chunks
                nc.vector.tensor_tensor(K.mod[:, a:b], K.bank[0][:, a:b], K.par[:, a:b], ALU.add)
                dve.drain()
                if first == 0:
                    nc.vector.scalar_tensor_tensor(K.coef[:, 8:16], K.mod[:, 8:16], 1.0,
                                                   K.par[:, COL["mix_pre_norm"]:COL["mix_pre_norm"] + 8], ALU.add, ALU.mult)
                else:
                    nc.vector.tensor_tensor(K.coef[:, 16:24], K.mod[:, 16:24],
                                            K.par[:, COL["mix_post_norm"]:COL["mix_post_norm"] + 8], ALU.mult)
                    nc.vector.scalar_tensor_tensor(K.coef[:, 24:32], K.mod[:, 32:40], 1.0,
                                                   K.par[:, COL["ffn_pre_norm"]:COL["ffn_pre_norm"] + 8], ALU.add, ALU.mult)
                    nc.vector.tensor_tensor(K.coef[:, 32:40], K.mod[:, 40:48],
                                            K.par[:, COL["ffn_post_norm"]:COL["ffn_post_norm"] + 8], ALU.mult)

            @block.tensor
            def _(pe):
                if first == 0:
                    pe.wait_ge(s_silu, 1)
                with pe.Fori(0, n_chunks // RING) as i:
                    for r in range(RING):
                        w = K.chunk(pe, name, r, WC, i)
                        for m in range(2):
                            out = K.bank[0][:, bass.ds(first + 2 * r + m + 2 * RING * i, 1)]
                            for k in range(KD):
                                last = pe.matmul(out, w[:, k, m * P:(m + 1) * P], K.coef[:, k:k + 1],
                                                 start=k == 0, stop=k == KD - 1)
                        last.then_inc(K.tiles_done, 1)


def norm_stage(K, name, src, n, width, write, sem_extra=None, eps_col=0, ones="ones", after=None):
    nc = K.nc
    with stage(K, name) as st:
        sq = st.sb("sq", [P, 2, T])
        s_sq, s_sum, s_root, s_w = st.sems("squared", "summed", "root", "written")
        with nc.Block() as block:
            @block.scalar
            def _(act):
                for i in range(n):
                    if i >= 2:
                        act.wait_ge(s_sum, i - 1)
                    nc.scalar.activation(sq[:, i % 2, :], src(i), ACT.Square).then_inc(s_sq, 1)
                act.wait_ge(s_sum, n)
                nc.scalar.activation(K.rstd[:, :], K.bank[7][:, :], ACT.Sqrt, bias=K.k("eps")[:, eps_col:eps_col + 1],
                                     scale=1.0 / width).then_inc(s_root, 1)
                if sem_extra == "shift":
                    for i in range(n):
                        act.wait_ge(s_w, i + 1)
                        write("act", i, act)

            @block.tensor
            def _(pe):
                for i in range(n):
                    pe.wait_ge(s_sq, i + 1)
                    pe.matmul(K.bank[7][:, :], K.k(ones), sq[:, i % 2, :], start=i == 0, stop=i == n - 1).then_inc(s_sum, 1)

            @block.vector
            def _(dve):
                dve.wait_ge(s_root, 1)
                nc.vector.reciprocal(K.rstd[:, :], K.rstd[:, :])
                dve.drain()
                for i in range(n):
                    w = write("dve", i, dve)
                    if sem_extra == "shift":
                        w.then_inc(s_w, 1)

            @block.sync
            def _(sp):
                K.stream(sp, K.issued)


def model_norm(K, name, gain, shift=None):
    nc = K.nc

    def write(engine, i, e):
        if engine == "dve":
            return nc.vector.scalar_tensor_tensor(K.h[:, i, :], K.x[:, i, :], gain(i), K.rstd[:, :], ALU.mult, ALU.mult)
        return nc.scalar.activation(K.h[:, i, :], K.h[:, i, :], ACT.Identity, bias=shift(i))

    norm_stage(K, name, lambda i: K.x[:, i, :], KD, D, write, sem_extra="shift" if shift else None)


def residual_norm(K, name, coef):
    nc = K.nc

    def write(engine, i, e):
        nc.vector.scalar_tensor_tensor(K.h[:, i, :], K.h[:, i, :], coef(i), K.rstd[:, :], ALU.mult, ALU.mult)
        e.drain()
        return nc.vector.tensor_tensor(K.x[:, i, :], K.x[:, i, :], K.h[:, i, :], ALU.add)

    norm_stage(K, name, lambda i: K.h[:, i, :], KD, D, write)


def ffn_stage(K, name, residual):
    nc, plan = K.nc, K.plan
    up, down = name + "_up", name + "_down"
    steps = F // WC
    with stage(K, name) as st:
        a = st.sb("act", [P, KF * T])
        g = st.sb("silu", [P, 4, T])
        s_gate, s_silu, s_act, s_free, s_out = st.sems("gate", "silu", "act", "free", "out")

        def pe_step(pe, q, par, step_par):
            for which in range(2):
                w = K.chunk(pe, up, 2 * par + which, WC, q)
                for m in range(2):
                    bank = 4 * step_par + 2 * which + m
                    pe.wait_ge(s_silu if which == 0 else s_act, 2 * par + m + 1 + 4 * q)
                    product(pe, K.bank[bank][:, :], [(w[:, k, m * P:(m + 1) * P], K.h[:, k, :]) for k in range(KD)]
                            ).then_inc(K.tiles_done, 1)

        def act_step(act, q, par):
            for m in range(2):
                act.wait_ge(K.tiles_done, plan.tile(up, 2 * par, m, q))
                act.wait_ge(s_act, 2 * par + m + 1 + 4 * q)
                nc.scalar.activation(g[:, 2 * par + m, :], K.bank[4 * par + m][:, :], ACT.Silu).then_inc(s_silu, 1)

        def dve_step(dve, q, par):
            for m in range(2):
                dve.wait_ge(K.tiles_done, plan.tile(up, 2 * par + 1, m, q))
                dve.wait_ge(s_silu, 4 + 2 * par + m + 1 + 4 * q)
                nc.vector.tensor_tensor(a[:, bass.ds((2 * par + m) * T + 4 * T * q, T)], g[:, 2 * par + m, :],
                                        K.bank[4 * par + 2 + m][:, :], ALU.mult).then_inc(s_act, 1)

        with nc.Block() as block:
            @block.sync
            def _(sp):
                K.stream(sp, K.end_of(down) + RING)

            @block.tensor
            def _(pe):
                with pe.Fori(0, steps // 2) as i:
                    for par in range(2):
                        pe_step(pe, i, par, par)
                pe_step(pe, steps // 2, 0, 0)
                pe.wait_ge(s_act, 4 + KF)
                pe.wait_ge(s_silu, 4 + KF)
                with pe.Fori(0, 2) as i:
                    for pair in range(2):
                        for half in range(2):
                            w = K.chunk(pe, down, 2 * pair + half, WC, i)
                            for m in range(2):
                                if half == 0:
                                    pe.wait_ge(s_free, 2 * pair + m + 1 + 4 * i)
                                last = product(pe, K.bank[4 + 2 * pair + m][:, :],
                                               [(w[:, f, m * P:(m + 1) * P], a[:, (11 * half + f) * T:(11 * half + f + 1) * T])
                                                for f in range(11)], start=half == 0, stop=half == 1)
                                if half == 1 or m == 1:
                                    last.then_inc(K.tiles_done, 1)

            @block.scalar
            def _(act):
                for _ in range(4):
                    act.sem_inc(s_silu, 1)
                with act.Fori(0, steps // 2) as i:
                    for par in range(2):
                        act_step(act, i, par)
                act_step(act, steps // 2, 0)

            @block.vector
            def _(dve):
                for _ in range(4):
                    dve.sem_inc(s_act, 1)
                    dve.sem_inc(s_free, 1)
                with dve.Fori(0, steps // 2) as i:
                    for par in range(2):
                        dve_step(dve, i, par)
                dve_step(dve, steps // 2, 0)
                with dve.Fori(0, 2) as i:
                    for pair in range(2):
                        for m in range(2):
                            dve.wait_ge(K.tiles_done, plan.tile(down, 2 * pair + 1, m, i))
                            n = 2 * pair + m + 4 * i
                            bank = K.bank[4 + 2 * pair + m][:, :]
                            if residual:
                                xo = K.x[:, bass.ds(n, 1), :].rearrange("p a t -> p (a t)")
                                nc.vector.scalar_tensor_tensor(xo, bank, 0.5, xo, ALU.mult, ALU.add).then_inc(s_free, 1)
                            else:
                                ho = K.h[:, bass.ds(n, 1), :].rearrange("p a t -> p (a t)")
                                nc.vector.tensor_copy(ho, bank).then_inc(s_free, 1)


def out_stage(K, name, y, residual):
    nc, plan = K.nc, K.plan
    with stage(K, name) as st:
        with nc.Block() as block:
            @block.sync
            def _(sp):
                K.stream(sp, K.end_of(name) + RING)

            @block.tensor
            def _(pe):
                for j in range(4):
                    w = K.chunk(pe, name, j, WC)
                    for m in range(2):
                        product(pe, K.bank[2 * j + m][:, :], [(w[:, k, m * P:(m + 1) * P], y(k)) for k in range(KD)]
                                ).then_inc(K.tiles_done, 1)

            @block.vector
            def _(dve):
                for n in range(KD):
                    dve.wait_ge(K.tiles_done, plan.tile(name, n // 2, n % 2))
                    if residual:
                        nc.vector.tensor_tensor(K.x[:, n, :], K.bank[n][:, :], K.x[:, n, :], ALU.add)
                    else:
                        nc.vector.tensor_copy(K.h[:, n, :], K.bank[n][:, :])


def finish_stage(K):
    nc = K.nc
    with stage(K, "finish") as st:
        out = st.sb("out", [P, TB, D])
        s_t, s_c, s_d = st.sems("turned", "copied", "stored")
        with nc.Block() as block:
            @block.tensor
            def _(pe):
                for t in range(TB):
                    for half in range(2):
                        for k in range(4):
                            last = pe.transpose(K.bank[2 * t + half][:, k * P:(k + 1) * P],
                                                K.h[:, 4 * half + k, t * P:(t + 1) * P], K.k("ident"))
                        last.then_inc(s_t, 1)

            @block.vector
            def _(dve):
                for n in range(2 * TB):
                    dve.wait_ge(s_t, n + 1)
                    nc.vector.tensor_copy(out[:, n // 2, (n % 2) * 512:(n % 2) * 512 + 512], K.bank[n][:, :]).then_inc(s_c, 1)

            @block.sync
            def _(sp):
                for t in range(TB):
                    sp.wait_ge(s_c, 2 * t + 2)
                    sp.dma_start(K.io["out"][0, t * P:(t + 1) * P, :], out[:, t, :]).then_inc(s_d, 16)
                sp.wait_ge(s_d, 16 * TB)


def in_proj_stage(K, M):
    nc, plan, io = K.nc, K.plan, K.io
    w_in = io["w_in"][0].rearrange("(k p) n -> p k n", p=P)
    with stage(K, "inproj") as st:
        wik = st.sb("wik", [P, KD, 2 * IDX_D])
        wiw = st.sb("wiw", [P, KD, 8])
        part = st.sb("part", [P, 2, T + 1])
        s_w, s_side, s_part, s_evac, s_zero = st.sems("side_in", "side", "part", "evac", "zero")
        tiles = [("in_q", 0, 0, P, None, M.cq[:, 0, :]), ("in_q", 0, P, P, None, M.cq[:, 1, :]),
                 ("in_kv", 0, 0, P, None, M.ckv[:, :])]
        for n in range(12):
            tiles.append(("in_rkv", n // 2, (n % 2) * P, P, n, M.rkv[:, n, :]))
        for n, (rows, dst) in enumerate(((P, M.wa[:, :]), (P, M.g[:, :]), (32, M.g2[:, :]))):
            tiles.append(("in_lora", 0, n * P, rows, 12 + n, dst))
        width = {"in_q": WC, "in_kv": P, "in_rkv": WC, "in_lora": 288}

        def signal(name, j, c0):
            return plan.tile(name, j, c0 // P)

        with nc.Block() as block:
            @block.sync
            def _(sp):
                for half in range(2):
                    sp.dma_start(wik[:, :, half * IDX_D:(half + 1) * IDX_D], w_in[:, :, O_IK:O_IW]).then_inc(s_w, 16)
                sp.dma_start(wiw[:, :, :], w_in[:, :, O_IW:O_R]).then_inc(s_w, 16)
                K.stream(sp, K.end_of("in_lora") + RING)

            @block.tensor
            def _(pe):
                for t, (name, j, c0, rows, _, _) in enumerate(tiles):
                    w = K.chunk(pe, name, j, width[name])
                    if t >= 6:
                        pe.wait_ge(s_evac, t - 5)
                    product(pe, K.bank[t % 6][0:rows, :], [(w[:, k, c0:c0 + rows], K.h[:, k, :]) for k in range(KD)]
                            ).then_inc(K.tiles_done, 1)
                pe.wait_ge(s_w, 48)
                product(pe, K.bank[6][:, :], [(wik[:, k, :], K.h[:, k, :]) for k in range(KD)]).then_inc(s_side, 1)
                for b in range(TB):
                    last = product(pe, K.bank[7][:, 8 * b:8 * b + 8],
                                   [(K.h[:, k, b * P:(b + 1) * P], wiw[:, k, :]) for k in range(KD)])
                last.then_inc(s_side, 1)

            @block.scalar
            def _(act):
                act.wait_ge(s_zero, 1)
                for t, (name, j, c0, rows, mu, _) in enumerate(tiles):
                    if mu is None:
                        continue
                    act.wait_ge(K.tiles_done, signal(name, j, c0))
                    if t >= 5:
                        act.wait_ge(s_evac, t - 1)
                    nc.scalar.activation(part[0:rows, t % 2, 1:T + 1], K.bank[t % 6][0:rows, :], ACT.Copy,
                                         scale=K.p("mu_rkv", mu)[0:rows, :]).then_inc(s_part, 1)

            @block.vector
            def _(dve):
                nc.vector.memset(part[:, :, 0:1], 0.0).then_inc(s_zero, 1)
                nc.vector.tensor_scalar(K.coef[:, 40:55], K.par[:, COL["mu_rkv"]:COL["mu_rkv"] + 15], -1.0, 1.0, ALU.mult, ALU.add)
                dve.drain()
                parts = 0
                for t, (name, j, c0, rows, mu, dst) in enumerate(tiles):
                    dve.wait_ge(K.tiles_done, signal(name, j, c0))
                    if mu is None:
                        nc.vector.tensor_copy(dst, K.bank[t % 6][:, :]).then_inc(s_evac, 1)
                    else:
                        parts += 1
                        dve.wait_ge(s_part, parts)
                        nc.vector.scalar_tensor_tensor(dst[0:rows, :], K.bank[t % 6][0:rows, :], K.coef[0:rows, 40 + mu:41 + mu],
                                                       part[0:rows, t % 2, 0:T], ALU.mult, ALU.add).then_inc(s_evac, 1)
                dve.wait_ge(s_side, 1)
                nc.vector.tensor_copy(M.ik[:, :], K.bank[6][:, :])
                dve.wait_ge(s_side, 2)
                nc.vector.tensor_scalar(M.iw[:, :], K.bank[7][:, 0:32], (8 * IDX_D) ** -0.5, None, ALU.mult)


IDX_D = 64


def small_norm(K, name, tiles, gains, width):
    nc = K.nc

    def write(engine, i, e):
        return nc.vector.scalar_tensor_tensor(tiles[i], tiles[i], gains[i], K.rstd[:, :], ALU.mult, ALU.mult)

    norm_stage(K, name, lambda i: tiles[i], len(tiles), width, write)


def dsa_prep_stage(K, A, M):
    nc, io = K.nc, K.io
    with stage(K, "dsaprep") as st:
        wuq = st.sb("wuq", [P, 2, 512])
        wiq = st.sb("wiq", [P, 2, 512])
        wuk = st.sb("wuk", [P, 512])
        wukt = st.sb("wukt", [P, 4, P])
        rb = st.sb("rb", [32, 8])
        bucket = st.sb("bucket", [32, 640])
        rev = st.sb("rev", [8, 640])
        shifted = A.o
        q = st.sb("q", [P, 4, T])
        far = nc.dram_tensor("bias_by_distance", (8, 640), F32, kind="Internal").ap()
        s_w, s_rb, s_rev, s_far, s_sh, s_pe, s_ev = st.sems("w", "rb", "rev", "far", "sh", "pe", "ev")
        steps = []

        def put(mms, evac):
            steps.append((mms, evac))

        idt = K.k("ident")
        put([(K.bank[0][0:8, :], rb[:, :], bucket[:, 0:512])], lambda: nc.scalar.copy(rev[:, 0:512], K.bank[0][0:8, :]))
        put([(K.bank[1][0:8, 0:128], rb[:, :], bucket[:, 512:640])],
            lambda: nc.scalar.activation(rev[:, 512:640], K.bank[1][0:8, 0:128], ACT.Copy, bias=-BIG, scale=0.0))
        n_rev = len(steps)
        put([(K.bank[2][:, n * P:(n + 1) * P], wuk[:, n * P:(n + 1) * P], None) for n in range(4)],
            lambda: nc.scalar.copy(wukt[:, :, :].rearrange("p a b -> p (a b)"), K.bank[2][:, :]))
        n_ukt = len(steps)
        put([(K.bank[3][:, b * P:(b + 1) * P], M.ckv[:, b * P:(b + 1) * P], None) for b in range(4)],
            lambda: nc.scalar.copy(A.ckvt[:, :, :].rearrange("p a b -> p (a b)"), K.bank[3][:, :]))
        for n in range(4):
            b = (4 + n) % 8
            put([(K.bank[b][:, :], wuq[:, k, n * P:(n + 1) * P], M.cq[:, k, :]) for k in range(2)],
                lambda n=n, b=b: nc.scalar.copy(q[:, n, :], K.bank[b][:, :]))
        n_q = len(steps)
        for n in range(4):
            put([(K.bank[n][:, :], wiq[:, k, n * P:(n + 1) * P], M.cq[:, k, :]) for k in range(2)],
                lambda n=n: nc.scalar.copy(A.iq[:, n, :], K.bank[n][:, :]))
        for h in range(8):
            r, b = slice((h % 2) * 64, (h % 2) * 64 + 64), (4 + h) % 8
            put([(K.bank[b][:, :], wukt[r, h // 2, :], q[r, h // 2, :])],
                lambda h=h, b=b: nc.scalar.mul(A.qa[:, h, :], K.bank[b][:, :], HD ** -0.5))
        n_flip = len(steps)
        for h in range(8):
            b = (4 + h) % 8
            put([(K.bank[b][:, :], K.k("flip"), shifted[:, h, :])],
                lambda h=h, b=b: nc.scalar.copy(A.bias[:, h, :], K.bank[b][:, :]))

        with nc.Block() as block:
            @block.sync
            def _(sp):
                sp.dma_start(rb[:, :], io["rel_bias"]).then_inc(s_rb, 16)
                sp.dma_start(bucket[:, :], io["bucket"]).then_inc(s_rb, 16)
                for h in range(8):
                    sp.dma_start(wuk[:, h * 64:(h + 1) * 64], io["w_uk"][0, h]).then_inc(s_w, 16)
                    sp.dma_start(A.wuv[:, h, :], io["w_uv"][0, h]).then_inc(s_w, 16)
                sp.dma_start(wuq[:, :, :], io["w_uq"][0].rearrange("(k p) h d -> p k (h d)", p=P)).then_inc(s_w, 16)
                sp.dma_start(wiq[:, :, :], io["w_idx_q"][0].rearrange("(k p) h d -> p k (h d)", p=P)).then_inc(s_w, 16)
                sp.wait_ge(s_ev, n_rev)
                sp.dma_start(far, rev[:, :]).then_inc(s_far, 16)
                sp.wait_ge(s_far, 16)
                sp.dma_start(shifted[:, :, :], bass.AP(tensor=far.tensor, offset=0, ap=[[1, P], [640, 8], [1, T]])).then_inc(s_sh, 16)

            @block.tensor
            def _(pe):
                pe.wait_ge(s_rb, 32)
                for n, (mms, _) in enumerate(steps):
                    if n == n_rev:
                        pe.wait_ge(s_w, 16 * 18)
                    if n == n_flip:
                        pe.wait_ge(s_sh, 16)
                    need = max(n_q if n >= n_q + 4 else 0, n - 3)
                    if need > 0:
                        pe.wait_ge(s_ev, need)
                    for m, (out, a, b) in enumerate(mms):
                        if b is None:
                            last = pe.transpose(out, a, idt)
                        else:
                            last = pe.matmul(out, a, b, start=m == 0, stop=m == len(mms) - 1)
                    last.then_inc(s_pe, 1)

            @block.scalar
            def _(act):
                for n, (_, evac) in enumerate(steps):
                    act.wait_ge(s_pe, n + 1)
                    evac().then_inc(s_ev, 1)


def topk_stage(K, A, M):
    nc = K.nc
    with stage(K, "topk") as st:
        relu = st.sb("relu", [P, 2, T])
        sc = st.sb("scores", [P, 3, T])
        top = st.sb("top", [P, 8])
        s_pe, s_relu, s_acc, s_done, s_mask = st.sems("dots", "relu", "acc", "scored", "masked")
        with nc.Block() as block:
            @block.tensor
            def _(pe):
                for i in range(1, TB):
                    n = (i + 1) * P
                    for h in range(8):
                        m = (i - 1) * 8 + h
                        r = slice((h % 2) * 64, (h % 2) * 64 + 64)
                        if m >= 4:
                            pe.wait_ge(s_relu, m - 3)
                        pe.matmul(K.bank[m % 4][:, 0:n], A.iq[r, h // 2, i * P:(i + 1) * P], M.ik[r, 0:n],
                                  start=True, stop=True).then_inc(s_pe, 1)

            @block.scalar
            def _(act):
                for m in range(24):
                    n = (m // 8 + 2) * P
                    act.wait_ge(s_pe, m + 1)
                    if m >= 2:
                        act.wait_ge(s_acc, m - 1)
                    nc.scalar.activation(relu[:, m % 2, 0:n], K.bank[m % 4][:, 0:n], ACT.Relu).then_inc(s_relu, 1)

            @block.gpsimd
            def _(pool):
                for i in range(1, TB):
                    pool.wait_ge(s_done, i)
                    part = sc[:, i - 1, i * P:(i + 1) * P]
                    nc.gpsimd.affine_select(out=part, in_=part, compare_op=ALU.is_ge, fill=CAUSAL_FILL, base=0,
                                            pattern=[[-1, P]], channel_multiplier=1).then_inc(s_mask, 1)

            @block.vector
            def _(dve):
                for m in range(24):
                    i, h = m // 8 + 1, m % 8
                    n = (i + 1) * P
                    dve.wait_ge(s_relu, m + 1)
                    acc, w = sc[:, i - 1, 0:n], M.iw[:, 8 * i + h:8 * i + h + 1]
                    if h == 0:
                        ins = nc.vector.tensor_scalar(acc, relu[:, m % 2, 0:n], w, None, ALU.mult)
                    else:
                        ins = nc.vector.scalar_tensor_tensor(acc, relu[:, m % 2, 0:n], w, acc, ALU.mult, ALU.add)
                    ins.then_inc(s_acc, 1)
                    if h == 7:
                        dve.drain()
                        dve.sem_inc(s_done, 1)
                    else:
                        dve.drain()
                for i in range(1, TB):
                    n = (i + 1) * P
                    buf = sc[:, i - 1, 0:n]
                    dve.wait_ge(s_mask, i)
                    for _ in range(TOPK // 8):
                        nc.vector.max(top[:, :], buf)
                        dve.drain()
                        nc.vector.match_replace(buf, top[:, :], buf, TAKEN)
                        dve.drain()
                    nc.vector.tensor_scalar(A.mask[:, i - 1, 0:n], buf, TAKEN, -BIG, ALU.not_equal, ALU.mult)


def attention_stage(K, name, H, rows, q, k, v, vw, dest, bias=None, prep=None):
    nc = K.nc
    items = [(h, i) for h in range(H) for i in range(TB)]
    N = len(items)
    with stage(K, name) as st:
        S = st.sb("S", [P, 3, T])
        pt = st.sb("pt", [P, 2, T])
        bm = st.sb("bm", [P, 2, T]) if prep else None
        stat = st.sb("stat", [P, 4, 4])
        s_score, s_bm, s_biased, s_exp, s_norm, s_turned, s_pt, s_pv, s_out = st.sems(
            "scored", "bias_made", "biased", "exp", "normed", "turned", "probs_out", "pv", "out")
        lo = lambda h: (h % 2) * 64 if vw == 64 else 0
        with nc.Block() as block:
            @block.sync
            def _(sp):
                pass

            @block.tensor
            def _(pe):
                for n in range(N + 2):
                    if n < N:
                        h, i = items[n]
                        if n >= 2:
                            pe.wait_ge(s_biased, n - 1)
                        w = (i + 1) * P
                        pe.matmul(K.bank[n % 2][:, 0:w], q(h, i), k(h, w), start=True, stop=True).then_inc(s_score, 1)
                    if 1 <= n <= N:
                        m = n - 1
                        h, i = items[m]
                        pe.wait_ge(s_norm, m + 1)
                        if m >= 2:
                            pe.wait_ge(s_pt, m - 1)
                        for s in range(i + 1):
                            last = pe.transpose(K.bank[2 + m % 2][:, s * P:(s + 1) * P], S[:, m % 3, s * P:(s + 1) * P], K.k("ident"))
                        last.then_inc(s_turned, 1)
                    if n >= 2:
                        m = n - 2
                        h, i = items[m]
                        pe.wait_ge(s_pt, m + 1)
                        if m >= 2:
                            pe.wait_ge(s_out, m - 1)
                        product(pe, K.bank[4 + m % 2][lo(h):lo(h) + vw, 0:P],
                                [(v(h, s), pt[:, m % 2, s * P:(s + 1) * P]) for s in range(i + 1)]).then_inc(s_pv, 1)

            @block.gpsimd
            def _(pool):
                if prep:
                    for n, (h, i) in enumerate(items):
                        if n >= 2:
                            pool.wait_ge(s_biased, n - 1)
                        prep(pool, bm[:, n % 2, 0:(i + 1) * P], h, i).then_inc(s_bm, 1)

            @block.vector
            def _(dve):
                for n in range(N + 1):
                    if n < N:
                        h, i = items[n]
                        w = (i + 1) * P
                        dve.wait_ge(s_score, n + 1)
                        if prep:
                            dve.wait_ge(s_bm, n + 1)
                        if n >= 3:
                            dve.wait_ge(s_turned, n - 2)
                        table = bm[:, n % 2, 0:w] if prep else bias(h, i)
                        nc.vector.tensor_tensor_reduce(out=S[:, n % 3, 0:w], in0=K.bank[n % 2][:, 0:w], in1=table, scale=1.0,
                                                       scalar=-3.0e38, op0=ALU.add, op1=ALU.max, accum_out=stat[:, n % 4, 0:1])
                        dve.drain()
                        nc.vector.tensor_scalar(stat[:, n % 4, 1:2], stat[:, n % 4, 0:1], -1.0, None, ALU.mult).then_inc(s_biased, 1)
                    if n >= 1:
                        m = n - 1
                        w = (items[m][1] + 1) * P
                        dve.wait_ge(s_exp, m + 1)
                        nc.vector.reciprocal(stat[:, m % 4, 3:4], stat[:, m % 4, 2:3])
                        dve.drain()
                        nc.vector.tensor_scalar(S[:, m % 3, 0:w], S[:, m % 3, 0:w], stat[:, m % 4, 3:4], None, ALU.mult).then_inc(s_norm, 1)

            @block.scalar
            def _(act):
                for n in range(N + 2):
                    if n < N:
                        w = (items[n][1] + 1) * P
                        act.wait_ge(s_biased, n + 1)
                        nc.scalar.activation(S[:, n % 3, 0:w], S[:, n % 3, 0:w], ACT.Exp, bias=stat[:, n % 4, 1:2], scale=1.0,
                                             accum_out=stat[:, n % 4, 2:3]).then_inc(s_exp, 1)
                    if 1 <= n <= N:
                        m = n - 1
                        w = (items[m][1] + 1) * P
                        act.wait_ge(s_turned, m + 1)
                        if m >= 2:
                            act.wait_ge(s_pv, m - 1)
                        nc.scalar.copy(pt[:, m % 2, 0:w], K.bank[2 + m % 2][:, 0:w]).then_inc(s_pt, 1)
                    if n >= 2:
                        m = n - 2
                        h, i = items[m]
                        act.wait_ge(s_pv, m + 1)
                        nc.scalar.copy(dest(h, i), K.bank[4 + m % 2][lo(h):lo(h) + vw, 0:P]).then_inc(s_out, 1)


def value_stage(K, A, y):
    nc = K.nc
    with stage(K, "value") as st:
        s_pe, = st.sems("pe")
        with nc.Block() as block:
            @block.tensor
            def _(pe):
                for h in range(8):
                    pe.matmul(K.bank[h // 2][(h % 2) * 64:(h % 2) * 64 + 64, :], A.wuv[:, h, :], A.o[:, h, :],
                              start=True, stop=True).then_inc(s_pe, 1)

            @block.vector
            def _(dve):
                for n in range(4):
                    dve.wait_ge(s_pe, 2 * n + 2)
                    nc.vector.tensor_copy(y[:, n, :], K.bank[n][:, :])


class Bag:
    pass


def mixer1(K):
    nc = K.nc
    with ExitStack() as st:
        sb = lambda n, shape: st.enter_context(nc.sbuf_tensor(n, shape, F32))
        M = Bag()
        y = sb("y", [P, KD, T])
        M.cq, M.ckv, M.ik, M.iw = sb("cq", [P, 2, T]), sb("ckv", [P, T]), sb("ik", [P, T]), sb("iw", [P, 32])
        with ExitStack() as rs:
            rb = lambda n, shape: rs.enter_context(nc.sbuf_tensor(n, shape, F32))
            M.rkv, M.wa, M.g, M.g2 = rb("rkv", [P, 12, T]), rb("wa", [P, T]), rb("g", [P, T]), rb("g2", [32, T])
            in_proj_stage(K, M)
            rwkv(K, M, y)
        with ExitStack() as as_:
            ab = lambda n, shape: as_.enter_context(nc.sbuf_tensor(n, shape, F32))
            A = Bag()
            A.qa = K.h
            A.iq, A.ckvt, A.bias = ab("iq", [P, 4, T]), ab("ckvt", [P, TB, P]), ab("bias", [P, 8, T])
            A.o, A.wuv, A.mask = ab("o", [P, 8, T]), ab("wuv", [P, 8, 64]), ab("mask", [P, 3, T])
            small_norm(K, "norm_q", [M.cq[:, 0, :], M.cq[:, 1, :]], [K.p("q_norm", 0), K.p("q_norm", 1)], 256)
            small_norm(K, "norm_kv", [M.ckv[:, :]], [K.p("kv_norm")], 128)
            small_norm(K, "norm_ik", [M.ik[:, :]], [K.p("idx_k_norm")], 128)
            dsa_prep_stage(K, A, M)
            topk_stage(K, A, M)

            def prep(pool, out, h, i):
                w = (i + 1) * P
                table = A.bias[:, h, 384 - i * P:384 - i * P + w]
                if i == 0:
                    return nc.gpsimd.tensor_copy(out, table)
                return nc.gpsimd.tensor_tensor(out, table, A.mask[:, i - 1, 0:w], ALU.add)

            attention_stage(K, "dsa", 8, P, lambda h, i: A.qa[:, h, i * P:(i + 1) * P], lambda h, w: M.ckv[:, 0:w],
                            lambda h, s: A.ckvt[:, s, :], P, lambda h, i: A.o[:, h, i * P:(i + 1) * P], prep=prep)
            value_stage(K, A, y)
        mod_stage(K, "mod2", 16, 16)
        out_stage(K, "out1", lambda k: y[:, k, :], False)


def rwkv_prep_stage(K, M, R, p):
    nc, io = K.nc, K.io
    r, k, v = M.rkv[:, p, :], M.rkv[:, 4 + p, :], M.rkv[:, 8 + p, :]
    tmp = lambda i: K.h[:, i, :]
    lw, L, a, kk, t0, eN, eA, eC = (tmp(i) for i in range(8))
    chunks = lambda ap: ap.rearrange("p (c t) -> p c t", t=C)
    with stage(K, f"rprep{p}") as st:
        s_w, s_lora, s_dots, s_sig, s_kk, s_sq, s_norm, s_root, s_l, s_exp, s_bd, s_zero = st.sems(
            "w", "lora", "dots", "sigmoid", "kk", "square", "norm", "root", "logs", "exp", "scaled", "zero")
        with nc.Block() as block:
            @block.sync
            def _(sp):
                if p == 0:
                    sp.dma_start(R.wl[0:64, :], io["w_decay_up"][0]).then_inc(s_w, 16)
                    sp.dma_start(R.wl[64:128, :], io["w_aaa_up"][0]).then_inc(s_w, 16)

            @block.tensor
            def _(pe):
                if p == 0:
                    pe.wait_ge(s_w, 32)
                    pe.wait_ge(s_lora, 1)
                pe.matmul(K.bank[0][:, :], R.wl[0:64, p * P:(p + 1) * P], M.wa[0:64, :], start=True, stop=True).then_inc(s_dots, 1)
                pe.matmul(K.bank[1][:, :], R.wl[64:128, p * P:(p + 1) * P], M.wa[64:128, :], start=True, stop=True).then_inc(s_dots, 1)
                pe.wait_ge(s_sq, 1)
                pe.matmul(K.bank[2][:, :], K.k("heads"), t0, start=True, stop=True).then_inc(s_norm, 1)

            @block.scalar
            def _(act):
                if p == 0:
                    nc.scalar.activation(M.wa[0:64, :], M.wa[0:64, :], ACT.Tanh).then_inc(s_lora, 1)
                    nc.scalar.activation(M.g[:, :], M.g[:, :], ACT.Sigmoid)
                    nc.scalar.activation(M.g2[:, :], M.g2[:, :], ACT.Sigmoid)
                act.wait_ge(s_dots, 1)
                nc.scalar.activation(lw, K.bank[0][:, :], ACT.Sigmoid, bias=K.p("w0", p)).then_inc(s_sig, 1)
                act.wait_ge(s_dots, 2)
                nc.scalar.activation(a, K.bank[1][:, :], ACT.Sigmoid, bias=K.p("a0", p)).then_inc(s_sig, 1)
                act.wait_ge(s_kk, 1)
                nc.scalar.activation(t0, kk, ACT.Square).then_inc(s_sq, 1)
                act.wait_ge(s_norm, 1)
                nc.scalar.activation(t0, K.bank[2][:, :], ACT.Sqrt).then_inc(s_root, 1)
                act.wait_ge(s_l, 1)
                nc.scalar.activation(eA, eA, ACT.Exp).then_inc(s_exp, 1)
                nc.scalar.activation(eN, L, ACT.Exp, scale=-1.0).then_inc(s_exp, 1)
                nc.scalar.activation(eC, eC, ACT.Exp).then_inc(s_exp, 1)
                nc.scalar.activation(R.eP[:, :], L, ACT.Exp).then_inc(s_exp, 1)

            @block.gpsimd
            def _(pool):
                if p == 0:
                    for n in range(6):
                        nc.gpsimd.memset(R.bd[:, n, :, :], 0.0)
                    pool.drain().then_inc(s_zero, 1)
                    pool.wait_ge(s_zero, 1)
                for hh in range(2):
                    q = slice(64 * hh, 64 * hh + 64)
                    nc.gpsimd.tensor_copy(R.bd[q, 5, :, q], chunks(v)[q])
                pool.wait_ge(s_bd, 1)
                pool.wait_ge(s_exp, 3)
                for hh in range(2):
                    q = slice(64 * hh, 64 * hh + 64)
                    nc.gpsimd.tensor_tensor(R.bd[q, 3, :, q], chunks(k)[q], chunks(eC)[q], ALU.mult)
                    nc.gpsimd.tensor_tensor(R.bd[q, 4, :, q], chunks(a)[q], chunks(eC)[q], ALU.mult)

            @block.vector
            def _(dve):
                nc.vector.tensor_scalar(kk, k, K.p("k_k", p), None, ALU.mult).then_inc(s_kk, 1)
                nc.vector.tensor_scalar(R.oka[:, :], K.p("k_a", p), -1.0, 1.0, ALU.mult, ALU.add)
                dve.wait_ge(s_sig, 1)
                nc.vector.tensor_scalar(lw, lw, NEG_SQRT_E, None, ALU.mult)
                dve.drain()
                nc.vector.tensor_tensor_scan(L, K.k("reset"), lw, 0.0, ALU.mult, ALU.add)
                dve.drain()
                nc.vector.tensor_tensor(eA, L, lw, ALU.subtract)
                end = chunks(L)[:, :, C - 1:C].broadcast_to([P, NCH, C])
                nc.vector.tensor_tensor(chunks(eC), end, chunks(L), ALU.subtract).then_inc(s_l, 1)
                dve.wait_ge(s_root, 1)
                nc.vector.tensor_scalar(t0, t0, 1e-12, None, ALU.max)
                dve.drain()
                nc.vector.reciprocal(t0, t0)
                dve.drain()
                nc.vector.scalar_tensor_tensor(kk, kk, -1.0, t0, ALU.mult, ALU.mult)
                dve.drain()
                dve.wait_ge(s_sig, 2)
                nc.vector.tensor_scalar(t0, a, K.p("k_a", p), R.oka[:, :], ALU.mult, ALU.add)
                dve.drain()
                nc.vector.tensor_tensor(k, k, t0, ALU.mult)
                nc.vector.scalar_tensor_tensor(a, kk, -1.0, a, ALU.mult, ALU.mult)
                dve.drain().then_inc(s_bd, 1)
                if p == 0:
                    dve.wait_ge(s_zero, 1)
                dve.wait_ge(s_exp, 1)
                for n, (x, e) in enumerate(((kk, eA), (a, eN), (k, eN))):
                    if n == 1:
                        dve.wait_ge(s_exp, 2)
                    for hh in range(2):
                        q = slice(64 * hh, 64 * hh + 64)
                        nc.vector.tensor_tensor(R.bd[q, n, :, q], chunks(x)[q], chunks(e)[q], ALU.mult)
                dve.wait_ge(s_exp, 4)
                nc.vector.tensor_tensor(R.rt[:, :], r, R.eP[:, :], ALU.mult)


def rwkv_chunk_stage(K, R, p, yout):
    nc = K.nc
    BD_A, BD_B, BD_K, BD_KH, BD_BH, BD_V = range(6)
    idt = K.k("ident")
    wide = lambda ap: ap.unsqueeze(1).broadcast_to([P, 4, P])
    with stage(K, f"rchunk{p}") as st:
        G = []
        for g in range(2):
            B = Bag()
            B.vt, B.kht, B.bht = (K.h[:, 2 + 3 * g + n, :].rearrange("p (c t) -> p c t", t=P) for n in range(3))
            B.at, B.akt, B.nt, B.T, B.TT, B.X, B.rbk = (
                st.sb(f"{n}{g}", [P, 4, P]) for n in ("at", "akt", "nt", "t", "tt", "x", "rbk"))
            G.append(B)
        S = st.sb("state", [P, 2, P])
        s_pe, s_dve, s_act, s_sp, s_sv = st.sems("products", "vector_out", "scalar_out", "state_product", "state")
        steps = []

        def flat(t):
            return t[:, :, :].rearrange("p a b -> p (a b)")

        def add(g, mms, evacs):
            steps.append((g, mms, evacs))

        def group_steps(g):
            B = G[g]
            b0 = 4 * g
            bd = lambda n, c: R.bd[:, n, 4 * g + c, :]
            rt = lambda c: R.rt[:, (4 * g + c) * C:(4 * g + c + 1) * C]
            out = []

            def put(mms, evacs):
                out.append((g, mms, evacs))

            def full(lhs, rhs, bank, w=P, at=0, more=None):
                ms = []
                for c in range(4):
                    o = K.bank[bank][:, c * P + at:c * P + at + w]
                    ms.append((o, lhs(c), rhs(c), True, more is None))
                    if more:
                        ms.append((o, more[0](c), more[1](c), False, True))
                return ms

            def turn(n, bank):
                return [(K.bank[bank][:, c * P:(c + 1) * P], bd(n, c), None, True, True) for c in range(4)]

            v = nc.vector
            a = nc.scalar
            bank = lambda n: K.bank[b0 + n][:, :]
            bank3 = lambda n: K.bank[b0 + n][:, :].rearrange("p (c t) -> p c t", t=P)
            sl = lambda t: (lambda c: t[:, c, :])
            put(full(lambda c: bd(BD_B, c), lambda c: bd(BD_A, c), b0),
                [("dve", lambda: v.tensor_tensor(B.nt[:, :, :], bank3(0), wide(K.k("strict")), ALU.mult)),
                 ("dve", lambda: v.tensor_tensor(B.TT[:, :, :], bank3(0), wide(K.k("first_t")), ALU.mult))])
            put(full(lambda c: bd(BD_A, c), lambda c: bd(BD_B, c), b0 + 1),
                [("dve", lambda: v.tensor_tensor(B.T[:, :, :], bank3(1), wide(K.k("first")), ALU.mult)),
                 ("dve", lambda: v.tensor_tensor(B.TT[:, :, :], B.TT[:, :, :], wide(idt), ALU.add)),
                 ("drain", None),
                 ("dve", lambda: v.tensor_tensor(B.T[:, :, :], B.T[:, :, :], wide(idt), ALU.add))])
            turns = [(BD_V, B.vt), (BD_KH, B.kht), (BD_BH, B.bht), (BD_A, B.at)]
            extra = []
            for m, (n, dst) in enumerate(turns):
                extra.append((g, turn(n, b0 + 3), [("act", lambda dst=dst: a.copy(flat(dst), bank(3)))]))
            extra.append((g, full(lambda c: bd(BD_K, c), lambda c: bd(BD_A, c), b0 + 3),
                [("dve", lambda: v.tensor_tensor(B.akt[:, :, :], bank3(3), wide(K.k("strict")), ALU.mult))]))
            up = K.k("upto").unsqueeze(1).broadcast_to([P, 8, C])
            extra.append((g, full(lambda c: bd(BD_B, c), rt, b0 + 3, C) + full(lambda c: bd(BD_K, c), rt, b0 + 3, C, C),
                [("dve", lambda: v.tensor_tensor(B.rbk[:, :, :].rearrange("p a (b t) -> p (a b) t", t=C),
                                                 K.bank[b0 + 3][:, :].rearrange("p (c t) -> p c t", t=C), up, ALU.mult))]))
            extra.append((g, full(sl(B.akt), sl(B.vt), b0 + 3), [("act", lambda: a.copy(flat(B.akt), bank(3)))]))
            for s in LEVELS[1:]:
                put(full(sl(B.nt), sl(B.T), b0),
                    [("dve", lambda s=s: v.tensor_tensor(B.X[:, :, :], bank3(0), wide(K.k(f"low{s}")), ALU.mult))])
                if extra:
                    out.append(extra.pop(0))
                last = s == LEVELS[-1]
                mms = full(sl(B.X), sl(B.TT), b0 + 2)
                ev = [("dve", lambda: v.tensor_tensor(B.TT[:, :, :], bank3(2), B.TT[:, :, :], ALU.add))]
                if not last:
                    mms = full(sl(B.TT), sl(B.X), b0 + 1) + mms
                    ev = [("dve", lambda: v.tensor_tensor(B.T[:, :, :], bank3(1), B.T[:, :, :], ALU.add))] + ev
                put(mms, ev)
                if extra:
                    out.append(extra.pop(0))
            assert not extra
            put(full(sl(B.TT), sl(B.at), b0), [("act", lambda: a.copy(flat(B.X), bank(0)))])
            put(full(sl(B.TT), sl(B.akt), b0 + 1), [("act", lambda: a.copy(flat(B.T), bank(1)))])
            ta, takv = B.X, B.T
            rb = lambda c: B.rbk[:, c, 0:C]
            rk = lambda c: B.rbk[:, c, C:P]

            def m_out(c):
                end = R.eP[:, (4 * g + c + 1) * C - 1:(4 * g + c + 1) * C]
                return lambda: v.scalar_tensor_tensor(R.M[:, 4 * g + c, :], idt, end, K.bank[b0 + 2][:, c * P:(c + 1) * P], ALU.mult, ALU.add)

            put(full(sl(ta), sl(B.bht), b0 + 2), [("dve", m_out(c)) for c in range(4)])
            sp4 = lambda t: t[:, 4 * g * C:4 * (g + 1) * C].rearrange("p (c t) -> p c t", t=C)
            put(full(sl(ta), rb, b0 + 3, C),
                [("dve", lambda: v.tensor_tensor(sp4(R.Q), bank3(3)[:, :, 0:C], sp4(R.rt), ALU.add))])
            put(full(sl(B.bht), sl(takv), b0, P, 0, (sl(B.kht), sl(B.vt))),
                [("act", lambda: a.copy(R.Z[:, 4 * g:4 * g + 4, :].rearrange("p a b -> p (a b)"), bank(0)))])
            put(full(sl(takv), rb, b0 + 1, C, 0, (sl(B.vt), rk)),
                [("act", lambda: a.copy(sp4(R.Y), bank3(1)[:, :, 0:C]))])
            return out

        one, two = group_steps(0), group_steps(1)
        for x, z in zip(one, two):
            steps += [x, z]
        n_dve = [sum(e == "dve" for e, _ in ev) for _, _, ev in steps]
        n_act = [sum(e == "act" for e, _ in ev) for _, _, ev in steps]
        N = len(steps)

        with nc.Block() as block:
            @block.sync
            def _(sp):
                pass

            @block.tensor
            def _(pe):
                for n, (g, mms, _) in enumerate(steps):
                    if n >= 2:
                        d, a = sum(n_dve[:n - 1]), sum(n_act[:n - 1])
                        if d:
                            pe.wait_ge(s_dve, d)
                        if a:
                            pe.wait_ge(s_act, a)
                    for out, l, r, start, stop in mms:
                        if r is None:
                            last = pe.transpose(out, l, idt)
                        else:
                            last = pe.matmul(out, l, r, start=start, stop=stop)
                    last.then_inc(s_pe, 1)
                pe.wait_ge(s_dve, sum(n_dve))
                pe.wait_ge(s_act, sum(n_act))
                for c in range(1, NCH):
                    pe.wait_ge(s_sv, c)
                    if c < NCH - 1:
                        pe.matmul(K.bank[c % 2][:, 0:P], R.M[:, c, :], S[:, (c - 1) % 2, :], start=True, stop=True).then_inc(s_sp, 1)
                    last = pe.matmul(K.bank[2][:, c * C:(c + 1) * C], S[:, (c - 1) % 2, :], R.Q[:, c * C:(c + 1) * C], start=True, stop=True)
                last.then_inc(s_sp, 1)

            @block.vector
            def _(dve):
                for n, (g, _, evacs) in enumerate(steps):
                    if n_dve[n]:
                        dve.wait_ge(s_pe, n + 1)
                        dve.drain()
                    for e, f in evacs:
                        if e == "dve":
                            f().then_inc(s_dve, 1)
                        elif e == "drain":
                            dve.drain()
                dve.wait_ge(s_act, sum(n_act))
                nc.vector.tensor_copy(S[:, 0, :], R.Z[:, 0, :]).then_inc(s_sv, 1)
                for c in range(1, NCH - 1):
                    dve.wait_ge(s_sp, c)
                    nc.vector.tensor_tensor(S[:, c % 2, :], K.bank[c % 2][:, 0:P], R.Z[:, c, :], ALU.add).then_inc(s_sv, 1)
                dve.wait_ge(s_sp, NCH - 1)
                nc.vector.tensor_copy(yout[:, 0:C], R.Y[:, 0:C])
                nc.vector.tensor_tensor(yout[:, C:T], K.bank[2][:, C:T], R.Y[:, C:T], ALU.add)

            @block.scalar
            def _(act):
                for n, (g, _, evacs) in enumerate(steps):
                    if n_act[n]:
                        act.wait_ge(s_pe, n + 1)
                    for e, f in evacs:
                        if e == "act":
                            f().then_inc(s_act, 1)


def rwkv_finish_stage(K, M, y):
    nc, io = K.nc, K.io
    with stage(K, "rfin") as st:
        wg = st.sb("wg", [P, 512])
        wg2 = st.sb("wg2", [32, 512])
        sq = st.sb("sq", [P, 2, T])
        rs = st.sb("rs", [P, 2, T])
        s_w, s_mean, s_yc, s_sq, s_var, s_root, s_rk, s_bonus, s_done = st.sems(
            "w", "mean", "centred", "square", "var", "root", "rk", "bonus", "done")
        with nc.Block() as block:
            @block.sync
            def _(sp):
                sp.dma_start(wg[:, :], io["w_gate_up"][0, 0:P, :]).then_inc(s_w, 16)
                sp.dma_start(wg2[:, :], io["w_gate_up"][0, P:P + 32, :]).then_inc(s_w, 16)

            @block.tensor
            def _(pe):
                pe.wait_ge(s_w, 32)
                for p in range(4):
                    b = 4 * (p % 2)
                    if p >= 2:
                        pe.wait_ge(s_done, p - 1)
                    pe.matmul(K.bank[b][:, :], K.k("heads"), y[:, 4 + p, :], start=True, stop=True).then_inc(s_mean, 1)
                    pe.wait_ge(s_rk, p + 1)
                    pe.matmul(K.bank[b + 1][:, :], K.k("heads"), K.h[:, p, :], start=True, stop=True)
                    pe.matmul(K.bank[b + 2][:, :], wg[:, p * P:(p + 1) * P], M.g[:, :], start=True, stop=False)
                    pe.matmul(K.bank[b + 2][:, :], wg2[:, p * P:(p + 1) * P], M.g2[:, :], start=False, stop=True).then_inc(s_bonus, 1)
                    pe.wait_ge(s_sq, p + 1)
                    pe.matmul(K.bank[b + 3][:, :], K.k("heads"), sq[:, p % 2, :], start=True, stop=True).then_inc(s_var, 1)

            @block.scalar
            def _(act):
                for p in range(4):
                    act.wait_ge(s_yc, p + 1)
                    if p >= 2:
                        act.wait_ge(s_var, p - 1)
                        act.wait_ge(s_done, p - 1)
                    nc.scalar.activation(sq[:, p % 2, :], y[:, 4 + p, :], ACT.Square).then_inc(s_sq, 1)
                    act.wait_ge(s_var, p + 1)
                    nc.scalar.activation(rs[:, p % 2, :], K.bank[4 * (p % 2) + 3][:, :], ACT.Sqrt, bias=K.k("eps")[:, 1:2],
                                         scale=1.0 / HD).then_inc(s_root, 1)

            @block.vector
            def _(dve):
                for p in range(4):
                    nc.vector.scalar_tensor_tensor(K.h[:, p, :], M.rkv[:, p, :], K.p("r_k", p), M.rkv[:, 4 + p, :],
                                                   ALU.mult, ALU.mult).then_inc(s_rk, 1)
                for p in range(4):
                    b = 4 * (p % 2)
                    yt = y[:, 4 + p, :]
                    dve.wait_ge(s_mean, p + 1)
                    nc.vector.scalar_tensor_tensor(yt, K.bank[b][:, :], -1.0 / HD, yt, ALU.mult, ALU.add).then_inc(s_yc, 1)
                    dve.wait_ge(s_bonus, p + 1)
                    nc.vector.tensor_tensor(M.rkv[:, p, :], K.bank[b + 1][:, :], M.rkv[:, 8 + p, :], ALU.mult)
                    dve.wait_ge(s_root, p + 1)
                    nc.vector.reciprocal(rs[:, p % 2, :], rs[:, p % 2, :])
                    dve.drain()
                    nc.vector.scalar_tensor_tensor(yt, yt, K.p("ln_x_gain", p), rs[:, p % 2, :], ALU.mult, ALU.mult)
                    dve.drain()
                    nc.vector.scalar_tensor_tensor(yt, yt, K.p("ln_x_bias", p), M.rkv[:, p, :], ALU.add, ALU.add)
                    dve.drain()
                    nc.vector.tensor_tensor(yt, yt, K.bank[b + 2][:, :], ALU.mult).then_inc(s_done, 1)


def rwkv(K, M, y):
    nc = K.nc
    with ExitStack() as st:
        sb = lambda n, shape: st.enter_context(nc.sbuf_tensor(n, shape, F32))
        R = Bag()
        with ExitStack() as inner:
            isb = lambda n, shape: inner.enter_context(nc.sbuf_tensor(n, shape, F32))
            R.wl, R.oka, R.eP, R.rt = isb("wl", [P, 512]), isb("oka", [P, 1]), isb("eP", [P, T]), isb("rt", [P, T])
            R.bd = isb("bd", [P, 6, NCH, P])
            R.M = y[:, 0:2, :].rearrange("p a (c j) -> p (a c) j", j=P)
            R.Z = y[:, 2:4, :].rearrange("p a (c j) -> p (a c) j", j=P)
            R.Q, R.Y = K.h[:, 0, :], K.h[:, 1, :]
            for p in range(4):
                rwkv_prep_stage(K, M, R, p)
                rwkv_chunk_stage(K, R, p, y[:, 4 + p, :])
        rwkv_finish_stage(K, M, y)


PAD = 16


def linear_stage(K, name, tiles, banks=8, scalar=lambda t: t % 2 == 1, extra=None):
    nc, plan = K.nc, K.plan
    extra = extra or {}
    with stage(K, name) as st:
        s_v, s_s = st.sems("vector_out", "scalar_out")
        mine = [scalar(t) for t in range(len(tiles))]
        if "sems" in extra:
            extra["sems"](st)
        with nc.Block() as block:
            @block.sync
            def _(sp):
                if "sync" in extra:
                    extra["sync"](sp)
                K.stream(sp, K.end_of(tiles[-1][0]) + RING)

            @block.tensor
            def _(pe):
                for t, (seg, j, m, width, pairs, shape, _) in enumerate(tiles):
                    w = K.chunk(pe, seg, j, width)
                    if t >= banks:
                        o = t - banks
                        pe.wait_ge(s_s if mine[o] else s_v, sum(x == mine[o] for x in mine[:o + 1]))
                    product(pe, K.bank[t % banks][0:shape[0], 0:shape[1]], pairs(w)).then_inc(K.tiles_done, 1)
                if "tensor" in extra:
                    extra["tensor"](pe)

            def evacuate(e, side):
                for t, (seg, j, m, _, _, shape, evac) in enumerate(tiles):
                    if mine[t] == side:
                        e.wait_ge(K.tiles_done, plan.tile(seg, j, m))
                        evac(K.bank[t % banks][0:shape[0], 0:shape[1]], "scalar" if side else "vector").then_inc(s_s if side else s_v, 1)

            @block.scalar
            def _(act):
                evacuate(act, True)
                if "scalar" in extra:
                    extra["scalar"](act)

            @block.vector
            def _(dve):
                if "before" in extra:
                    extra["before"](dve)
                evacuate(dve, False)
                if "vector" in extra:
                    extra["vector"](dve)


def copier(nc, dst, scale=None):
    def go(bank, engine):
        if engine == "scalar":
            return nc.scalar.copy(dst, bank) if scale is None else nc.scalar.activation(dst, bank, ACT.Copy, scale=scale)
        return nc.vector.tensor_copy(dst, bank) if scale is None else nc.vector.tensor_scalar(dst, bank, scale, None, ALU.mult)
    return go


def feature_pairs(K, m, rows=P):
    return lambda w: [(w[:, k, m * P:m * P + rows], K.h[:, k, :]) for k in range(KD)]


def ab_in_stage(K, B):
    nc, io = K.nc, K.io
    tiles = []
    for n in range(12):
        dst = B.u[:, n, PAD:] if n < 4 else (B.q if n < 8 else B.k)[:, n % 4, :]
        tiles.append(("ab_in", n // 2, n % 2, WC, feature_pairs(K, n % 2), (P, T),
                      copier(nc, dst, HD ** -0.5 if n // 4 == 1 else None)))
    for j in range(2):
        for b in range(TB):
            pairs = lambda w, b=b: [(K.h[:, k, b * P:(b + 1) * P], w[:, k, :]) for k in range(KD)]
            tiles.append(("ab_v", j, b, WC, pairs, (P, WC), copier(nc, B.v[:, b, j * WC:(j + 1) * WC])))
    wf = B.wf
    box = {}

    def sems(st):
        box["w"], box["pe"] = st.sems("wf", "f")

    def sync(sp):
        sp.dma_start(wf[:, :, :], io["ab_w_in_2"][0].rearrange("(k p) n -> p k n", p=P)[:, :, AB_F:AB_F + 8]).then_inc(box["w"], 16)

    def tensor(pe):
        pe.wait_ge(box["w"], 16)
        product(pe, K.bank[7][0:8, :], [(wf[:, k, :], K.h[:, k, :]) for k in range(KD)]).then_inc(box["pe"], 1)

    def vector(dve):
        dve.wait_ge(box["pe"], 1)
        nc.vector.tensor_scalar(B.z[:, :], K.bank[7][0:8, :], K.p("ab_b_forget_2")[0:8, :], None, ALU.add)

    linear_stage(K, "abin", tiles, banks=7, extra={"sems": sems, "sync": sync, "tensor": tensor, "vector": vector})


def fox_prep_stage(K, B, y):
    nc, io = K.nc, K.io
    with stage(K, "foxprep") as st:
        e, l, one = st.sb("e", [8, T]), st.sb("l", [8, T]), st.sb("one", [8, T])
        inv = st.sb("inv", [P, 4, T])
        wp = st.sb("wp", [P, 4, P])
        acc = st.sb("acc", [P, 2, T + PAD])
        dif = st.sb("dif", [P, 4, T])
        s_w, s_z, s_exp, s_e1, s_ln, s_F, s_pe, s_ev, s_dif, s_pool, s_pp = st.sems(
            "w", "z", "exp", "e1", "ln", "F", "turned", "out", "dif", "pool", "pooled")
        with nc.Block() as block:
            @block.sync
            def _(sp):
                for g in range(4):
                    sp.dma_start(inv[:, g, :], io["window"][g].partition_broadcast(P)).then_inc(s_w, 16)
                sp.dma_start(wp[:, :, :], io["pool_w_2"][0].rearrange("g k n -> k g n")).then_inc(s_w, 16)

            @block.gpsimd
            def _(pool):
                nc.gpsimd.memset(B.u[:, :, 0:PAD], 0.0)
                nc.gpsimd.memset(acc[:, :, 0:PAD], 0.0)
                pool.drain()
                pool.wait_ge(s_w, 80)
                for g in range(4):
                    cur = B.u[:, g, :]
                    for n in range(g + 1):
                        d = 1 << n
                        nc.gpsimd.tensor_tensor(acc[:, n % 2, PAD:], cur[:, PAD:], cur[:, PAD - d:T + PAD - d], ALU.add)
                        pool.drain()
                        cur = acc[:, n % 2, :]
                    nc.gpsimd.tensor_tensor(dif[:, g, :], cur[:, PAD:], inv[:, g, :], ALU.mult)
                    pool.drain()
                    nc.gpsimd.tensor_tensor(dif[:, g, :], dif[:, g, :], B.u[:, g, PAD:], ALU.subtract).then_inc(s_pool, 1)

            @block.scalar
            def _(act):
                act.wait_ge(s_z, 1)
                nc.scalar.activation(e[:, :], e[:, :], ACT.Exp).then_inc(s_exp, 1)
                act.wait_ge(s_e1, 1)
                nc.scalar.activation(l[:, :], e[:, :], ACT.Ln).then_inc(s_ln, 1)
                act.wait_ge(s_pe, 1)
                nc.scalar.copy(B.F[:, :], K.bank[0][:, 0:32])
                for h in range(8):
                    act.wait_ge(s_pe, 2 + h)
                    nc.scalar.copy(B.nF[:, h, :], K.bank[1 + h % 2][:, :]).then_inc(s_ev, 1)

            @block.vector
            def _(dve):
                nc.vector.tensor_scalar(e[:, :], B.z[:, :], -1.0, None, ALU.mult)
                nc.vector.memset(one[:, :], 1.0)
                dve.drain()
                nc.vector.tensor_tensor(e[:, :], e[:, :], B.z[:, :], ALU.min).then_inc(s_z, 1)
                dve.wait_ge(s_exp, 1)
                nc.vector.tensor_scalar(e[:, :], e[:, :], 1.0, None, ALU.add).then_inc(s_e1, 1)
                dve.wait_ge(s_ln, 1)
                nc.vector.scalar_tensor_tensor(l[:, :], B.z[:, :], 0.0, l[:, :], ALU.min, ALU.subtract)
                dve.drain()
                nc.vector.tensor_tensor_scan(B.z[:, :], one[:, :], l[:, :], 0.0, ALU.mult, ALU.add)
                dve.drain()
                nc.vector.tensor_scalar(e[:, :], B.z[:, :], -1.0, None, ALU.mult).then_inc(s_F, 1)
                for g in range(4):
                    dve.wait_ge(s_pp, g + 1)
                    nc.vector.tensor_scalar(y[:, g, :], K.bank[4 + g][:, :], K.p("pool_scale_2", g), None, ALU.mult)

            @block.tensor
            def _(pe):
                pe.wait_ge(s_F, 1)
                for b in range(TB):
                    last = pe.transpose(K.bank[0][:, 8 * b:8 * b + 8], B.z[:, b * P:(b + 1) * P], K.k("ident")[0:8, 0:8])
                last.then_inc(s_pe, 1)
                for h in range(8):
                    if h >= 2:
                        pe.wait_ge(s_ev, h - 1)
                    pe.matmul(K.bank[1 + h % 2][:, :], K.k("ident")[0:8, h:h + 1].broadcast_to([8, P]), e[:, :],
                              start=True, stop=True).then_inc(s_pe, 1)
                for g in range(4):
                    pe.wait_ge(s_pool, g + 1)
                    pe.matmul(K.bank[4 + g][:, :], wp[:, g, :], dif[:, g, :], start=True, stop=True).then_inc(s_pp, 1)


def mixer2(K):
    nc = K.nc
    with ExitStack() as st:
        sb = lambda n, shape: st.enter_context(nc.sbuf_tensor(n, shape, F32))
        B = Bag()
        B.q, B.k, B.v, B.F = sb("fq", [P, 4, T]), sb("fk", [P, 4, T]), sb("fv", [P, TB, 512]), sb("fF", [P, 32])
        B.nF, y = sb("fnF", [P, 8, T]), sb("fy", [P, KD, T])
        with ExitStack() as inner:
            isb = lambda n, shape: inner.enter_context(nc.sbuf_tensor(n, shape, F32))
            B.u, B.wf, B.z = isb("fu", [P, 4, T + PAD]), isb("fwf", [P, KD, 8]), isb("fz", [8, T])
            ab_in_stage(K, B)
            fox_prep_stage(K, B, y)

        def prep(pool, out, h, i):
            w = (i + 1) * P
            nc.gpsimd.tensor_scalar(out, B.nF[:, h, 0:w], B.F[:, 8 * i + h:8 * i + h + 1], None, ALU.add)
            pool.drain()
            return nc.gpsimd.tensor_tensor(out[:, w - P:w], out[:, w - P:w], K.k("causal")[:, T - P:T], ALU.add)

        r = lambda h: slice((h % 2) * 64, (h % 2) * 64 + 64)
        attention_stage(K, "fox", 8, HD, lambda h, i: B.q[r(h), h // 2, i * P:(i + 1) * P], lambda h, w: B.k[r(h), h // 2, 0:w],
                        lambda h, s: B.v[:, s, h * 64:(h + 1) * 64], 64, lambda h, i: y[r(h), 4 + h // 2, i * P:(i + 1) * P], prep=prep)
        out_stage(K, "ab_out", lambda k: y[:, k, :], True)


ROPE = 32
QK = 96
MH = 16
TWO_PI_HI = 6.28125
TWO_PI_MID = float(np.float32(int((2 * math.pi - 6.28125) * 2 ** 20) / 2 ** 20))
TWO_PI_LO = 2 * math.pi - TWO_PI_HI - TWO_PI_MID
ROUND = 12582912.0


def mla_in_stage(K, B):
    nc, io = K.nc, K.io
    w_in = io["mla_w_in_2"][0].rearrange("(k p) n -> p k n", p=P)
    tiles = [("mla_q", 0, m, WC, feature_pairs(K, m), (P, T), copier(nc, B.cq[:, m, :])) for m in range(2)]
    tiles.append(("mla_kv", 0, 0, P, feature_pairs(K, 0), (P, T), copier(nc, B.ckv[:, :])))
    box = {}
    R = slice(64, 96)

    def sems(st):
        box["w"], box["pe"], box["pos"], box["ang"], box["sin"], box["rope"] = st.sems("wr", "rope", "pos", "angle", "sin", "rotated")
        box["wr"] = st.sb("wr", [P, KD, 2 * ROPE])
        box["pos_i"] = st.sb("pos_i", [P, T], I32)
        box["ang_t"], box["turn"] = st.sb("ang", [P, T]), st.sb("turn", [P, T])

    def sync(sp):
        for a, b in ((0, 384), (16, 400), (32, 400), (48, 384)):
            sp.dma_start(box["wr"][:, :, a:a + 16], w_in[:, :, b:b + 16]).then_inc(box["w"], 16)
        sp.dma_start(box["pos_i"][:, :], io["positions_2"][0].partition_broadcast(P)).then_inc(box["pos"], 16)

    def tensor(pe):
        pe.wait_ge(box["w"], 64)
        for n in range(2):
            product(pe, K.bank[5 + n][R, :], [(box["wr"][:, k, n * ROPE:(n + 1) * ROPE], K.h[:, k, :]) for k in range(KD)]
                    ).then_inc(box["pe"], 1)

    def before(dve):
        ang, turn = box["ang_t"], box["turn"]
        dve.wait_ge(box["pos"], 16)
        nc.vector.tensor_copy(ang[:, :], box["pos_i"][:, :])
        dve.drain()
        nc.vector.tensor_scalar(ang[:, :], ang[:, :], K.k("freq")[:, 0:1], None, ALU.mult)
        dve.drain()
        nc.vector.tensor_scalar(turn[:, :], ang[:, :], 1.0 / (2 * math.pi), ROUND, ALU.mult, ALU.add)
        dve.drain()
        nc.vector.tensor_scalar(turn[:, :], turn[:, :], ROUND, None, ALU.subtract)
        dve.drain()
        for part in (TWO_PI_HI, TWO_PI_MID, TWO_PI_LO):
            nc.vector.scalar_tensor_tensor(ang[:, :], turn[:, :], -part, ang[:, :], ALU.mult, ALU.add)
            dve.drain()
        nc.vector.tensor_scalar(ang[:, :], ang[:, :], 3.1415925, -3.1415925, ALU.min, ALU.max).then_inc(box["ang"], 1)

    def scalar(act):
        act.wait_ge(box["ang"], 1)
        nc.scalar.activation(B.sin[:, :], box["ang_t"][:, :], ACT.Sin)
        nc.scalar.activation(B.cos[:, :], box["ang_t"][:, :], ACT.Sin, scale=0.5).then_inc(box["sin"], 1)

    def vector(dve):
        dve.wait_ge(box["sin"], 1)
        nc.vector.tensor_tensor(B.cos[:, :], B.cos[:, :], B.cos[:, :], ALU.mult)
        nc.vector.tensor_scalar(B.sin[:, :], B.sin[:, :], K.k("freq")[:, 1:2], None, ALU.mult)
        dve.drain()
        nc.vector.tensor_scalar(B.cos[:, :], B.cos[:, :], -2.0, 1.0, ALU.mult, ALU.add)
        dve.drain()
        dve.wait_ge(box["pe"], 2)
        nc.vector.tensor_tensor(B.kr[R, :], K.bank[5][R, :], B.cos[R, :], ALU.mult)
        nc.vector.tensor_tensor(box["turn"][R, :], K.bank[6][R, :], B.sin[R, :], ALU.mult)
        dve.drain()
        nc.vector.tensor_tensor(B.kr[R, :], B.kr[R, :], box["turn"][R, :], ALU.add)

    linear_stage(K, "mlain", tiles, banks=4, scalar=lambda t: True,
                 extra={"sems": sems, "sync": sync, "tensor": tensor, "scalar": scalar, "before": before, "vector": vector})


def mla_prep_stage(K, B):
    nc, io = K.nc, K.io
    R = slice(64, 96)
    swap = K.h
    with stage(K, "mlaprep") as st:
        wq, wkv = B.wq, B.wkv
        s_w, s_pe, s_v, s_s, s_swap, s_q, s_rot, s_tmp = st.sems("w", "pe", "vector_out", "scalar_out", "swapped", "q", "rotated", "tmp")
        steps = []
        for h in range(MH):
            steps.append((QK, T, [(wq[:, k, h * QK:(h + 1) * QK], B.cq[:, k, :]) for k in range(2)], B.Q[0:QK, h, :], QK ** -0.5))
        for h in range(MH):
            steps.append((64, T, [(wkv[:, h * P:h * P + 64], B.ckv[:, :])], B.K[0:64, h, :], None))
        wv = wkv[:, :].rearrange("p (h d) -> p h d", d=P)[:, :, 64:]
        for b in range(TB):
            for half in range(2):
                steps.append((P, T, [(B.ckv[:, b * P:(b + 1) * P], wv[:, 8 * half:8 * half + 8, :])],
                              B.V[:, b, half * 512:(half + 1) * 512], None))
        with nc.Block() as block:
            @block.sync
            def _(sp):
                sp.dma_start(wq[:, :, :], io["mla_w_q_b_2"][0].rearrange("(k p) n -> p k n", p=P)).then_inc(s_w, 16)
                sp.dma_start(wkv[:, :], io["mla_w_kv_b_2"][0]).then_inc(s_w, 16)
                for g in range(4):
                    sp.wait_ge(s_v, 2 * g + 2)
                    sp.wait_ge(s_s, 2 * g + 2)
                    if g >= 2:
                        sp.wait_ge(s_rot, g - 1)
                    o = 4 * (g % 2)
                    sp.dma_start(swap[64:80, o:o + 4, :], B.Q[80:96, 4 * g:4 * g + 4, :]).then_inc(s_swap, 16)
                    sp.dma_start(swap[80:96, o:o + 4, :], B.Q[64:80, 4 * g:4 * g + 4, :]).then_inc(s_swap, 16)
                    sp.wait_ge(s_swap, 32 * g + 32)
                    sp.sem_inc(s_q, 1)

            @block.tensor
            def _(pe):
                pe.wait_ge(s_w, 32)
                for t, (rows, _, pairs, _, _) in enumerate(steps):
                    if t >= 8:
                        pe.wait_ge(s_s if t % 2 else s_v, (t - 8) // 2 + 1)
                    product(pe, K.bank[t % 8][0:rows, :], pairs).then_inc(s_pe, 1)

            def evacuate(e, side):
                for t, (rows, _, _, dst, scale) in enumerate(steps):
                    if t % 2 == side:
                        e.wait_ge(s_pe, t + 1)
                        copier(nc, dst, scale)(K.bank[t % 8][0:rows, :], "scalar" if side else "vector").then_inc(s_s if side else s_v, 1)

            @block.scalar
            def _(act):
                evacuate(act, 1)

            @block.vector
            def _(dve):
                evacuate(dve, 0)

            @block.gpsimd
            def _(pool):
                nc.gpsimd.tensor_copy(B.K[R, :, :], B.kr[R, :].unsqueeze(1).broadcast_to([ROPE, MH, T]))
                wide = lambda ap: ap[R, :].unsqueeze(1).broadcast_to([ROPE, 4, T])
                for g in range(4):
                    pool.wait_ge(s_q, g + 1)
                    o = 4 * (g % 2)
                    q, w = B.Q[R, 4 * g:4 * g + 4, :], swap[R, o:o + 4, :]
                    nc.gpsimd.tensor_tensor(q, q, wide(B.cos), ALU.mult)
                    nc.gpsimd.tensor_tensor(w, w, wide(B.sin), ALU.mult)
                    pool.drain()
                    nc.gpsimd.tensor_tensor(q, q, w, ALU.add).then_inc(s_rot, 1)


def mixer3(K):
    nc = K.nc
    with ExitStack() as st:
        sb = lambda n, shape: st.enter_context(nc.sbuf_tensor(n, shape, F32))
        B = Bag()
        B.V = sb("mV", [P, TB, 1024])
        B.Q, B.K = sb("mQ", [QK, MH, T]), sb("mK", [QK, MH, T])
        with ExitStack() as inner:
            isb = lambda n, shape: inner.enter_context(nc.sbuf_tensor(n, shape, F32))
            B.cq, B.ckv, B.sin, B.cos, B.kr = isb("mcq", [P, 2, T]), isb("mckv", [P, T]), isb("msin", [P, T]), isb("mcos", [P, T]), isb("mkr", [P, T])
            mla_in_stage(K, B)
            small_norm(K, "norm_mq", [B.cq[:, 0, :], B.cq[:, 1, :]], [K.p("mla_q_norm_2", 0), K.p("mla_q_norm_2", 1)], 256)
            small_norm(K, "norm_mkv", [B.ckv[:, :]], [K.p("mla_kv_norm_2")], 128)
            B.wq, B.wkv = isb("mwq", [P, 2, MH * QK]), isb("mwkv", [P, MH * P])
            mla_prep_stage(K, B)
        y = K.h
        r = lambda h: slice((h % 2) * 64, (h % 2) * 64 + 64)
        attention_stage(K, "mla", MH, QK, lambda h, i: B.Q[:, h, i * P:(i + 1) * P], lambda h, w: B.K[:, h, 0:w],
                        lambda h, s: B.V[:, s, h * 64:(h + 1) * 64], 64, lambda h, i: y[r(h), h // 2, i * P:(i + 1) * P],
                        bias=lambda h, i: K.k("chunked")[:, 384 - i * P:384 - i * P + (i + 1) * P])
        out_stage(K, "mla_out", lambda k: y[:, k, :], True)


def build(nc, io):
    plan = Plan()

    def cols(w, a, width, k=KD):
        v = w.rearrange("(k p) n -> p k n", p=P)
        return lambda q, r: v[:, :, bass.ds(a + width * r + 4 * width * q, width)]

    def ffn_chunks(name, wg, wu, wd):
        g, u = (w.rearrange("(k p) n -> p k n", p=P) for w in (wg, wu))
        d = wd.rearrange("(k p) n -> p k n", p=P)
        plan.add(name + "_up", 2 * F // WC,
                 lambda q, r: (g, u)[r % 2][:, :, bass.ds((r // 2) * WC + 2 * WC * q, WC)])
        plan.add(name + "_down", 8,
                 lambda q, r: d[:, 11 * (r % 2):11 * (r % 2) + 11, bass.ds((r // 2) * WC + 2 * WC * q, WC)], marks=(1, 2))

    w_in = io["w_in"][0]
    plan.add("mod1", 8, cols(io["ada_w"][0], 0, WC), marks=(1,))
    plan.add("in_q", 1, cols(w_in, 0, WC))
    plan.add("in_kv", 1, cols(w_in, O_KV, P), marks=(1,))
    plan.add("in_rkv", 6, cols(w_in, O_R, WC))
    plan.add("in_lora", 1, cols(w_in, O_WA, 288), marks=(3,))
    plan.add("mod2", 16, cols(io["ada_w"][0], 2048, WC), marks=(1,))
    plan.add("out1", 4, cols(io["w_out"][0], 0, WC))
    ffn_chunks("ffn1", io["w_ffn_gate"][0], io["w_ffn_up"][0], io["w_ffn_down"][0])

    def ffn2(name, l, i):
        ffn_chunks(name, io["ffn_w_gate_2"][l, i], io["ffn_w_up_2"][l, i], io["ffn_w_down_2"][l, i])

    ffn2("ffn2", 0, 0)
    plan.add("ab_in", 6, cols(io["ab_w_in_2"][0], 0, WC))
    plan.add("ab_v", 2, cols(io["ab_w_in_2"][0], 1536, WC), marks=(4,))
    plan.add("ab_out", 4, cols(io["ab_w_out_2"][0], 0, WC))
    ffn2("ffn3", 0, 1)
    ffn2("ffn4", 1, 0)
    plan.add("mla_q", 1, cols(io["mla_w_in_2"][0], 0, WC))
    plan.add("mla_kv", 1, cols(io["mla_w_in_2"][0], 256, P), marks=(1,))
    plan.add("mla_out", 4, cols(io["mla_w_out_2"][0], 0, WC))
    ffn2("ffn5", 1, 1)

    with ExitStack() as ctx:
        K = Core(nc, ctx, io, plan)
        par, coef, mod = K.p, K.coef, K.mod
        steps = [
            ("mod1", lambda: mod_stage(K, "mod1", 0, 8)),
            ("h", lambda: model_norm(K, "norm1", lambda i: coef[:, 8 + i:9 + i], lambda i: mod[:, i:i + 1])),
            ("mix1", lambda: mixer1(K)),
            ("x1", lambda: residual_norm(K, "post1", lambda i: coef[:, 16 + i:17 + i])),
            ("h2", lambda: model_norm(K, "norm2", lambda i: coef[:, 24 + i:25 + i], lambda i: mod[:, 24 + i:25 + i])),
            ("f1", lambda: ffn_stage(K, "ffn1", False)),
            ("x2", lambda: residual_norm(K, "post2", lambda i: coef[:, 32 + i:33 + i])),
            ("h3", lambda: model_norm(K, "norm3", lambda i: par("norm_ffn_2", i))),
            ("x3", lambda: ffn_stage(K, "ffn2", True)),
            ("h4", lambda: model_norm(K, "norm4", lambda i: par("norm_mix_2", i))),
            ("x4", lambda: mixer2(K)),
            ("h5", lambda: model_norm(K, "norm5", lambda i: par("norm_ffn_2", 8 + i))),
            ("x5", lambda: ffn_stage(K, "ffn3", True)),
            ("h6", lambda: model_norm(K, "norm6", lambda i: par("norm_ffn_2", 16 + i))),
            ("x6", lambda: ffn_stage(K, "ffn4", True)),
            ("h7", lambda: model_norm(K, "norm7", lambda i: par("norm_mix_2", 8 + i))),
            ("x7", lambda: mixer3(K)),
            ("h8", lambda: model_norm(K, "norm8", lambda i: par("norm_ffn_2", 24 + i))),
            ("x8", lambda: ffn_stage(K, "ffn5", True)),
            ("h9", lambda: model_norm(K, "norm9", lambda i: par("norm_final_2", i))),
            ("out", lambda: finish_stage(K)),
        ]
        start_stage(K, None)
        for _, step in steps:
            step()


def const_table():
    t = np.zeros((P, CONST_W), np.float32)

    def put(name, v):
        a, b = CONST[name]
        t[:, a:b] = v

    i, j = np.arange(P)[:, None], np.arange(P)[None, :]
    same = (i // C) == (j // C)
    ii, jj = i % C, j % C
    put("ident", i == j)
    put("flip", i + j == P - 1)
    put("ones", 1.0)
    put("heads", same)
    for s in LEVELS:
        low = same & (ii // (2 * s) == jj // (2 * s)) & (ii // s > jj // s)
        put("first" if s == 1 else f"low{s}", low)
        if s == 1:
            put("first_t", low.T)
    put("strict", same & (ii < jj))
    put("upto", np.arange(P)[:, None] % C <= np.arange(C)[None, :])
    x = np.arange(T)[None, :]
    put("causal", np.where(x - 384 > i, -BIG, 0.0))
    put("chunked", np.where((x - 384) // C > i // C, -BIG, 0.0))
    put("reset", x % C != 0)
    put("eps", np.array([EPS, GN_EPS, 0.0, 0.0], np.float32)[None, :])
    inv = (np.float32(10000.0) ** (-np.arange(0, 32, 2, dtype=np.float32) / np.float32(32))).astype(np.float32)
    put("freq", np.stack([np.tile(inv, 8), np.where(np.arange(P) % 32 < 16, -1.0, 1.0)], 1))
    return t


def bucket_table():
    d = np.arange(T)
    nf = np.maximum(d, 1).astype(np.float32)
    large = 16 + (np.log(nf / np.float32(16)) / np.float32(math.log(8.0)) * np.float32(16)).astype(np.int32)
    b = np.where(d < 16, d, np.minimum(large, 31))
    t = (b[None, ::-1] == np.arange(32)[:, None]).astype(np.float32)
    return np.concatenate([t, np.zeros((32, P), np.float32)], 1)


def window_table():
    n = np.arange(T) + 1
    return np.stack([(np.float32(1.0) / np.minimum(n, w).astype(np.float32)) for w in (2, 4, 8, 16)]).astype(np.float32)


TABLES = {"const": const_table, "bucket": bucket_table, "window": window_table}
INS = ["x", "c", "rel_bias", "ada_w", "ada_b", "mix_pre_norm", "mix_post_norm", "ffn_pre_norm", "ffn_post_norm",
       "w_in", "q_norm", "w_uq", "w_idx_q", "kv_norm", "idx_k_norm", "w_uk", "w_uv", "mu_shift", "w0", "w_decay_up",
       "a0", "w_aaa_up", "w_gate_up", "k_k", "k_a", "r_k", "ln_x_gain", "ln_x_bias", "w_out", "w_ffn_gate",
       "w_ffn_up", "w_ffn_down", "positions_2", "norm_ffn_2", "norm_mix_2", "norm_final_2", "ffn_w_gate_2",
       "ffn_w_up_2", "ffn_w_down_2", "ab_w_in_2", "ab_b_forget_2", "pool_w_2", "pool_scale_2", "ab_w_out_2",
       "mla_w_in_2", "mla_q_norm_2", "mla_kv_norm_2", "mla_w_q_b_2", "mla_w_kv_b_2", "mla_w_out_2"]


def kernel(**inputs):
    import concourse.bacc as bacc
    from concourse.bass_utils import run_bass_kernel_spmd

    nc = bacc.Bacc("TRN2", target_bir_lowering=False, num_devices=1)
    arrays, io = {}, {}
    for name in INS + list(TABLES):
        a = np.ascontiguousarray(inputs[name] if name in inputs else TABLES[name]())
        arrays[f"in_{name}"] = a
        io[name] = nc.dram_tensor(f"in_{name}", a.shape, mybir.dt.from_np(a.dtype), kind="ExternalInput").ap()
    io["out"] = nc.dram_tensor("out", (1, T, D), F32, kind="ExternalOutput").ap()
    build(nc, io)
    r = run_bass_kernel_spmd(nc, [arrays], core_ids=[0])
    return r.results[0]["out"]
```

```python
import math
from contextlib import ExitStack

import numpy as np

import concourse.bass as bass
from concourse import mybir

F32 = mybir.dt.float32
F32R = mybir.dt.float32r
I32 = mybir.dt.int32
ALU = mybir.AluOpType
ACT = mybir.ActivationFunctionType
AX = mybir.AxisListType

P = 128
T = 512
D = 1024
KD = D // P
F = 2816
KF = F // P
HD = 64
TB = T // P
C = 64
NCH = T // C
EPS = 1e-6
GN_EPS = 64e-5
BIG = 1e30
CAUSAL_FILL = -3.0e38
TAKEN = -3.3e38
TOPK = min(256, T // 4)
RING = 4
WC = 256
SLOT = KD * WC

LEVELS = (1, 2, 4, 8, 16, 32)
CONST = {}
_at = 0
for _name, _n in (("ident", P), ("flip", P), ("ones", P), ("heads", P), ("first", P), ("first_t", P)) + tuple(
        (f"low{s}", P) for s in LEVELS[1:]) + (("strict", P), ("upto", C), ("causal", T),
                                           ("chunked", T), ("reset", T), ("eps", 4), ("freq", 2)):
    CONST[_name] = (_at, _at + _n)
    _at += _n
CONST_W = _at

ROWS_A = (("ada_b", 48), ("mix_pre_norm", 8), ("mix_post_norm", 8), ("ffn_pre_norm", 8), ("ffn_post_norm", 8),
          ("c", 8), ("q_norm", 2), ("kv_norm", 1), ("w0", 4), ("a0", 4), ("k_k", 4), ("k_a", 4), ("r_k", 4),
          ("ln_x_gain", 4), ("ln_x_bias", 4))
ROWS_B = (("norm_ffn_2", 32), ("norm_mix_2", 16), ("norm_final_2", 8), ("mla_q_norm_2", 2), ("mla_kv_norm_2", 1),
          ("pool_scale_2", 4), ("mu_rkv", 12), ("mu_wa", 1), ("mu_g", 1), ("mu_g2", 1), ("idx_k_norm", 1),
          ("ab_b_forget_2", 1))


def columns(rows, base):
    at, out = base, {}
    for name, n in rows:
        out[name] = at
        at += n
    return out, at


COL, _end = columns(ROWS_A, 0)
_colb, PAR_W = columns(ROWS_B, P)
COL.update(_colb)
N_A, N_B = sum(n for _, n in ROWS_A), sum(n for _, n in ROWS_B)

O_KV, O_IK, O_IW, O_R = 256, 384, 448, 456
O_WA = O_R + 3 * 512
O_G = O_WA + 128
IN_COLS = O_G + 160
AB_F = 2048
NEG_SQRT_E = -math.exp(-0.5)


class Plan:

    def __init__(self):
        self.segments, self.order, self.n, self.mark, self.splits = {}, [], 0, 0, 0

    def add(self, name, count, src, marks=2, split=True):
        s = {"name": name, "n0": self.n, "count": count, "src": src, "marks": marks, "mark0": self.mark,
             "split": split, "split0": self.splits}
        self.segments[name] = s
        self.order.append(s)
        self.n += count
        self.mark += marks * count
        self.splits += count * split

    def at(self, n):
        return [x for x in self.order if x["n0"] <= n][-1]

    def used(self, n):
        s = self.at(n)
        return s["mark0"] + s["marks"] * (n - s["n0"] + 1)

    def tile(self, name, c, k):
        s = self.segments[name]
        return s["mark0"] + k + 1 + s["marks"] * c

    def end(self, name):
        s = self.segments[name]
        return s["n0"] + s["count"]


class Core:

    def __init__(self, nc, ctx, io, plan):
        self.nc, self.ctx, self.io, self.plan = nc, ctx, io, plan
        sb = lambda name, shape, dt=F32: ctx.enter_context(nc.sbuf_tensor(name, shape, dt))
        sem = lambda name: ctx.enter_context(nc.semaphore(name))
        self.const = sb("const", [P, CONST_W])
        self.par = sb("par", [P, PAR_W])
        self.mod = sb("mod", [P, 48])
        self.coef = sb("coef", [P, 64])
        self.x = sb("x", [P, KD, T])
        self.h = sb("h", [P, KD, T])
        self.ring = sb("ring", [P, RING, SLOT])
        self.rstd = sb("rstd", [P, T])
        self.bank = [ctx.enter_context(nc.psum_tensor(f"bank{i}", [P, 512], F32)) for i in range(8)]
        self.loaded = [sem(f"chunk_loaded{i}") for i in range(RING)]
        self.tiles_done, self.high_done, self.low_done = sem("tiles_done"), sem("high_done"), sem("low_done")
        self.issued = 0

    def k(self, name):
        a, b = CONST[name]
        return self.const[:, a:b]

    def p(self, name, i=0):
        return self.par[:, COL[name] + i:COL[name] + i + 1]

    def stream(self, sp, upto):
        for n in range(self.issued, min(upto, self.plan.n)):
            if n >= RING:
                o = self.plan.at(n - RING)
                if o["split"]:
                    sp.wait_ge(self.low_done, o["split0"] + n - RING - o["n0"] + 1)
                else:
                    sp.wait_ge(self.tiles_done, self.plan.used(n - RING))
            s = self.plan.at(n)
            self.load(sp, n, s["src"](n - s["n0"]))
        self.issued = max(self.issued, min(upto, self.plan.n))

    def load(self, sp, n, src):
        a, b = src.shape[1], src.shape[2]
        dst = self.ring[:, n % RING, 0:a * b].rearrange("p (a b) -> p a b", a=a)
        sp.dma_start(dst, src).then_inc(self.loaded[n % RING], 16)


class Split:
    PERIOD = 12

    def __init__(self, K, st, norm=None):
        self.K, self.nc, self.norm = K, K.nc, norm
        if norm:
            self.s_sq, self.s_sum, self.s_root, self.s_h = st.sems("squared", "summed", "root", "normed")
        self.hh, self.hl = st.sb("feat_hi", [P, KD, T], F32R), st.sb("feat_lo", [P, KD, T], F32R)
        self.wh, self.wl = st.sb("wt_hi", [P, 2, SLOT], F32R), st.sb("wt_lo", [P, 2, SLOT], F32R)
        self.s_hh, self.s_hl, self.s_hl2 = st.sems("feat_high", "feat_low_even", "feat_low_odd")

    def high(self, act, name, r, t=0, words=SLOT):
        K, s = self.K, self.K.plan.segments[name]
        n = s["n0"] + r
        act.wait_ge(K.loaded[n % RING], 16 * (n // RING + 1) + 16 * (self.PERIOD // RING) * t)
        if not isinstance(t, int):
            act.wait_ge(K.tiles_done, s["mark0"] + s["marks"] * (r - 1) + s["marks"] * self.PERIOD * t)
        elif n + self.PERIOD * t >= 2:
            act.wait_ge(K.tiles_done, K.plan.used(n + self.PERIOD * t - 2))
        self.nc.scalar.copy(self.wh[:, n % 2, 0:words], K.ring[:, n % RING, 0:words]).then_inc(K.high_done, 1)

    def low(self, dve, name, r, t=0, words=SLOT):
        K, s = self.K, self.K.plan.segments[name]
        n = s["n0"] + r
        dve.wait_ge(K.high_done, s["split0"] + r + 1 + self.PERIOD * t)
        self.nc.vector.tensor_tensor(self.wl[:, n % 2, 0:words], K.ring[:, n % RING, 0:words],
                                     self.wh[:, n % 2, 0:words].bitcast(F32), ALU.subtract).then_inc(K.low_done, 1)

    def chunk(self, pe, name, r, width, t=0):
        K, s = self.K, self.K.plan.segments[name]
        n = s["n0"] + r
        pe.wait_ge(K.low_done, s["split0"] + r + 1 + self.PERIOD * t)
        k = SLOT // width
        return tuple(w[:, n % 2, 0:k * width].rearrange("p (k n) -> p k n", n=width) for w in (self.wh, self.wl))

    def squares(self, act):
        K = self.K
        if self.norm:
            for k in range(KD):
                self.nc.scalar.activation(K.h[:, k, :], K.x[:, k, :], ACT.Square).then_inc(self.s_sq, 1)

    def sums(self, pe):
        K = self.K
        if self.norm:
            for k in range(KD):
                pe.wait_ge(self.s_sq, k + 1)
                last = pe.matmul(K.bank[7][:, :], K.k("ones"), K.h[:, k, :], start=k == 0, stop=k == KD - 1)
            last.then_inc(self.s_sum, 1)

    def features_scalar(self, act):
        K = self.K
        if self.norm:
            act.wait_ge(self.s_sum, 1)
            self.nc.scalar.activation(K.rstd[:, :], K.bank[7][:, :], ACT.Sqrt, bias=K.k("eps")[:, 0:1], scale=1.0 / D).then_inc(self.s_root, 1)
            for k in range(KD):
                act.wait_ge(self.s_h, k + 1)
                self.nc.scalar.copy(self.hh[:, k, :], K.h[:, k, :]).then_inc(self.s_hh, 1)

    def normed_vector(self, dve):
        K, v = self.K, self.nc.vector
        gain, shift = self.norm
        dve.wait_ge(self.s_root, 1)
        v.reciprocal(K.rstd[:, :], K.rstd[:, :])
        dve.drain()
        for k in range(KD + 1):
            if k < KD:
                ins = v.scalar_tensor_tensor(K.h[:, k, :], K.x[:, k, :], gain(k), K.rstd[:, :], ALU.mult, ALU.mult)
                if shift:
                    dve.drain()
                    ins = v.tensor_scalar(K.h[:, k, :], K.h[:, k, :], shift(k), None, ALU.add)
                ins.then_inc(self.s_h, 1)
            if k % 2 == 0 and k > 0:
                dve.wait_ge(self.s_hh, k)
                v.tensor_tensor(self.hl[:, k - 1, :], K.h[:, k - 1, :], self.hh[:, k - 1, :].bitcast(F32), ALU.subtract).then_inc(self.s_hl2, 1)

    def features_vector(self, dve, src):
        if self.norm:
            return self.normed_vector(dve)
        for k in range(KD):
            self.nc.vector.tensor_copy(self.hh[:, k, :], src(k)).then_inc(self.s_hh, 1)
            if k % 2 == 0:
                dve.drain()
                self.nc.vector.tensor_tensor(self.hl[:, k, :], src(k), self.hh[:, k, :].bitcast(F32), ALU.subtract).then_inc(self.s_hl, 1)

    def features_pool(self, pool, src):
        for k in range(0 if self.norm else 1, KD, 2):
            pool.wait_ge(self.s_hh, k + 1)
            self.nc.gpsimd.tensor_tensor(self.hl[:, k, :], src(k), self.hh[:, k, :].bitcast(F32), ALU.subtract
                                         ).then_inc(self.s_hl if self.norm else self.s_hl2, 1)

    def feature(self, pe, k, wait, cols=slice(0, T)):
        if wait:
            pe.wait_ge(self.s_hl2 if k % 2 else self.s_hl, k // 2 + 1)
        return self.hh[:, k, cols], self.hl[:, k, cols]


def product3(pe, out, pairs, start=True, stop=True):
    last, n = None, 0
    pairs = iter(pairs)
    cur = next(pairs)
    while cur is not None:
        (ah, al), (bh, bl) = cur
        passes = ((ah, bh), (ah, bl), (al, bh))
        for m, (a, b) in enumerate(passes[:2]):
            pe.matmul(out, a, b, start=start and n == 0 and m == 0, stop=False)
        cur, n = next(pairs, None), n + 1
        last = pe.matmul(out, al, bh, start=False, stop=stop and cur is None)
    return last


def product(pe, out, pairs, start=True, stop=True):
    for n, (a, b) in enumerate(pairs):
        last = pe.matmul(out, a, b, start=start and n == 0, stop=stop and n == len(pairs) - 1)
    return last


def stage(K, name):
    st = ExitStack()
    nc = K.nc
    mine = []

    def sem(n):
        mine.append(nc.alloc_semaphore(f"{name}_{n}"))
        return mine[-1]

    def give_back():
        for x in mine:
            nc.gpsimd.sem_clear(x)
            nc.release_semaphore(x)

    st.callback(give_back)
    st.sem = sem
    st.sb = lambda n, shape, dt=F32: st.enter_context(nc.sbuf_tensor(f"{name}_{n}", shape, dt))
    st.sems = lambda *ns: [sem(n) for n in ns]
    return st


def start_stage(K, xin_rows):
    nc, io = K.nc, K.io
    with stage(K, "start") as st:
        rows = st.sb("rows", [P, 2, P])
        xin = st.sb("xin", [P, TB, D])
        s_const, s_rows, s_x, s_zero, s_turned, s_copied = st.sems("const", "rows", "x", "zero", "turned", "copied")
        with nc.Block() as block:
            @block.sync
            def _(sp):
                sp.dma_start(K.const[:, :], io["const"]).then_inc(s_const, 16)
                for t in range(TB):
                    sp.dma_start(xin[:, t, :], io["x"][0, t * P:(t + 1) * P, :]).then_inc(s_x, 16)
                K.stream(sp, RING)

            @block.gpsimd
            def _(pool):
                pass

            @block.scalar
            def _(act):
                act.wait_ge(s_zero, 1)
                n = 0
                for which, group in enumerate((ROWS_A, ROWS_B)):
                    at = 0
                    for name, cnt in group:
                        for dst, src in param_rows(io, name, cnt, rows, which, at):
                            act.dma_start(dst, src).then_inc(s_rows, 16)
                            n += 1
                        at += cnt
                st.n_rows = n
                for k in range(1, KD, 2):
                    act.wait_ge(s_turned, 2 + k + 1)
                    nc.scalar.copy(K.x[:, k, :], K.bank[k][:, :])

            @block.vector
            def _(dve):
                nc.vector.memset(rows[:, :, :], 0.0).then_inc(s_zero, 1)
                dve.wait_ge(s_turned, 2)
                nc.vector.tensor_copy(K.par[:, 0:N_A], K.bank[0][:, 0:N_A])
                nc.vector.tensor_copy(K.par[:, P:P + N_B], K.bank[1][:, 0:N_B]).then_inc(s_copied, 1)
                for k in range(0, KD, 2):
                    dve.wait_ge(s_turned, 2 + k + 1)
                    nc.vector.tensor_copy(K.x[:, k, :], K.bank[k][:, :])

            @block.tensor
            def _(pe):
                pe.wait_ge(s_const, 16)
                pe.wait_ge(s_rows, 16 * st.n_rows)
                pe.transpose(K.bank[0][:, 0:N_A], rows[0:N_A, 0, :], K.k("ident")[0:N_A, 0:N_A]).then_inc(s_turned, 1)
                pe.transpose(K.bank[1][:, 0:N_B], rows[0:N_B, 1, :], K.k("ident")[0:N_B, 0:N_B]).then_inc(s_turned, 1)
                pe.wait_ge(s_x, 16 * TB)
                for k in range(KD):
                    if k == 0:
                        pe.wait_ge(s_copied, 1)
                    for t in range(TB):
                        last = pe.transpose(K.bank[k][:, t * P:(t + 1) * P], xin[:, t, k * P:(k + 1) * P], K.k("ident"))
                    last.then_inc(s_turned, 1)


def param_rows(io, name, cnt, rows, which, at):
    dst = rows[at:at + cnt, which, :]
    mu = io["mu_shift"]
    if name == "mu_rkv":
        return [(dst, mu[0:1, 0:1536].rearrange("a (n p) -> (a n) p", p=P))]
    if name == "mu_wa":
        return [(dst, mu[0:1, 1536:1664])]
    if name == "mu_g":
        return [(dst, mu[0:1, 1664:1792])]
    if name == "mu_g2":
        return [(dst[:, 0:32], mu[0:1, 1792:1824])]
    if name == "idx_k_norm":
        return [(dst[:, 0:64], io[name]), (dst[:, 64:128], io[name])]
    if name == "ab_b_forget_2":
        return [(dst[:, 0:8], io[name])]
    ap = io[name]
    if name == "norm_ffn_2":
        return [(dst, ap.rearrange("a b (n p) -> (a b n) p", p=P))]
    if name == "r_k":
        return [(dst, ap.rearrange("a (n h) d -> (a n) (h d)", h=2))]
    if len(ap.shape) == 1:
        return [(dst, ap.rearrange("(n p) -> n p", p=P))]
    return [(dst, ap.rearrange("a (n p) -> (a n) p", p=P))]


class Modulation:

    def __init__(self, K, st, name, first):
        self.K, self.nc, self.name, self.first = K, K.nc, name, first
        self.seg = K.plan.segments[name]
        self.row = st.sb("row", [1, WC])
        self.s_silu, self.s_row, self.s_turned = st.sems("silu_c", "row_out", "row_turned")

    def loop(self, e, body):
        with e.Fori(0, self.seg["count"] // RING) as i:
            for r in range(RING):
                body(r, i)

    def tensor(self, pe):
        K = self.K
        if self.first == 0:
            pe.wait_ge(self.s_silu, 1)

        def body(r, i):
            n = self.seg["n0"] + r
            pe.wait_ge(K.loaded[n % RING], 16 * (n // RING + 1) + 16 * i)
            w = K.ring[:, n % RING, :].rearrange("p (k n) -> p k n", n=WC)
            product(pe, K.bank[6][0:1, 0:WC], [(K.coef[:, k:k + 1], w[:, k, :]) for k in range(KD)]).then_inc(K.tiles_done, 1)
            pe.wait_ge(self.s_row, r + 1 + RING * i)
            for m in range(2):
                last = pe.matmul(K.bank[5][:, bass.ds(self.first + 2 * r + m + 2 * RING * i, 1)],
                                 self.row[:, m * P:(m + 1) * P], K.k("ident")[0:1, 0:1], start=True, stop=True)
            last.then_inc(self.s_turned, 1)
        self.loop(pe, body)

    def scalar(self, act):
        K = self.K
        if self.first == 0:
            self.nc.scalar.activation(K.coef[:, 0:8], K.par[:, COL["c"]:COL["c"] + 8], ACT.Silu).then_inc(self.s_silu, 1)

        def body(r, i):
            act.wait_ge(K.tiles_done, self.seg["mark0"] + r + 1 + RING * i)
            self.nc.scalar.activation(self.row[:, :], K.bank[6][0:1, 0:WC], ACT.Copy).then_inc(self.s_row, 1)
        self.loop(act, body)

    def vector(self, dve):
        K, v, mod, coef = self.K, self.nc.vector, self.K.mod, self.K.coef
        par = lambda name: K.par[:, COL[name]:COL[name] + KD]
        dve.wait_ge(self.s_turned, self.seg["count"])
        a, b = self.first, self.first + 2 * self.seg["count"]
        v.tensor_tensor(mod[:, a:b], K.bank[5][:, a:b], K.par[:, a:b], ALU.add)
        dve.drain()
        if self.first == 0:
            v.scalar_tensor_tensor(coef[:, 8:16], mod[:, 8:16], 1.0, par("mix_pre_norm"), ALU.add, ALU.mult)
        else:
            v.tensor_tensor(coef[:, 16:24], mod[:, 16:24], par("mix_post_norm"), ALU.mult)
            v.scalar_tensor_tensor(coef[:, 24:32], mod[:, 32:40], 1.0, par("ffn_pre_norm"), ALU.add, ALU.mult)
            v.tensor_tensor(coef[:, 32:40], mod[:, 40:48], par("ffn_post_norm"), ALU.mult)


def mod_stage(K):
    nc = K.nc
    with stage(K, "mod1") as st:
        M = Modulation(K, st, "mod1", 0)
        with nc.Block() as block:
            @block.sync
            def _(sp):
                K.stream(sp, K.plan.end("mod1") + RING)

            @block.tensor
            def _(pe):
                M.tensor(pe)

            @block.scalar
            def _(act):
                M.scalar(act)

            @block.vector
            def _(dve):
                M.vector(dve)


def norm_stage(K, name, src, n, width, write):
    nc = K.nc
    with stage(K, name) as st:
        sq = st.sb("sq", [P, 2, T])
        s_sq, s_sum, s_root = st.sems("squared", "summed", "root")
        with nc.Block() as block:
            @block.scalar
            def _(act):
                for i in range(n):
                    if i >= 2:
                        act.wait_ge(s_sum, i - 1)
                    nc.scalar.activation(sq[:, i % 2, :], src(i), ACT.Square).then_inc(s_sq, 1)
                act.wait_ge(s_sum, n)
                nc.scalar.activation(K.rstd[:, :], K.bank[7][:, :], ACT.Sqrt, bias=K.k("eps")[:, 0:1],
                                     scale=1.0 / width).then_inc(s_root, 1)

            @block.tensor
            def _(pe):
                for i in range(n):
                    pe.wait_ge(s_sq, i + 1)
                    pe.matmul(K.bank[7][:, :], K.k("ones"), sq[:, i % 2, :], start=i == 0, stop=i == n - 1).then_inc(s_sum, 1)

            @block.vector
            def _(dve):
                dve.wait_ge(s_root, 1)
                nc.vector.reciprocal(K.rstd[:, :], K.rstd[:, :])
                dve.drain()
                for i in range(n):
                    write("dve", i, dve)


def final_norm(K):
    norm_stage(K, "normout", lambda i: K.x[:, i, :], KD, D, lambda engine, i, e: K.nc.vector.scalar_tensor_tensor(
        K.h[:, i, :], K.x[:, i, :], K.p("norm_final_2", i), K.rstd[:, :], ALU.mult, ALU.mult))


def residual_norm(K, name, coef):
    nc = K.nc

    def write(engine, i, e):
        nc.vector.scalar_tensor_tensor(K.h[:, i, :], K.h[:, i, :], coef(i), K.rstd[:, :], ALU.mult, ALU.mult)
        e.drain()
        return nc.vector.tensor_tensor(K.x[:, i, :], K.x[:, i, :], K.h[:, i, :], ALU.add)

    norm_stage(K, name, lambda i: K.h[:, i, :], KD, D, write)


THIRDS = (4, 4, 3)


def ffn_chunk(g, u, d, r, t=0):
    ups = 8 if isinstance(t, int) is False or t < 2 else 6
    if r >= Split.PERIOD:
        r, t = r - Split.PERIOD, t + 1
        ups = 8
    if r < ups:
        return (g, u)[r % 2][:, :, bass.ds((r // 2) * WC + 4 * WC * t, WC)]
    return d[:, bass.ds(8 * t, ups), (r - ups) * WC:(r - ups + 1) * WC]


def ffn_stage(K, name, residual, norm):
    nc, plan = K.nc, K.plan
    s = plan.segments[name]
    g_dram, u_dram, d_dram = s["parts"]
    with stage(K, name) as st:
        S = Split(K, st, norm)
        ah, al = st.sb("act_hi", [P, 8, T], F32R), st.sb("act_lo", [P, 8, T], F32R)
        g, a = st.sb("silu", [P, 2, T]), st.sb("act", [P, 2, T])
        s_silu, s_act, s_al, s_free, s_feat = st.sems("silu", "act", "act_low", "out_read", "features")
        C_SILU, C_ACT, C_AL, C_FREE = 2, 2, 2, 4

        def thirds(e, body):
            with e.Fori(0, 2) as t:
                body(t, THIRDS[0], False)
            body(2, THIRDS[2], True)

        def words_of(r, t, steps, last):
            return 2 * steps * WC if last and r >= 2 * steps else SLOT

        with nc.Block() as block:
            @block.sync
            def _(sp):
                def load(r, t):
                    sp.wait_ge(K.low_done, s["split0"] + r - 3 + S.PERIOD * t)
                    K.load(sp, s["n0"] + r, ffn_chunk(g_dram, u_dram, d_dram, r, t))

                with sp.Fori(0, 2) as t:
                    for r in range(RING, RING + S.PERIOD):
                        load(r, t)
                for r in range(RING, 10):
                    load(r, 2)
                K.issued = plan.end(name)
                K.stream(sp, K.issued + RING)

            @block.tensor
            def _(pe):
                S.sums(pe)

                def body(t, steps, last):
                    for p in range(steps):
                        for which in range(2):
                            wh, wl = S.chunk(pe, name, 2 * p + which, WC, t)
                            for m in range(2):
                                pe.wait_ge((s_silu, s_act)[which], 2 * p + m + 1 + 8 * t)
                                c = slice(m * P, (m + 1) * P)
                                product3(pe, K.bank[2 * which + m][:, :],
                                         (((wh[:, k, c], wl[:, k, c]), S.feature(pe, k, p == which == m == 0)) for k in range(KD))
                                         ).then_inc(K.tiles_done, 1)
                    nf = 2 * steps

                    def hidden(f, wait):
                        if wait:
                            pe.wait_ge(s_al, f + 1 + C_AL + 8 * t)
                        return ah[:, f, :], al[:, f, :]

                    for d in range(4):
                        wh, wl = S.chunk(pe, name, nf + d, WC, t)
                        for m in range(2):
                            pe.wait_ge(s_free, 2 * d + m + 1 + 8 * t)
                            c = slice(m * P, (m + 1) * P)
                            product3(pe, K.bank[4 + 2 * (d % 2) + m][:, :],
                                     (((wh[:, f, c], wl[:, f, c]), hidden(f, d == m == 0)) for f in range(nf))
                                     ).then_inc(K.tiles_done, 1)
                thirds(pe, body)

            @block.scalar
            def _(act):
                for _ in range(C_SILU):
                    act.sem_inc(s_silu, 1)
                S.squares(act)
                S.high(act, name, 0)
                S.features_scalar(act)

                def body(t, steps, last):
                    n = 2 * steps + 4
                    for r in range(n):
                        if not (last and r == n - 1):
                            S.high(act, name, r + 1, t, words_of(r + 1, t, steps, last))
                        if r < 2 * steps and r % 2 == 0:
                            for m in range(2):
                                act.wait_ge(K.tiles_done, plan.tile(name, r, m) + 2 * S.PERIOD * t)
                                act.wait_ge(s_act, r + m + 1 + 8 * t)
                                nc.scalar.activation(g[:, m, :], K.bank[m][:, :], ACT.Silu).then_inc(s_silu, 1)
                thirds(act, body)

            @block.vector
            def _(dve):
                for _ in range(C_ACT):
                    dve.sem_inc(s_act, 1)
                for _ in range(C_FREE):
                    dve.sem_inc(s_free, 1)
                S.low(dve, name, 0)
                S.features_vector(dve, lambda k: K.h[:, k, :])
                if not residual:
                    dve.wait_ge(S.s_hl, KD // 2)
                    dve.wait_ge(S.s_hl2, KD // 2)
                    nc.vector.memset(K.h[:, :, :], 0.0)
                    dve.drain()

                def body(t, steps, last):
                    n = 2 * steps + 4
                    for r in range(n):
                        if not (last and r == n - 1):
                            S.low(dve, name, r + 1, t, words_of(r + 1, t, steps, last))
                        if r >= 2 * steps:
                            for m in range(2):
                                d = r - 2 * steps
                                to = (K.x if residual else K.h)[:, 2 * d + m, :]
                                dve.wait_ge(K.tiles_done, plan.tile(name, r, m) + 2 * S.PERIOD * t)
                                nc.vector.scalar_tensor_tensor(to, K.bank[4 + 2 * (d % 2) + m][:, :], 0.5 if residual else 1.0,
                                                               to, ALU.mult, ALU.add).then_inc(s_free, 1)
                        elif r % 2 == 1:
                            for m in range(2):
                                i = r - 1 + m
                                dve.wait_ge(K.tiles_done, plan.tile(name, r, m) + 2 * S.PERIOD * t)
                                dve.wait_ge(s_silu, i + 1 + C_SILU + 8 * t)
                                dve.wait_ge(s_al, i + 1 + 8 * t)
                                nc.vector.tensor_tensor(a[:, m, :], g[:, m, :], K.bank[2 + m][:, :], ALU.mult).then_inc(s_act, 1)
                thirds(dve, body)

            @block.gpsimd
            def _(pool):
                for _ in range(C_AL):
                    pool.sem_inc(s_al, 1)
                S.features_pool(pool, lambda k: K.h[:, k, :])

                def body(t, steps, last):
                    for i in range(2 * steps):
                        pool.wait_ge(s_act, i + 1 + C_ACT + 8 * t)
                        nc.gpsimd.tensor_tensor(ah[:, i, :], a[:, i % 2, :], K.k("ones")[:, 0:1].broadcast_to([P, T]), ALU.mult)
                        pool.drain()
                        nc.gpsimd.tensor_tensor(al[:, i, :], a[:, i % 2, :], ah[:, i, :].bitcast(F32), ALU.subtract).then_inc(s_al, 1)
                thirds(pool, body)


def linear_stage(K, name, tiles, banks=8, scalar=lambda t: t % 2 == 1, extra=None, src=None, norm=None):
    nc, plan = K.nc, K.plan
    extra = extra or {}
    src = src or (lambda k: K.h[:, k, :])
    with stage(K, name) as st:
        S = Split(K, st, norm)
        s_v, s_s = st.sems("vector_out", "scalar_out")
        mine = [scalar(t) for t in range(len(tiles))]
        if "sems" in extra:
            extra["sems"](st)
        if "box" in extra:
            extra["box"]["read"] = s_v
        chunks = []
        for t, (seg, j, _, _, _, _, _, words) in enumerate(tiles):
            if not chunks or chunks[-1][:2] != (seg, j):
                chunks.append((seg, j, words, []))
            chunks[-1][3].append(t)

        with nc.Block() as block:
            @block.sync
            def _(sp):
                if "sync" in extra:
                    extra["sync"](sp)
                K.stream(sp, plan.end(tiles[-1][0]) + RING)

            @block.tensor
            def _(pe):
                S.sums(pe)
                for seg, j, _, members in chunks:
                    w = S.chunk(pe, seg, j, tiles[members[0]][3])
                    for t in members:
                        shape = tiles[t][5]
                        if t >= banks:
                            o = t - banks
                            pe.wait_ge(s_s if mine[o] else s_v, sum(x == mine[o] for x in mine[:o + 1]))
                        product3(pe, K.bank[t % banks][0:shape[0], 0:shape[1]], tiles[t][4](S, pe, w, t == 0)).then_inc(K.tiles_done, 1)
                if "tensor" in extra:
                    extra["tensor"](pe)

            def evacuate(e, side, split):
                for n, (seg, j, words, members) in enumerate(chunks):
                    if n + 1 < len(chunks):
                        a, b, w, _ = chunks[n + 1]
                        split(e, a, b, 0, w)
                    for t in members:
                        if mine[t] == side:
                            e.wait_ge(K.tiles_done, plan.tile(seg, j, tiles[t][2]))
                            shape = tiles[t][5]
                            ins = tiles[t][6](K.bank[t % banks][0:shape[0], 0:shape[1]], "scalar" if side else "vector")
                            ins.then_inc(s_s if side else s_v, 1)
                        elif "helper" in extra:
                            extra["helper"](e, t, K.bank[t % banks])

            @block.scalar
            def _(act):
                S.squares(act)
                S.high(act, chunks[0][0], chunks[0][1], 0, chunks[0][2])
                S.features_scalar(act)
                evacuate(act, True, S.high)
                if "scalar" in extra:
                    extra["scalar"](act)

            @block.vector
            def _(dve):
                S.low(dve, chunks[0][0], chunks[0][1], 0, chunks[0][2])
                S.features_vector(dve, src)
                if "before" in extra:
                    extra["before"](dve)
                evacuate(dve, False, S.low)
                if "vector" in extra:
                    extra["vector"](dve)

            @block.gpsimd
            def _(pool):
                S.features_pool(pool, src)


def copier(nc, dst, scale=None):
    def go(bank, engine):
        if engine == "scalar":
            return nc.scalar.copy(dst, bank) if scale is None else nc.scalar.activation(dst, bank, ACT.Copy, scale=scale)
        return nc.vector.tensor_copy(dst, bank) if scale is None else nc.vector.tensor_scalar(dst, bank, scale, None, ALU.mult)
    return go


def feature_pairs(c0, rows=P):
    return lambda S, pe, w, wait: (((w[0][:, k, c0:c0 + rows], w[1][:, k, c0:c0 + rows]), S.feature(pe, k, wait))
                                   for k in range(KD))


def token_pairs(b):
    return lambda S, pe, w, wait: ((S.feature(pe, k, wait, slice(b * P, (b + 1) * P)), (w[0][:, k, :], w[1][:, k, :]))
                                   for k in range(KD))


def out_stage(K, name, y, residual):
    nc = K.nc

    def evac(n):
        if residual:
            return lambda bank, engine: nc.vector.tensor_tensor(K.x[:, n, :], bank, K.x[:, n, :], ALU.add)
        return copier(nc, K.h[:, n, :])

    tiles = [(name, n // 2, n % 2, WC, feature_pairs((n % 2) * P), (P, T), evac(n), SLOT) for n in range(KD)]
    linear_stage(K, name, tiles, scalar=(lambda t: False) if residual else (lambda t: t % 2 == 1), src=y)


def finish_stage(K):
    nc = K.nc
    with stage(K, "finish") as st:
        out = st.sb("out", [P, TB, D])
        s_t, s_c, s_d = st.sems("turned", "copied", "stored")
        with nc.Block() as block:
            @block.tensor
            def _(pe):
                for t in range(TB):
                    for half in range(2):
                        for k in range(4):
                            last = pe.transpose(K.bank[2 * t + half][:, k * P:(k + 1) * P],
                                                K.h[:, 4 * half + k, t * P:(t + 1) * P], K.k("ident"))
                        last.then_inc(s_t, 1)

            @block.vector
            def _(dve):
                for n in range(2 * TB):
                    dve.wait_ge(s_t, n + 1)
                    nc.vector.tensor_copy(out[:, n // 2, (n % 2) * 512:(n % 2) * 512 + 512], K.bank[n][:, :]).then_inc(s_c, 1)

            @block.sync
            def _(sp):
                for t in range(TB):
                    sp.wait_ge(s_c, 2 * t + 2)
                    sp.dma_start(K.io["out"][0, t * P:(t + 1) * P, :], out[:, t, :]).then_inc(s_d, 16)
                sp.wait_ge(s_d, 16 * TB)


def in_proj_stage(K, M, norm):
    nc, plan, io = K.nc, K.plan, K.io
    w_in = io["w_in"][0].rearrange("(k p) n -> p k n", p=P)
    box = {}

    def shifted(t, rows, mu, dst):
        def go(bank, engine):
            nc.vector.wait_ge(box["part_done"], t - 2)
            return nc.vector.scalar_tensor_tensor(dst, bank, K.coef[0:rows, 40 + mu:41 + mu],
                                                  box["part"][0:rows, t % 2, 0:T], ALU.mult, ALU.add)
        return go

    tiles = [("in_q", 0, m, WC, feature_pairs(m * P), (P, T), copier(nc, M.cq[:, m, :]), SLOT) for m in range(2)]
    tiles.append(("in_kv", 0, 0, P, feature_pairs(0), (P, T), copier(nc, M.ckv[:, :]), KD * P))
    mus = [None] * 3
    for n in range(12):
        tiles.append(("in_rkv", n // 2, n % 2, WC, feature_pairs((n % 2) * P), (P, T), shifted(3 + n, P, n, M.rkv[:, n, :]), SLOT))
        mus.append(n)
    for n, (seg, m, width, rows, dst) in enumerate((("in_lora", 0, WC, P, M.wa), ("in_lora", 1, WC, P, M.g), ("in_lora2", 0, 32, 32, M.g2))):
        tiles.append((seg, 0, m, width, feature_pairs(m * P, rows), (rows, T), shifted(15 + n, rows, 12 + n, dst[0:rows, :]), KD * width))
        mus.append(12 + n)

    def sems(st):
        box["wik"], box["wiw"] = st.sb("wik", [P, KD, 2 * IDX_D]), st.sb("wiw", [P, KD, 8])
        box["part"] = st.sb("part", [P, 2, T + 1])
        box["w"], box["side"], box["part_done"], box["zero"] = st.sems("side_in", "side", "part", "zero")
        box["evac"] = None

    def sync(sp):
        for half in range(2):
            sp.dma_start(box["wik"][:, :, half * IDX_D:(half + 1) * IDX_D], w_in[:, :, O_IK:O_IW]).then_inc(box["w"], 16)
        sp.dma_start(box["wiw"][:, :, :], w_in[:, :, O_IW:O_R]).then_inc(box["w"], 16)

    def tensor(pe):
        pe.wait_ge(box["w"], 48)
        product(pe, K.bank[6][:, :], [(box["wik"][:, k, :], K.h[:, k, :]) for k in range(KD)]).then_inc(box["side"], 1)
        for b in range(TB):
            last = product(pe, K.bank[7][:, 8 * b:8 * b + 8],
                           [(K.h[:, k, b * P:(b + 1) * P], box["wiw"][:, k, :]) for k in range(KD)])
        last.then_inc(box["side"], 1)

    def before(dve):
        nc.vector.memset(box["part"][:, :, 0:1], 0.0).then_inc(box["zero"], 1)
        nc.vector.tensor_scalar(K.coef[:, 40:55], K.par[:, COL["mu_rkv"]:COL["mu_rkv"] + 15], -1.0, 1.0, ALU.mult, ALU.add)
        dve.drain()

    def helper(e, t, bank):
        seg, j, m, _, _, shape, _, _ = tiles[t]
        if mus[t] is None:
            return
        if t == 3:
            e.wait_ge(box["zero"], 1)
        e.wait_ge(K.tiles_done, plan.tile(seg, j, m))
        if t >= 5:
            e.wait_ge(box["read"], t - 1)
        nc.scalar.activation(box["part"][0:shape[0], t % 2, 1:T + 1], bank[0:shape[0], :], ACT.Copy,
                             scale=K.p("mu_rkv", mus[t])[0:shape[0], :]).then_inc(box["part_done"], 1)

    def vector(dve):
        dve.wait_ge(box["side"], 1)
        nc.vector.tensor_copy(M.ik[:, :], K.bank[6][:, :])
        dve.wait_ge(box["side"], 2)
        nc.vector.tensor_scalar(M.iw[:, :], K.bank[7][:, 0:32], (8 * IDX_D) ** -0.5, None, ALU.mult)

    linear_stage(K, "inproj", tiles, banks=6, scalar=lambda t: False,
                 extra={"sems": sems, "box": box, "sync": sync, "tensor": tensor, "before": before, "helper": helper, "vector": vector}, norm=norm)


IDX_D = 64


def small_norm(K, name, tiles, gains, width):
    nc = K.nc

    def write(engine, i, e):
        return nc.vector.scalar_tensor_tensor(tiles[i], tiles[i], gains[i], K.rstd[:, :], ALU.mult, ALU.mult)

    norm_stage(K, name, lambda i: tiles[i], len(tiles), width, write)


def dsa_prep_stage(K, A, M):
    nc, io = K.nc, K.io
    with stage(K, "dsaprep") as st:
        wuq = st.sb("wuq", [P, 2, 512])
        wiq = st.sb("wiq", [P, 2, 512])
        wuk = st.sb("wuk", [P, 512])
        wukt = st.sb("wukt", [P, 4, P])
        rb = st.sb("rb", [32, 8])
        bucket = st.sb("bucket", [32, 640])
        rev = st.sb("rev", [8, 640])
        shifted = A.o
        q = st.sb("q", [P, 4, T])
        far = nc.dram_tensor("bias_by_distance", (8, 640), F32, kind="Internal").ap()
        s_w, s_rb, s_rev, s_far, s_sh, s_pe, s_ev = st.sems("w", "rb", "rev", "far", "sh", "pe", "ev")
        steps = []

        def put(mms, evac):
            steps.append((mms, evac))

        idt = K.k("ident")
        put([(K.bank[0][0:8, :], rb[:, :], bucket[:, 0:512])], lambda: nc.scalar.copy(rev[:, 0:512], K.bank[0][0:8, :]))
        put([(K.bank[1][0:8, 0:128], rb[:, :], bucket[:, 512:640])],
            lambda: nc.scalar.activation(rev[:, 512:640], K.bank[1][0:8, 0:128], ACT.Copy, bias=-BIG, scale=0.0))
        n_rev = len(steps)
        put([(K.bank[2][:, n * P:(n + 1) * P], wuk[:, n * P:(n + 1) * P], None) for n in range(4)],
            lambda: nc.scalar.copy(wukt[:, :, :].rearrange("p a b -> p (a b)"), K.bank[2][:, :]))
        n_ukt = len(steps)
        put([(K.bank[3][:, b * P:(b + 1) * P], M.ckv[:, b * P:(b + 1) * P], None) for b in range(4)],
            lambda: nc.scalar.copy(A.ckvt[:, :, :].rearrange("p a b -> p (a b)"), K.bank[3][:, :]))
        for n in range(4):
            b = (4 + n) % 8
            put([(K.bank[b][:, :], wuq[:, k, n * P:(n + 1) * P], M.cq[:, k, :]) for k in range(2)],
                lambda n=n, b=b: nc.scalar.copy(q[:, n, :], K.bank[b][:, :]))
        n_q = len(steps)
        for n in range(4):
            put([(K.bank[n][:, :], wiq[:, k, n * P:(n + 1) * P], M.cq[:, k, :]) for k in range(2)],
                lambda n=n: nc.scalar.copy(A.iq[:, n, :], K.bank[n][:, :]))
        for h in range(8):
            r, b = slice((h % 2) * 64, (h % 2) * 64 + 64), (4 + h) % 8
            put([(K.bank[b][:, :], wukt[r, h // 2, :], q[r, h // 2, :])],
                lambda h=h, b=b: nc.scalar.mul(A.qa[:, h, :], K.bank[b][:, :], HD ** -0.5))
        n_flip = len(steps)
        for h in range(8):
            b = (4 + h) % 8
            put([(K.bank[b][:, :], K.k("flip"), shifted[:, h, :])],
                lambda h=h, b=b: nc.scalar.copy(A.bias[:, h, :], K.bank[b][:, :]))

        with nc.Block() as block:
            @block.sync
            def _(sp):
                sp.dma_start(rb[:, :], io["rel_bias"]).then_inc(s_rb, 16)
                sp.dma_start(bucket[:, :], io["bucket"]).then_inc(s_rb, 16)
                for h in range(8):
                    sp.dma_start(wuk[:, h * 64:(h + 1) * 64], io["w_uk"][0, h]).then_inc(s_w, 16)
                    sp.dma_start(A.wuv[:, h, :], io["w_uv"][0, h]).then_inc(s_w, 16)
                sp.dma_start(wuq[:, :, :], io["w_uq"][0].rearrange("(k p) h d -> p k (h d)", p=P)).then_inc(s_w, 16)
                sp.dma_start(wiq[:, :, :], io["w_idx_q"][0].rearrange("(k p) h d -> p k (h d)", p=P)).then_inc(s_w, 16)
                sp.wait_ge(s_ev, n_rev)
                sp.dma_start(far, rev[:, :]).then_inc(s_far, 16)
                sp.wait_ge(s_far, 16)
                sp.dma_start(shifted[:, :, :], bass.AP(tensor=far.tensor, offset=0, ap=[[1, P], [640, 8], [1, T]])).then_inc(s_sh, 16)

            @block.tensor
            def _(pe):
                pe.wait_ge(s_rb, 32)
                for n, (mms, _) in enumerate(steps):
                    if n == n_rev:
                        pe.wait_ge(s_w, 16 * 18)
                    if n == n_flip:
                        pe.wait_ge(s_sh, 16)
                    need = max(n_q if n >= n_q + 4 else 0, n - 3)
                    if need > 0:
                        pe.wait_ge(s_ev, need)
                    for m, (out, a, b) in enumerate(mms):
                        if b is None:
                            last = pe.transpose(out, a, idt)
                        else:
                            last = pe.matmul(out, a, b, start=m == 0, stop=m == len(mms) - 1)
                    last.then_inc(s_pe, 1)

            @block.scalar
            def _(act):
                for n, (_, evac) in enumerate(steps):
                    act.wait_ge(s_pe, n + 1)
                    evac().then_inc(s_ev, 1)


def topk_stage(K, A, M):
    nc = K.nc
    with stage(K, "topk") as st:
        relu = st.sb("relu", [P, 2, T])
        sc = st.sb("scores", [P, 3, T])
        top = st.sb("top", [P, 8])
        s_pe, s_relu, s_acc, s_done, s_mask = st.sems("dots", "relu", "acc", "scored", "masked")
        mod = Modulation(K, st, "mod2", 16)
        with nc.Block() as block:
            @block.sync
            def _(sp):
                K.stream(sp, K.plan.end("mod2") + RING)

            @block.tensor
            def _(pe):
                for i in range(1, TB):
                    n = (i + 1) * P
                    for h in range(8):
                        m = (i - 1) * 8 + h
                        r = slice((h % 2) * 64, (h % 2) * 64 + 64)
                        if m >= 4:
                            pe.wait_ge(s_relu, m - 3)
                        pe.matmul(K.bank[m % 4][:, 0:n], A.iq[r, h // 2, i * P:(i + 1) * P], M.ik[r, 0:n],
                                  start=True, stop=True).then_inc(s_pe, 1)
                mod.tensor(pe)

            @block.scalar
            def _(act):
                for m in range(24):
                    n = (m // 8 + 2) * P
                    act.wait_ge(s_pe, m + 1)
                    if m >= 2:
                        act.wait_ge(s_acc, m - 1)
                    nc.scalar.activation(relu[:, m % 2, 0:n], K.bank[m % 4][:, 0:n], ACT.Relu).then_inc(s_relu, 1)
                mod.scalar(act)

            @block.gpsimd
            def _(pool):
                for i in range(1, TB):
                    pool.wait_ge(s_done, i)
                    part = sc[:, i - 1, i * P:(i + 1) * P]
                    nc.gpsimd.affine_select(out=part, in_=part, compare_op=ALU.is_ge, fill=CAUSAL_FILL, base=0,
                                            pattern=[[-1, P]], channel_multiplier=1).then_inc(s_mask, 1)

            @block.vector
            def _(dve):
                for m in range(24):
                    i, h = m // 8 + 1, m % 8
                    n = (i + 1) * P
                    dve.wait_ge(s_relu, m + 1)
                    acc, w = sc[:, i - 1, 0:n], M.iw[:, 8 * i + h:8 * i + h + 1]
                    if h == 0:
                        ins = nc.vector.tensor_scalar(acc, relu[:, m % 2, 0:n], w, None, ALU.mult)
                    else:
                        ins = nc.vector.scalar_tensor_tensor(acc, relu[:, m % 2, 0:n], w, acc, ALU.mult, ALU.add)
                    ins.then_inc(s_acc, 1)
                    if h == 7:
                        dve.drain()
                        dve.sem_inc(s_done, 1)
                    else:
                        dve.drain()
                for i in range(1, TB):
                    n = (i + 1) * P
                    buf = sc[:, i - 1, 0:n]
                    dve.wait_ge(s_mask, i)
                    for _ in range(TOPK // 8):
                        nc.vector.max(top[:, :], buf)
                        dve.drain()
                        nc.vector.match_replace(buf, top[:, :], buf, TAKEN)
                        dve.drain()
                    nc.vector.tensor_scalar(A.mask[:, i - 1, 0:n], buf, TAKEN, -BIG, ALU.not_equal, ALU.mult)
                mod.vector(dve)


def attention_stage(K, name, H, rows, q, k, v, vw, dest, bias=None, prep=None):
    nc = K.nc
    items = [(h, i) for h in range(H) for i in range(TB)]
    N = len(items)
    with stage(K, name) as st:
        S = st.sb("S", [P, 3, T])
        pt = st.sb("pt", [P, 2, T])
        bm = st.sb("bm", [P, 2, T]) if prep else None
        stat = st.sb("stat", [P, 4, 4])
        s_score, s_bm, s_biased, s_exp, s_norm, s_turned, s_pt, s_pv, s_out = st.sems(
            "scored", "bias_made", "biased", "exp", "normed", "turned", "probs_out", "pv", "out")
        lo = lambda h: (h % 2) * 64 if vw == 64 else 0
        with nc.Block() as block:
            @block.sync
            def _(sp):
                pass

            @block.tensor
            def _(pe):
                for n in range(N + 3):
                    if n < N:
                        h, i = items[n]
                        if n >= 2:
                            pe.wait_ge(s_biased, n - 1)
                        w = (i + 1) * P
                        pe.matmul(K.bank[n % 2][:, 0:w], q(h, i), k(h, w), start=True, stop=True).then_inc(s_score, 1)
                    if 2 <= n <= N + 1:
                        m = n - 2
                        h, i = items[m]
                        pe.wait_ge(s_norm, m + 1)
                        if m >= 2:
                            pe.wait_ge(s_pt, m - 1)
                        for s in range(i + 1):
                            last = pe.transpose(K.bank[2 + m % 2][:, s * P:(s + 1) * P], S[:, m % 3, s * P:(s + 1) * P], K.k("ident"))
                        last.then_inc(s_turned, 1)
                    if n >= 3:
                        m = n - 3
                        h, i = items[m]
                        pe.wait_ge(s_pt, m + 1)
                        if m >= 2:
                            pe.wait_ge(s_out, m - 1)
                        product(pe, K.bank[4 + m % 2][lo(h):lo(h) + vw, 0:P],
                                [(v(h, s), pt[:, m % 2, s * P:(s + 1) * P]) for s in range(i + 1)]).then_inc(s_pv, 1)

            @block.gpsimd
            def _(pool):
                if prep:
                    for n, (h, i) in enumerate(items):
                        if n >= 2:
                            pool.wait_ge(s_biased, n - 1)
                        prep(pool, bm[:, n % 2, 0:(i + 1) * P], h, i).then_inc(s_bm, 1)

            @block.vector
            def _(dve):
                for n in range(N + 1):
                    if n < N:
                        h, i = items[n]
                        w = (i + 1) * P
                        dve.wait_ge(s_score, n + 1)
                        if prep:
                            dve.wait_ge(s_bm, n + 1)
                        if n >= 3:
                            dve.wait_ge(s_turned, n - 2)
                        table = bm[:, n % 2, 0:w] if prep else bias(h, i)
                        nc.vector.tensor_tensor_reduce(out=S[:, n % 3, 0:w], in0=K.bank[n % 2][:, 0:w], in1=table, scale=1.0,
                                                       scalar=-3.0e38, op0=ALU.add, op1=ALU.max, accum_out=stat[:, n % 4, 0:1])
                        dve.drain()
                        nc.vector.tensor_scalar(stat[:, n % 4, 1:2], stat[:, n % 4, 0:1], -1.0, None, ALU.mult).then_inc(s_biased, 1)
                    if n >= 1:
                        m = n - 1
                        w = (items[m][1] + 1) * P
                        dve.wait_ge(s_exp, m + 1)
                        nc.vector.reciprocal(stat[:, m % 4, 3:4], stat[:, m % 4, 2:3])
                        dve.drain()
                        nc.vector.tensor_scalar(S[:, m % 3, 0:w], S[:, m % 3, 0:w], stat[:, m % 4, 3:4], None, ALU.mult).then_inc(s_norm, 1)

            @block.scalar
            def _(act):
                for n in range(N + 3):
                    if n < N:
                        w = (items[n][1] + 1) * P
                        act.wait_ge(s_biased, n + 1)
                        nc.scalar.activation(S[:, n % 3, 0:w], S[:, n % 3, 0:w], ACT.Exp, bias=stat[:, n % 4, 1:2], scale=1.0,
                                             accum_out=stat[:, n % 4, 2:3]).then_inc(s_exp, 1)
                    if 2 <= n <= N + 1:
                        m = n - 2
                        w = (items[m][1] + 1) * P
                        act.wait_ge(s_turned, m + 1)
                        if m >= 2:
                            act.wait_ge(s_pv, m - 1)
                        nc.scalar.copy(pt[:, m % 2, 0:w], K.bank[2 + m % 2][:, 0:w]).then_inc(s_pt, 1)
                    if n >= 3:
                        m = n - 3
                        h, i = items[m]
                        act.wait_ge(s_pv, m + 1)
                        nc.scalar.copy(dest(h, i), K.bank[4 + m % 2][lo(h):lo(h) + vw, 0:P]).then_inc(s_out, 1)


def value_stage(K, A, y):
    nc = K.nc
    with stage(K, "value") as st:
        s_pe, = st.sems("pe")
        with nc.Block() as block:
            @block.tensor
            def _(pe):
                for h in range(8):
                    pe.matmul(K.bank[h // 2][(h % 2) * 64:(h % 2) * 64 + 64, :], A.wuv[:, h, :], A.o[:, h, :],
                              start=True, stop=True).then_inc(s_pe, 1)

            @block.vector
            def _(dve):
                for n in range(4):
                    dve.wait_ge(s_pe, 2 * n + 2)
                    nc.vector.tensor_copy(y[:, n, :], K.bank[n][:, :])


class Bag:
    pass


def mixer1(K, norm):
    nc = K.nc
    with ExitStack() as st:
        sb = lambda n, shape: st.enter_context(nc.sbuf_tensor(n, shape, F32))
        M = Bag()
        y = sb("y", [P, KD, T])
        M.cq, M.ckv, M.ik, M.iw = sb("cq", [P, 2, T]), sb("ckv", [P, T]), sb("ik", [P, T]), sb("iw", [P, 32])
        with ExitStack() as rs:
            rb = lambda n, shape: rs.enter_context(nc.sbuf_tensor(n, shape, F32))
            M.rkv, M.wa, M.g, M.g2 = rb("rkv", [P, 12, T]), rb("wa", [P, T]), rb("g", [P, T]), rb("g2", [32, T])
            in_proj_stage(K, M, norm)
            rwkv(K, M, y)
        with ExitStack() as as_:
            ab = lambda n, shape: as_.enter_context(nc.sbuf_tensor(n, shape, F32))
            A = Bag()
            A.qa = K.h
            A.iq, A.ckvt, A.bias = ab("iq", [P, 4, T]), ab("ckvt", [P, TB, P]), ab("bias", [P, 8, T])
            A.o, A.wuv, A.mask = ab("o", [P, 8, T]), ab("wuv", [P, 8, 64]), ab("mask", [P, 3, T])
            small_norm(K, "norm_q", [M.cq[:, 0, :], M.cq[:, 1, :]], [K.p("q_norm", 0), K.p("q_norm", 1)], 256)
            small_norm(K, "norm_kv", [M.ckv[:, :]], [K.p("kv_norm")], 128)
            small_norm(K, "norm_ik", [M.ik[:, :]], [K.p("idx_k_norm")], 128)
            dsa_prep_stage(K, A, M)
            topk_stage(K, A, M)

            def prep(pool, out, h, i):
                w = (i + 1) * P
                table = A.bias[:, h, 384 - i * P:384 - i * P + w]
                if i == 0:
                    return nc.gpsimd.tensor_copy(out, table)
                return nc.gpsimd.tensor_tensor(out, table, A.mask[:, i - 1, 0:w], ALU.add)

            attention_stage(K, "dsa", 8, P, lambda h, i: A.qa[:, h, i * P:(i + 1) * P], lambda h, w: M.ckv[:, 0:w],
                            lambda h, s: A.ckvt[:, s, :], P, lambda h, i: A.o[:, h, i * P:(i + 1) * P], prep=prep)
            value_stage(K, A, y)
        out_stage(K, "out1", lambda k: y[:, k, :], False)


def rwkv_prep_stage(K, M, R, p):
    nc, io = K.nc, K.io
    r, k, v = M.rkv[:, p, :], M.rkv[:, 4 + p, :], M.rkv[:, 8 + p, :]
    tmp = lambda i: K.h[:, i, :]
    lw, L, a, kk, t0, eN, eA, eC = (tmp(i) for i in range(8))
    chunks = lambda ap: ap.rearrange("p (c t) -> p c t", t=C)
    with stage(K, f"rprep{p}") as st:
        s_w, s_lora, s_dots, s_sig, s_kk, s_sq, s_norm, s_root, s_l, s_exp, s_bd, s_zero = st.sems(
            "w", "lora", "dots", "sigmoid", "kk", "square", "norm", "root", "logs", "exp", "scaled", "zero")
        with nc.Block() as block:
            @block.sync
            def _(sp):
                if p == 0:
                    sp.dma_start(R.wl[0:64, :], io["w_decay_up"][0]).then_inc(s_w, 16)
                    sp.dma_start(R.wl[64:128, :], io["w_aaa_up"][0]).then_inc(s_w, 16)

            @block.tensor
            def _(pe):
                if p == 0:
                    pe.wait_ge(s_w, 32)
                    pe.wait_ge(s_lora, 1)
                pe.matmul(K.bank[0][:, :], R.wl[0:64, p * P:(p + 1) * P], M.wa[0:64, :], start=True, stop=True).then_inc(s_dots, 1)
                pe.matmul(K.bank[1][:, :], R.wl[64:128, p * P:(p + 1) * P], M.wa[64:128, :], start=True, stop=True).then_inc(s_dots, 1)
                pe.wait_ge(s_sq, 1)
                pe.matmul(K.bank[2][:, :], K.k("heads"), t0, start=True, stop=True).then_inc(s_norm, 1)

            @block.scalar
            def _(act):
                if p == 0:
                    nc.scalar.activation(M.wa[0:64, :], M.wa[0:64, :], ACT.Tanh).then_inc(s_lora, 1)
                    nc.scalar.activation(M.g[:, :], M.g[:, :], ACT.Sigmoid)
                    nc.scalar.activation(M.g2[:, :], M.g2[:, :], ACT.Sigmoid)
                act.wait_ge(s_dots, 1)
                nc.scalar.activation(lw, K.bank[0][:, :], ACT.Sigmoid, bias=K.p("w0", p)).then_inc(s_sig, 1)
                act.wait_ge(s_dots, 2)
                nc.scalar.activation(a, K.bank[1][:, :], ACT.Sigmoid, bias=K.p("a0", p)).then_inc(s_sig, 1)
                act.wait_ge(s_kk, 1)
                nc.scalar.activation(t0, kk, ACT.Square).then_inc(s_sq, 1)
                act.wait_ge(s_norm, 1)
                nc.scalar.activation(t0, K.bank[2][:, :], ACT.Sqrt).then_inc(s_root, 1)
                act.wait_ge(s_l, 1)
                nc.scalar.activation(eA, eA, ACT.Exp).then_inc(s_exp, 1)
                nc.scalar.activation(eN, L, ACT.Exp, scale=-1.0).then_inc(s_exp, 1)
                nc.scalar.activation(eC, eC, ACT.Exp).then_inc(s_exp, 1)
                nc.scalar.activation(R.eP[:, :], L, ACT.Exp).then_inc(s_exp, 1)

            @block.gpsimd
            def _(pool):
                if p == 0:
                    for n in range(6):
                        nc.gpsimd.memset(R.bd[:, n, :, :], 0.0)
                    pool.drain().then_inc(s_zero, 1)
                    pool.wait_ge(s_zero, 1)
                for hh in range(2):
                    q = slice(64 * hh, 64 * hh + 64)
                    nc.gpsimd.tensor_copy(R.bd[q, 5, :, q], chunks(v)[q])
                pool.wait_ge(s_bd, 1)
                pool.wait_ge(s_exp, 3)
                for hh in range(2):
                    q = slice(64 * hh, 64 * hh + 64)
                    nc.gpsimd.tensor_tensor(R.bd[q, 3, :, q], chunks(k)[q], chunks(eC)[q], ALU.mult)
                    nc.gpsimd.tensor_tensor(R.bd[q, 4, :, q], chunks(a)[q], chunks(eC)[q], ALU.mult)

            @block.vector
            def _(dve):
                nc.vector.tensor_scalar(kk, k, K.p("k_k", p), None, ALU.mult).then_inc(s_kk, 1)
                nc.vector.tensor_scalar(R.oka[:, :], K.p("k_a", p), -1.0, 1.0, ALU.mult, ALU.add)
                dve.wait_ge(s_sig, 1)
                nc.vector.tensor_scalar(lw, lw, NEG_SQRT_E, None, ALU.mult)
                dve.drain()
                nc.vector.tensor_tensor_scan(L, K.k("reset"), lw, 0.0, ALU.mult, ALU.add)
                dve.drain()
                nc.vector.tensor_tensor(eA, L, lw, ALU.subtract)
                end = chunks(L)[:, :, C - 1:C].broadcast_to([P, NCH, C])
                nc.vector.tensor_tensor(chunks(eC), end, chunks(L), ALU.subtract).then_inc(s_l, 1)
                dve.wait_ge(s_root, 1)
                nc.vector.tensor_scalar(t0, t0, 1e-12, None, ALU.max)
                dve.drain()
                nc.vector.reciprocal(t0, t0)
                dve.drain()
                nc.vector.scalar_tensor_tensor(kk, kk, -1.0, t0, ALU.mult, ALU.mult)
                dve.drain()
                dve.wait_ge(s_sig, 2)
                nc.vector.tensor_scalar(t0, a, K.p("k_a", p), R.oka[:, :], ALU.mult, ALU.add)
                dve.drain()
                nc.vector.tensor_tensor(k, k, t0, ALU.mult)
                nc.vector.scalar_tensor_tensor(a, kk, -1.0, a, ALU.mult, ALU.mult)
                dve.drain().then_inc(s_bd, 1)
                if p == 0:
                    dve.wait_ge(s_zero, 1)
                dve.wait_ge(s_exp, 1)
                for n, (x, e) in enumerate(((kk, eA), (a, eN), (k, eN))):
                    if n == 1:
                        dve.wait_ge(s_exp, 2)
                    for hh in range(2):
                        q = slice(64 * hh, 64 * hh + 64)
                        nc.vector.tensor_tensor(R.bd[q, n, :, q], chunks(x)[q], chunks(e)[q], ALU.mult)
                dve.wait_ge(s_exp, 4)
                nc.vector.tensor_tensor(R.rt[:, :], r, R.eP[:, :], ALU.mult)


def rwkv_chunk_stage(K, R, p, yout):
    nc = K.nc
    BD_A, BD_B, BD_K, BD_KH, BD_BH, BD_V = range(6)
    idt = K.k("ident")
    wide = lambda ap: ap.unsqueeze(1).broadcast_to([P, 4, P])
    with stage(K, f"rchunk{p}") as st:
        G = []
        for g in range(2):
            B = Bag()
            B.vt, B.kht, B.bht = (K.h[:, 2 + 3 * g + n, :].rearrange("p (c t) -> p c t", t=P) for n in range(3))
            B.at, B.akt, B.nt, B.T, B.TT, B.X, B.rbk = (
                st.sb(f"{n}{g}", [P, 4, P]) for n in ("at", "akt", "nt", "t", "tt", "x", "rbk"))
            G.append(B)
        S = st.sb("state", [P, 2, P])
        s_pe, s_dve, s_act, s_sp, s_sv = st.sems("products", "vector_out", "scalar_out", "state_product", "state")
        steps = []

        def flat(t):
            return t[:, :, :].rearrange("p a b -> p (a b)")

        def add(g, mms, evacs):
            steps.append((g, mms, evacs))

        def group_steps(g):
            B = G[g]
            b0 = 4 * g
            bd = lambda n, c: R.bd[:, n, 4 * g + c, :]
            rt = lambda c: R.rt[:, (4 * g + c) * C:(4 * g + c + 1) * C]
            out = []

            def put(mms, evacs):
                out.append((g, mms, evacs))

            def full(lhs, rhs, bank, w=P, at=0, more=None):
                ms = []
                for c in range(4):
                    o = K.bank[bank][:, c * P + at:c * P + at + w]
                    ms.append((o, lhs(c), rhs(c), True, more is None))
                    if more:
                        ms.append((o, more[0](c), more[1](c), False, True))
                return ms

            def turn(n, bank):
                return [(K.bank[bank][:, c * P:(c + 1) * P], bd(n, c), None, True, True) for c in range(4)]

            v = nc.vector
            a = nc.scalar
            bank = lambda n: K.bank[b0 + n][:, :]
            bank3 = lambda n: K.bank[b0 + n][:, :].rearrange("p (c t) -> p c t", t=P)
            sl = lambda t: (lambda c: t[:, c, :])
            put(full(lambda c: bd(BD_B, c), lambda c: bd(BD_A, c), b0),
                [("dve", lambda: v.tensor_tensor(B.nt[:, :, :], bank3(0), wide(K.k("strict")), ALU.mult)),
                 ("dve", lambda: v.tensor_tensor(B.TT[:, :, :], bank3(0), wide(K.k("first_t")), ALU.mult))])
            put(full(lambda c: bd(BD_A, c), lambda c: bd(BD_B, c), b0 + 1),
                [("dve", lambda: v.tensor_tensor(B.T[:, :, :], bank3(1), wide(K.k("first")), ALU.mult)),
                 ("dve", lambda: v.tensor_tensor(B.TT[:, :, :], B.TT[:, :, :], wide(idt), ALU.add)),
                 ("drain", None),
                 ("dve", lambda: v.tensor_tensor(B.T[:, :, :], B.T[:, :, :], wide(idt), ALU.add))])
            turns = [(BD_V, B.vt), (BD_KH, B.kht), (BD_BH, B.bht), (BD_A, B.at)]
            extra = []
            for m, (n, dst) in enumerate(turns):
                extra.append((g, turn(n, b0 + 3), [("act", lambda dst=dst: a.copy(flat(dst), bank(3)))]))
            extra.append((g, full(lambda c: bd(BD_K, c), lambda c: bd(BD_A, c), b0 + 3),
                [("dve", lambda: v.tensor_tensor(B.akt[:, :, :], bank3(3), wide(K.k("strict")), ALU.mult))]))
            up = K.k("upto").unsqueeze(1).broadcast_to([P, 8, C])
            extra.append((g, full(lambda c: bd(BD_B, c), rt, b0 + 3, C) + full(lambda c: bd(BD_K, c), rt, b0 + 3, C, C),
                [("dve", lambda: v.tensor_tensor(B.rbk[:, :, :].rearrange("p a (b t) -> p (a b) t", t=C),
                                                 K.bank[b0 + 3][:, :].rearrange("p (c t) -> p c t", t=C), up, ALU.mult))]))
            extra.append((g, full(sl(B.akt), sl(B.vt), b0 + 3), [("act", lambda: a.copy(flat(B.akt), bank(3)))]))
            for s in LEVELS[1:]:
                put(full(sl(B.nt), sl(B.T), b0),
                    [("dve", lambda s=s: v.tensor_tensor(B.X[:, :, :], bank3(0), wide(K.k(f"low{s}")), ALU.mult))])
                if extra:
                    out.append(extra.pop(0))
                last = s == LEVELS[-1]
                mms = full(sl(B.X), sl(B.TT), b0 + 2)
                ev = [("dve", lambda: v.tensor_tensor(B.TT[:, :, :], bank3(2), B.TT[:, :, :], ALU.add))]
                if not last:
                    mms = full(sl(B.TT), sl(B.X), b0 + 1) + mms
                    ev = [("dve", lambda: v.tensor_tensor(B.T[:, :, :], bank3(1), B.T[:, :, :], ALU.add))] + ev
                put(mms, ev)
                if extra:
                    out.append(extra.pop(0))
            assert not extra
            put(full(sl(B.TT), sl(B.at), b0), [("act", lambda: a.copy(flat(B.X), bank(0)))])
            put(full(sl(B.TT), sl(B.akt), b0 + 1), [("act", lambda: a.copy(flat(B.T), bank(1)))])
            ta, takv = B.X, B.T
            rb = lambda c: B.rbk[:, c, 0:C]
            rk = lambda c: B.rbk[:, c, C:P]

            def m_out(c):
                end = R.eP[:, (4 * g + c + 1) * C - 1:(4 * g + c + 1) * C]
                return lambda: v.scalar_tensor_tensor(R.M[:, 4 * g + c, :], idt, end, K.bank[b0 + 2][:, c * P:(c + 1) * P], ALU.mult, ALU.add)

            put(full(sl(ta), sl(B.bht), b0 + 2), [("dve", m_out(c)) for c in range(4)])
            sp4 = lambda t: t[:, 4 * g * C:4 * (g + 1) * C].rearrange("p (c t) -> p c t", t=C)
            put(full(sl(ta), rb, b0 + 3, C),
                [("dve", lambda: v.tensor_tensor(sp4(R.Q), bank3(3)[:, :, 0:C], sp4(R.rt), ALU.add))])
            put(full(sl(B.bht), sl(takv), b0, P, 0, (sl(B.kht), sl(B.vt))),
                [("act", lambda: a.copy(R.Z[:, 4 * g:4 * g + 4, :].rearrange("p a b -> p (a b)"), bank(0)))])
            put(full(sl(takv), rb, b0 + 1, C, 0, (sl(B.vt), rk)),
                [("act", lambda: a.copy(sp4(R.Y), bank3(1)[:, :, 0:C]))])
            return out

        one, two = group_steps(0), group_steps(1)
        for x, z in zip(one, two):
            steps += [x, z]
        n_dve = [sum(e == "dve" for e, _ in ev) for _, _, ev in steps]
        n_act = [sum(e == "act" for e, _ in ev) for _, _, ev in steps]
        N = len(steps)

        with nc.Block() as block:
            @block.sync
            def _(sp):
                pass

            @block.tensor
            def _(pe):
                for n, (g, mms, _) in enumerate(steps):
                    if n >= 2:
                        d, a = sum(n_dve[:n - 1]), sum(n_act[:n - 1])
                        if d:
                            pe.wait_ge(s_dve, d)
                        if a:
                            pe.wait_ge(s_act, a)
                    for out, l, r, start, stop in mms:
                        if r is None:
                            last = pe.transpose(out, l, idt)
                        else:
                            last = pe.matmul(out, l, r, start=start, stop=stop)
                    last.then_inc(s_pe, 1)
                pe.wait_ge(s_dve, sum(n_dve))
                pe.wait_ge(s_act, sum(n_act))
                for c in range(1, NCH):
                    pe.wait_ge(s_sv, c)
                    if c < NCH - 1:
                        pe.matmul(K.bank[c % 2][:, 0:P], R.M[:, c, :], S[:, (c - 1) % 2, :], start=True, stop=True).then_inc(s_sp, 1)
                    last = pe.matmul(K.bank[2][:, c * C:(c + 1) * C], S[:, (c - 1) % 2, :], R.Q[:, c * C:(c + 1) * C], start=True, stop=True)
                last.then_inc(s_sp, 1)

            @block.vector
            def _(dve):
                for n, (g, _, evacs) in enumerate(steps):
                    if n_dve[n]:
                        dve.wait_ge(s_pe, n + 1)
                        dve.drain()
                    for e, f in evacs:
                        if e == "dve":
                            f().then_inc(s_dve, 1)
                        elif e == "drain":
                            dve.drain()
                dve.wait_ge(s_act, sum(n_act))
                nc.vector.tensor_copy(S[:, 0, :], R.Z[:, 0, :]).then_inc(s_sv, 1)
                for c in range(1, NCH - 1):
                    dve.wait_ge(s_sp, c)
                    nc.vector.tensor_tensor(S[:, c % 2, :], K.bank[c % 2][:, 0:P], R.Z[:, c, :], ALU.add).then_inc(s_sv, 1)
                dve.wait_ge(s_sp, NCH - 1)
                nc.vector.tensor_copy(yout[:, 0:C], R.Y[:, 0:C])
                nc.vector.tensor_tensor(yout[:, C:T], K.bank[2][:, C:T], R.Y[:, C:T], ALU.add)

            @block.scalar
            def _(act):
                for n, (g, _, evacs) in enumerate(steps):
                    if n_act[n]:
                        act.wait_ge(s_pe, n + 1)
                    for e, f in evacs:
                        if e == "act":
                            f().then_inc(s_act, 1)


def rwkv_finish_stage(K, M, y):
    nc, io = K.nc, K.io
    with stage(K, "rfin") as st:
        wg = st.sb("wg", [P, 512])
        wg2 = st.sb("wg2", [32, 512])
        sq = st.sb("sq", [P, 2, T])
        rs = st.sb("rs", [P, 2, T])
        s_w, s_mean, s_yc, s_sq, s_var, s_root, s_rk, s_bonus, s_done = st.sems(
            "w", "mean", "centred", "square", "var", "root", "rk", "bonus", "done")
        with nc.Block() as block:
            @block.sync
            def _(sp):
                sp.dma_start(wg[:, :], io["w_gate_up"][0, 0:P, :]).then_inc(s_w, 16)
                sp.dma_start(wg2[:, :], io["w_gate_up"][0, P:P + 32, :]).then_inc(s_w, 16)

            @block.tensor
            def _(pe):
                pe.wait_ge(s_w, 32)
                for p in range(4):
                    b = 4 * (p % 2)
                    if p >= 2:
                        pe.wait_ge(s_done, p - 1)
                    pe.matmul(K.bank[b][:, :], K.k("heads"), y[:, 4 + p, :], start=True, stop=True).then_inc(s_mean, 1)
                    pe.wait_ge(s_rk, p + 1)
                    pe.matmul(K.bank[b + 1][:, :], K.k("heads"), K.h[:, p, :], start=True, stop=True)
                    pe.matmul(K.bank[b + 2][:, :], wg[:, p * P:(p + 1) * P], M.g[:, :], start=True, stop=False)
                    pe.matmul(K.bank[b + 2][:, :], wg2[:, p * P:(p + 1) * P], M.g2[:, :], start=False, stop=True).then_inc(s_bonus, 1)
                    pe.wait_ge(s_sq, p + 1)
                    pe.matmul(K.bank[b + 3][:, :], K.k("heads"), sq[:, p % 2, :], start=True, stop=True).then_inc(s_var, 1)

            @block.scalar
            def _(act):
                for p in range(4):
                    act.wait_ge(s_yc, p + 1)
                    if p >= 2:
                        act.wait_ge(s_var, p - 1)
                        act.wait_ge(s_done, p - 1)
                    nc.scalar.activation(sq[:, p % 2, :], y[:, 4 + p, :], ACT.Square).then_inc(s_sq, 1)
                    act.wait_ge(s_var, p + 1)
                    nc.scalar.activation(rs[:, p % 2, :], K.bank[4 * (p % 2) + 3][:, :], ACT.Sqrt, bias=K.k("eps")[:, 1:2],
                                         scale=1.0 / HD).then_inc(s_root, 1)

            @block.vector
            def _(dve):
                for p in range(4):
                    nc.vector.scalar_tensor_tensor(K.h[:, p, :], M.rkv[:, p, :], K.p("r_k", p), M.rkv[:, 4 + p, :],
                                                   ALU.mult, ALU.mult).then_inc(s_rk, 1)
                for p in range(4):
                    b = 4 * (p % 2)
                    yt = y[:, 4 + p, :]
                    dve.wait_ge(s_mean, p + 1)
                    nc.vector.scalar_tensor_tensor(yt, K.bank[b][:, :], -1.0 / HD, yt, ALU.mult, ALU.add).then_inc(s_yc, 1)
                    dve.wait_ge(s_bonus, p + 1)
                    nc.vector.tensor_tensor(M.rkv[:, p, :], K.bank[b + 1][:, :], M.rkv[:, 8 + p, :], ALU.mult)
                    dve.wait_ge(s_root, p + 1)
                    nc.vector.reciprocal(rs[:, p % 2, :], rs[:, p % 2, :])
                    dve.drain()
                    nc.vector.scalar_tensor_tensor(yt, yt, K.p("ln_x_gain", p), rs[:, p % 2, :], ALU.mult, ALU.mult)
                    dve.drain()
                    nc.vector.scalar_tensor_tensor(yt, yt, K.p("ln_x_bias", p), M.rkv[:, p, :], ALU.add, ALU.add)
                    dve.drain()
                    nc.vector.tensor_tensor(yt, yt, K.bank[b + 2][:, :], ALU.mult).then_inc(s_done, 1)


def rwkv(K, M, y):
    nc = K.nc
    with ExitStack() as st:
        sb = lambda n, shape: st.enter_context(nc.sbuf_tensor(n, shape, F32))
        R = Bag()
        with ExitStack() as inner:
            isb = lambda n, shape: inner.enter_context(nc.sbuf_tensor(n, shape, F32))
            R.wl, R.oka, R.eP, R.rt = isb("wl", [P, 512]), isb("oka", [P, 1]), isb("eP", [P, T]), isb("rt", [P, T])
            R.bd = isb("bd", [P, 6, NCH, P])
            R.M = y[:, 0:2, :].rearrange("p a (c j) -> p (a c) j", j=P)
            R.Z = y[:, 2:4, :].rearrange("p a (c j) -> p (a c) j", j=P)
            R.Q, R.Y = K.h[:, 0, :], K.h[:, 1, :]
            for p in range(4):
                rwkv_prep_stage(K, M, R, p)
                rwkv_chunk_stage(K, R, p, y[:, 4 + p, :])
        rwkv_finish_stage(K, M, y)


PAD = 16


def ab_in_stage(K, B, norm):
    nc, io = K.nc, K.io
    tiles = []
    for n in range(12):
        dst = B.u[:, n, PAD:] if n < 4 else (B.q if n < 8 else B.k)[:, n % 4, :]
        tiles.append(("ab_in", n // 2, n % 2, WC, feature_pairs((n % 2) * P), (P, T),
                      copier(nc, dst, HD ** -0.5 if n // 4 == 1 else None), SLOT))
    for j in range(2):
        for b in range(TB):
            tiles.append(("ab_v", j, b, WC, token_pairs(b), (P, WC), copier(nc, B.v[:, b, j * WC:(j + 1) * WC]), SLOT))
    wf = B.wf
    box = {}

    def sems(st):
        box["w"], box["pe"] = st.sems("wf", "f")

    def sync(sp):
        sp.dma_start(wf[:, :, :], io["ab_w_in_2"][0].rearrange("(k p) n -> p k n", p=P)[:, :, AB_F:AB_F + 8]).then_inc(box["w"], 16)

    def tensor(pe):
        pe.wait_ge(box["w"], 16)
        product(pe, K.bank[7][0:8, :], [(wf[:, k, :], K.h[:, k, :]) for k in range(KD)]).then_inc(box["pe"], 1)

    def vector(dve):
        dve.wait_ge(box["pe"], 1)
        nc.vector.tensor_scalar(B.z[:, :], K.bank[7][0:8, :], K.p("ab_b_forget_2")[0:8, :], None, ALU.add)

    linear_stage(K, "abin", tiles, banks=7, extra={"sems": sems, "sync": sync, "tensor": tensor, "vector": vector}, norm=norm)


def fox_prep_stage(K, B, y):
    nc, io = K.nc, K.io
    with stage(K, "foxprep") as st:
        e, l, one = st.sb("e", [8, T]), st.sb("l", [8, T]), st.sb("one", [8, T])
        inv = st.sb("inv", [P, 4, T])
        wp = st.sb("wp", [P, 4, P])
        acc = st.sb("acc", [P, 2, T + PAD])
        dif = st.sb("dif", [P, 4, T])
        s_w, s_z, s_exp, s_e1, s_ln, s_F, s_pe, s_ev, s_dif, s_pool, s_pp = st.sems(
            "w", "z", "exp", "e1", "ln", "F", "turned", "out", "dif", "pool", "pooled")
        with nc.Block() as block:
            @block.sync
            def _(sp):
                for g in range(4):
                    sp.dma_start(inv[:, g, :], io["window"][g].partition_broadcast(P)).then_inc(s_w, 16)
                sp.dma_start(wp[:, :, :], io["pool_w_2"][0].rearrange("g k n -> k g n")).then_inc(s_w, 16)

            @block.gpsimd
            def _(pool):
                nc.gpsimd.memset(B.u[:, :, 0:PAD], 0.0)
                nc.gpsimd.memset(acc[:, :, 0:PAD], 0.0)
                pool.drain()
                pool.wait_ge(s_w, 80)
                for g in range(4):
                    cur = B.u[:, g, :]
                    for n in range(g + 1):
                        d = 1 << n
                        nc.gpsimd.tensor_tensor(acc[:, n % 2, PAD:], cur[:, PAD:], cur[:, PAD - d:T + PAD - d], ALU.add)
                        pool.drain()
                        cur = acc[:, n % 2, :]
                    nc.gpsimd.tensor_tensor(dif[:, g, :], cur[:, PAD:], inv[:, g, :], ALU.mult)
                    pool.drain()
                    nc.gpsimd.tensor_tensor(dif[:, g, :], dif[:, g, :], B.u[:, g, PAD:], ALU.subtract).then_inc(s_pool, 1)

            @block.scalar
            def _(act):
                act.wait_ge(s_z, 1)
                nc.scalar.activation(e[:, :], e[:, :], ACT.Exp).then_inc(s_exp, 1)
                act.wait_ge(s_e1, 1)
                nc.scalar.activation(l[:, :], e[:, :], ACT.Ln).then_inc(s_ln, 1)
                act.wait_ge(s_pe, 1)
                nc.scalar.copy(B.F[:, :], K.bank[0][:, 0:32])
                for h in range(8):
                    act.wait_ge(s_pe, 2 + h)
                    nc.scalar.copy(B.nF[:, h, :], K.bank[1 + h % 2][:, :]).then_inc(s_ev, 1)

            @block.vector
            def _(dve):
                nc.vector.tensor_scalar(e[:, :], B.z[:, :], -1.0, None, ALU.mult)
                nc.vector.memset(one[:, :], 1.0)
                dve.drain()
                nc.vector.tensor_tensor(e[:, :], e[:, :], B.z[:, :], ALU.min).then_inc(s_z, 1)
                dve.wait_ge(s_exp, 1)
                nc.vector.tensor_scalar(e[:, :], e[:, :], 1.0, None, ALU.add).then_inc(s_e1, 1)
                dve.wait_ge(s_ln, 1)
                nc.vector.scalar_tensor_tensor(l[:, :], B.z[:, :], 0.0, l[:, :], ALU.min, ALU.subtract)
                dve.drain()
                nc.vector.tensor_tensor_scan(B.z[:, :], one[:, :], l[:, :], 0.0, ALU.mult, ALU.add)
                dve.drain()
                nc.vector.tensor_scalar(e[:, :], B.z[:, :], -1.0, None, ALU.mult).then_inc(s_F, 1)
                for g in range(4):
                    dve.wait_ge(s_pp, g + 1)
                    nc.vector.tensor_scalar(y[:, g, :], K.bank[4 + g][:, :], K.p("pool_scale_2", g), None, ALU.mult)

            @block.tensor
            def _(pe):
                pe.wait_ge(s_F, 1)
                for b in range(TB):
                    last = pe.transpose(K.bank[0][:, 8 * b:8 * b + 8], B.z[:, b * P:(b + 1) * P], K.k("ident")[0:8, 0:8])
                last.then_inc(s_pe, 1)
                for h in range(8):
                    if h >= 2:
                        pe.wait_ge(s_ev, h - 1)
                    pe.matmul(K.bank[1 + h % 2][:, :], K.k("ident")[0:8, h:h + 1].broadcast_to([8, P]), e[:, :],
                              start=True, stop=True).then_inc(s_pe, 1)
                for g in range(4):
                    pe.wait_ge(s_pool, g + 1)
                    pe.matmul(K.bank[4 + g][:, :], wp[:, g, :], dif[:, g, :], start=True, stop=True).then_inc(s_pp, 1)


def mixer2(K, norm):
    nc = K.nc
    with ExitStack() as st:
        sb = lambda n, shape: st.enter_context(nc.sbuf_tensor(n, shape, F32))
        B = Bag()
        B.q, B.k, B.v, B.F = sb("fq", [P, 4, T]), sb("fk", [P, 4, T]), sb("fv", [P, TB, 512]), sb("fF", [P, 32])
        B.nF = sb("fnF", [P, 8, T])
        y = K.h
        with ExitStack() as inner:
            isb = lambda n, shape: inner.enter_context(nc.sbuf_tensor(n, shape, F32))
            B.u, B.wf, B.z = isb("fu", [P, 4, T + PAD]), isb("fwf", [P, KD, 8]), isb("fz", [8, T])
            ab_in_stage(K, B, norm)
            fox_prep_stage(K, B, y)

        def prep(pool, out, h, i):
            w = (i + 1) * P
            nc.gpsimd.tensor_scalar(out, B.nF[:, h, 0:w], B.F[:, 8 * i + h:8 * i + h + 1], None, ALU.add)
            pool.drain()
            return nc.gpsimd.tensor_tensor(out[:, w - P:w], out[:, w - P:w], K.k("causal")[:, T - P:T], ALU.add)

        r = lambda h: slice((h % 2) * 64, (h % 2) * 64 + 64)
        attention_stage(K, "fox", 8, HD, lambda h, i: B.q[r(h), h // 2, i * P:(i + 1) * P], lambda h, w: B.k[r(h), h // 2, 0:w],
                        lambda h, s: B.v[:, s, h * 64:(h + 1) * 64], 64, lambda h, i: y[r(h), 4 + h // 2, i * P:(i + 1) * P], prep=prep)
        out_stage(K, "ab_out", lambda k: y[:, k, :], True)


ROPE = 32
QK = 96
MH = 16
TWO_PI_HI = 6.28125
TWO_PI_MID = float(np.float32(int((2 * math.pi - 6.28125) * 2 ** 20) / 2 ** 20))
TWO_PI_LO = 2 * math.pi - TWO_PI_HI - TWO_PI_MID
ROUND = 12582912.0


def mla_in_stage(K, B, norm):
    nc, io = K.nc, K.io
    w_in = io["mla_w_in_2"][0].rearrange("(k p) n -> p k n", p=P)
    tiles = [("mla_q", 0, m, WC, feature_pairs(m * P), (P, T), copier(nc, B.cq[:, m, :]), SLOT) for m in range(2)]
    tiles.append(("mla_kv", 0, 0, P, feature_pairs(0), (P, T), copier(nc, B.ckv[:, :]), KD * P))
    box = {}
    R = slice(64, 96)

    def sems(st):
        box["w"], box["pe"], box["pos"], box["ang"], box["sin"], box["rope"] = st.sems("wr", "rope", "pos", "angle", "sin", "rotated")
        box["wr"] = st.sb("wr", [P, KD, 2 * ROPE])
        box["pos_i"] = st.sb("pos_i", [P, T], I32)
        box["ang_t"], box["turn"] = st.sb("ang", [P, T]), st.sb("turn", [P, T])

    def sync(sp):
        for a, b in ((0, 384), (16, 400), (32, 400), (48, 384)):
            sp.dma_start(box["wr"][:, :, a:a + 16], w_in[:, :, b:b + 16]).then_inc(box["w"], 16)
        sp.dma_start(box["pos_i"][:, :], io["positions_2"][0].partition_broadcast(P)).then_inc(box["pos"], 16)

    def tensor(pe):
        pe.wait_ge(box["w"], 64)
        for n in range(2):
            product(pe, K.bank[5 + n][R, :], [(box["wr"][:, k, n * ROPE:(n + 1) * ROPE], K.h[:, k, :]) for k in range(KD)]
                    ).then_inc(box["pe"], 1)

    def before(dve):
        ang, turn = box["ang_t"], box["turn"]
        dve.wait_ge(box["pos"], 16)
        nc.vector.tensor_copy(ang[:, :], box["pos_i"][:, :])
        dve.drain()
        nc.vector.tensor_scalar(ang[:, :], ang[:, :], K.k("freq")[:, 0:1], None, ALU.mult)
        dve.drain()
        nc.vector.tensor_scalar(turn[:, :], ang[:, :], 1.0 / (2 * math.pi), ROUND, ALU.mult, ALU.add)
        dve.drain()
        nc.vector.tensor_scalar(turn[:, :], turn[:, :], ROUND, None, ALU.subtract)
        dve.drain()
        for part in (TWO_PI_HI, TWO_PI_MID, TWO_PI_LO):
            nc.vector.scalar_tensor_tensor(ang[:, :], turn[:, :], -part, ang[:, :], ALU.mult, ALU.add)
            dve.drain()
        nc.vector.tensor_scalar(ang[:, :], ang[:, :], 3.1415925, -3.1415925, ALU.min, ALU.max).then_inc(box["ang"], 1)

    def scalar(act):
        act.wait_ge(box["ang"], 1)
        nc.scalar.activation(B.sin[:, :], box["ang_t"][:, :], ACT.Sin)
        nc.scalar.activation(B.cos[:, :], box["ang_t"][:, :], ACT.Sin, scale=0.5).then_inc(box["sin"], 1)

    def vector(dve):
        dve.wait_ge(box["sin"], 1)
        nc.vector.tensor_tensor(B.cos[:, :], B.cos[:, :], B.cos[:, :], ALU.mult)
        nc.vector.tensor_scalar(B.sin[:, :], B.sin[:, :], K.k("freq")[:, 1:2], None, ALU.mult)
        dve.drain()
        nc.vector.tensor_scalar(B.cos[:, :], B.cos[:, :], -2.0, 1.0, ALU.mult, ALU.add)
        dve.drain()
        dve.wait_ge(box["pe"], 2)
        nc.vector.tensor_tensor(B.kr[R, :], K.bank[5][R, :], B.cos[R, :], ALU.mult)
        nc.vector.tensor_tensor(box["turn"][R, :], K.bank[6][R, :], B.sin[R, :], ALU.mult)
        dve.drain()
        nc.vector.tensor_tensor(B.kr[R, :], B.kr[R, :], box["turn"][R, :], ALU.add)

    linear_stage(K, "mlain", tiles, banks=4, scalar=lambda t: True,
                 extra={"sems": sems, "sync": sync, "tensor": tensor, "scalar": scalar, "before": before, "vector": vector}, norm=norm)


def mla_prep_stage(K, B):
    nc, io = K.nc, K.io
    R = slice(64, 96)
    swap = K.h
    with stage(K, "mlaprep") as st:
        wq, wkv = B.wq, B.wkv
        s_w, s_pe, s_v, s_s, s_swap, s_q, s_rot, s_tmp = st.sems("w", "pe", "vector_out", "scalar_out", "swapped", "q", "rotated", "tmp")
        steps = []
        for h in range(MH):
            steps.append((QK, T, [(wq[:, k, h * QK:(h + 1) * QK], B.cq[:, k, :]) for k in range(2)], B.Q[0:QK, h, :], QK ** -0.5))
        for h in range(MH):
            steps.append((64, T, [(wkv[:, h * P:h * P + 64], B.ckv[:, :])], B.K[0:64, h, :], None))
        wv = wkv[:, :].rearrange("p (h d) -> p h d", d=P)[:, :, 64:]
        for b in range(TB):
            for half in range(2):
                steps.append((P, T, [(B.ckv[:, b * P:(b + 1) * P], wv[:, 8 * half:8 * half + 8, :])],
                              B.V[:, b, half * 512:(half + 1) * 512], None))
        with nc.Block() as block:
            @block.sync
            def _(sp):
                sp.dma_start(wq[:, :, :], io["mla_w_q_b_2"][0].rearrange("(k p) n -> p k n", p=P)).then_inc(s_w, 16)
                sp.dma_start(wkv[:, :], io["mla_w_kv_b_2"][0]).then_inc(s_w, 16)
                for g in range(4):
                    sp.wait_ge(s_v, 2 * g + 2)
                    sp.wait_ge(s_s, 2 * g + 2)
                    if g >= 2:
                        sp.wait_ge(s_rot, g - 1)
                    o = 4 * (g % 2)
                    sp.dma_start(swap[64:80, o:o + 4, :], B.Q[80:96, 4 * g:4 * g + 4, :]).then_inc(s_swap, 16)
                    sp.dma_start(swap[80:96, o:o + 4, :], B.Q[64:80, 4 * g:4 * g + 4, :]).then_inc(s_swap, 16)
                    sp.wait_ge(s_swap, 32 * g + 32)
                    sp.sem_inc(s_q, 1)

            @block.tensor
            def _(pe):
                pe.wait_ge(s_w, 32)
                for t, (rows, _, pairs, _, _) in enumerate(steps):
                    if t >= 8:
                        pe.wait_ge(s_s if t % 2 else s_v, (t - 8) // 2 + 1)
                    product(pe, K.bank[t % 8][0:rows, :], pairs).then_inc(s_pe, 1)

            def evacuate(e, side):
                for t, (rows, _, _, dst, scale) in enumerate(steps):
                    if t % 2 == side:
                        e.wait_ge(s_pe, t + 1)
                        copier(nc, dst, scale)(K.bank[t % 8][0:rows, :], "scalar" if side else "vector").then_inc(s_s if side else s_v, 1)

            @block.scalar
            def _(act):
                evacuate(act, 1)

            @block.vector
            def _(dve):
                evacuate(dve, 0)

            @block.gpsimd
            def _(pool):
                nc.gpsimd.tensor_copy(B.K[R, :, :], B.kr[R, :].unsqueeze(1).broadcast_to([ROPE, MH, T]))
                wide = lambda ap: ap[R, :].unsqueeze(1).broadcast_to([ROPE, 4, T])
                for g in range(4):
                    pool.wait_ge(s_q, g + 1)
                    o = 4 * (g % 2)
                    q, w = B.Q[R, 4 * g:4 * g + 4, :], swap[R, o:o + 4, :]
                    nc.gpsimd.tensor_tensor(q, q, wide(B.cos), ALU.mult)
                    nc.gpsimd.tensor_tensor(w, w, wide(B.sin), ALU.mult)
                    pool.drain()
                    nc.gpsimd.tensor_tensor(q, q, w, ALU.add).then_inc(s_rot, 1)


def mixer3(K, norm):
    nc = K.nc
    with ExitStack() as st:
        sb = lambda n, shape: st.enter_context(nc.sbuf_tensor(n, shape, F32))
        B = Bag()
        B.cq, B.ckv, B.sin, B.cos, B.kr = sb("mcq", [P, 2, T]), sb("mckv", [P, T]), sb("msin", [P, T]), sb("mcos", [P, T]), sb("mkr", [P, T])
        mla_in_stage(K, B, norm)
        with ExitStack() as inner:
            isb = lambda n, shape: inner.enter_context(nc.sbuf_tensor(n, shape, F32))
            B.V = isb("mV", [P, TB, 1024])
            B.Q, B.K = isb("mQ", [QK, MH, T]), isb("mK", [QK, MH, T])
            mla_body(K, B)
        out_stage(K, "mla_out", lambda k: K.h[:, k, :], True)


def mla_body(K, B):
    nc = K.nc
    with ExitStack() as st:
        with ExitStack() as inner:
            isb = lambda n, shape: inner.enter_context(nc.sbuf_tensor(n, shape, F32))
            small_norm(K, "norm_mq", [B.cq[:, 0, :], B.cq[:, 1, :]], [K.p("mla_q_norm_2", 0), K.p("mla_q_norm_2", 1)], 256)
            small_norm(K, "norm_mkv", [B.ckv[:, :]], [K.p("mla_kv_norm_2")], 128)
            B.wq, B.wkv = isb("mwq", [P, 2, MH * QK]), isb("mwkv", [P, MH * P])
            mla_prep_stage(K, B)
        y = K.h
        r = lambda h: slice((h % 2) * 64, (h % 2) * 64 + 64)
        attention_stage(K, "mla", MH, QK, lambda h, i: B.Q[:, h, i * P:(i + 1) * P], lambda h, w: B.K[:, h, 0:w],
                        lambda h, s: B.V[:, s, h * 64:(h + 1) * 64], 64, lambda h, i: y[r(h), h // 2, i * P:(i + 1) * P],
                        bias=lambda h, i: K.k("chunked")[:, 384 - i * P:384 - i * P + (i + 1) * P])


def build(nc, io):
    plan = Plan()

    def cols(w, a, width):
        v = w.rearrange("(k p) n -> p k n", p=P)
        return lambda c: v[:, :, a + width * c:a + width * (c + 1)]

    def ffn(name, *weights):
        parts = [w.rearrange("(k p) n -> p k n", p=P) for w in weights]
        plan.add(name, 34, lambda c: ffn_chunk(*parts, c))
        if name in plan.segments:
            plan.segments[name]["parts"] = parts

    w_in = io["w_in"][0]
    plan.add("mod1", 8, cols(io["ada_w"][0], 0, WC), marks=1, split=False)
    plan.add("in_q", 1, cols(w_in, 0, WC))
    plan.add("in_kv", 1, cols(w_in, O_KV, P), marks=1)
    plan.add("in_rkv", 6, cols(w_in, O_R, WC))
    plan.add("in_lora", 1, cols(w_in, O_WA, WC))
    plan.add("in_lora2", 1, cols(w_in, O_WA + WC, 32), marks=1)
    plan.add("mod2", 16, cols(io["ada_w"][0], 2048, WC), marks=1, split=False)
    plan.add("out1", 4, cols(io["w_out"][0], 0, WC))
    ffn("ffn1", io["w_ffn_gate"][0], io["w_ffn_up"][0], io["w_ffn_down"][0])

    def ffn2(name, l, i):
        ffn(name, io["ffn_w_gate_2"][l, i], io["ffn_w_up_2"][l, i], io["ffn_w_down_2"][l, i])

    ffn2("ffn2", 0, 0)
    plan.add("ab_in", 6, cols(io["ab_w_in_2"][0], 0, WC))
    plan.add("ab_v", 2, cols(io["ab_w_in_2"][0], 1536, WC), marks=4)
    plan.add("ab_out", 4, cols(io["ab_w_out_2"][0], 0, WC))
    ffn2("ffn3", 0, 1)
    ffn2("ffn4", 1, 0)
    plan.add("mla_q", 1, cols(io["mla_w_in_2"][0], 0, WC))
    plan.add("mla_kv", 1, cols(io["mla_w_in_2"][0], 256, P), marks=1)
    plan.add("mla_out", 4, cols(io["mla_w_out_2"][0], 0, WC))
    ffn2("ffn5", 1, 1)

    with ExitStack() as ctx:
        K = Core(nc, ctx, io, plan)
        par, coef, mod = K.p, K.coef, K.mod
        gain = lambda name, at=0: (lambda i: par(name, at + i), None)
        steps = [
            ("mod1", lambda: mod_stage(K)),
            ("mix1", lambda: mixer1(K, (lambda i: coef[:, 8 + i:9 + i], lambda i: mod[:, i:i + 1]))),
            ("x1", lambda: residual_norm(K, "post1", lambda i: coef[:, 16 + i:17 + i])),
            ("f1", lambda: ffn_stage(K, "ffn1", False, (lambda i: coef[:, 24 + i:25 + i], lambda i: mod[:, 24 + i:25 + i]))),
            ("x2", lambda: residual_norm(K, "post2", lambda i: coef[:, 32 + i:33 + i])),
            ("x3", lambda: ffn_stage(K, "ffn2", True, gain("norm_ffn_2"))),
            ("x4", lambda: mixer2(K, gain("norm_mix_2"))),
            ("x5", lambda: ffn_stage(K, "ffn3", True, gain("norm_ffn_2", 8))),
            ("x6", lambda: ffn_stage(K, "ffn4", True, gain("norm_ffn_2", 16))),
            ("x7", lambda: mixer3(K, gain("norm_mix_2", 8))),
            ("x8", lambda: ffn_stage(K, "ffn5", True, gain("norm_ffn_2", 24))),
            ("h9", lambda: final_norm(K)),
            ("out", lambda: finish_stage(K)),
        ]
        start_stage(K, None)
        for _, step in steps:
            step()


def const_table():
    t = np.zeros((P, CONST_W), np.float32)

    def put(name, v):
        a, b = CONST[name]
        t[:, a:b] = v

    i, j = np.arange(P)[:, None], np.arange(P)[None, :]
    same = (i // C) == (j // C)
    ii, jj = i % C, j % C
    put("ident", i == j)
    put("flip", i + j == P - 1)
    put("ones", 1.0)
    put("heads", same)
    for s in LEVELS:
        low = same & (ii // (2 * s) == jj // (2 * s)) & (ii // s > jj // s)
        put("first" if s == 1 else f"low{s}", low)
        if s == 1:
            put("first_t", low.T)
    put("strict", same & (ii < jj))
    put("upto", np.arange(P)[:, None] % C <= np.arange(C)[None, :])
    x = np.arange(T)[None, :]
    put("causal", np.where(x - 384 > i, -BIG, 0.0))
    put("chunked", np.where((x - 384) // C > i // C, -BIG, 0.0))
    put("reset", x % C != 0)
    put("eps", np.array([EPS, GN_EPS, 0.0, 0.0], np.float32)[None, :])
    inv = (np.float32(10000.0) ** (-np.arange(0, 32, 2, dtype=np.float32) / np.float32(32))).astype(np.float32)
    put("freq", np.stack([np.tile(inv, 8), np.where(np.arange(P) % 32 < 16, -1.0, 1.0)], 1))
    return t


def bucket_table():
    d = np.arange(T)
    nf = np.maximum(d, 1).astype(np.float32)
    large = 16 + (np.log(nf / np.float32(16)) / np.float32(math.log(8.0)) * np.float32(16)).astype(np.int32)
    b = np.where(d < 16, d, np.minimum(large, 31))
    t = (b[None, ::-1] == np.arange(32)[:, None]).astype(np.float32)
    return np.concatenate([t, np.zeros((32, P), np.float32)], 1)


def window_table():
    n = np.arange(T) + 1
    return np.stack([(np.float32(1.0) / np.minimum(n, w).astype(np.float32)) for w in (2, 4, 8, 16)]).astype(np.float32)


TABLES = {"const": const_table, "bucket": bucket_table, "window": window_table}
INS = ["x", "c", "rel_bias", "ada_w", "ada_b", "mix_pre_norm", "mix_post_norm", "ffn_pre_norm", "ffn_post_norm",
       "w_in", "q_norm", "w_uq", "w_idx_q", "kv_norm", "idx_k_norm", "w_uk", "w_uv", "mu_shift", "w0", "w_decay_up",
       "a0", "w_aaa_up", "w_gate_up", "k_k", "k_a", "r_k", "ln_x_gain", "ln_x_bias", "w_out", "w_ffn_gate",
       "w_ffn_up", "w_ffn_down", "positions_2", "norm_ffn_2", "norm_mix_2", "norm_final_2", "ffn_w_gate_2",
       "ffn_w_up_2", "ffn_w_down_2", "ab_w_in_2", "ab_b_forget_2", "pool_w_2", "pool_scale_2", "ab_w_out_2",
       "mla_w_in_2", "mla_q_norm_2", "mla_kv_norm_2", "mla_w_q_b_2", "mla_w_kv_b_2", "mla_w_out_2"]


def kernel(**inputs):
    import concourse.bacc as bacc
    from concourse.bass_utils import run_bass_kernel_spmd

    nc = bacc.Bacc("TRN2", target_bir_lowering=False, num_devices=1)
    arrays, io = {}, {}
    for name in INS + list(TABLES):
        a = np.ascontiguousarray(inputs[name] if name in inputs else TABLES[name]())
        arrays[f"in_{name}"] = a
        io[name] = nc.dram_tensor(f"in_{name}", a.shape, mybir.dt.from_np(a.dtype), kind="ExternalInput").ap()
    io["out"] = nc.dram_tensor("out", (1, T, D), F32, kind="ExternalOutput").ap()
    build(nc, io)
    r = run_bass_kernel_spmd(nc, [arrays], core_ids=[0])
    return r.results[0]["out"]
```

```python
import math
from contextlib import ExitStack

import numpy as np

import concourse.bass as bass
from concourse import mybir

F32 = mybir.dt.float32
F32R = mybir.dt.float32r
I32 = mybir.dt.int32
ALU = mybir.AluOpType
ACT = mybir.ActivationFunctionType
AX = mybir.AxisListType

P = 128
T = 512
D = 1024
KD = D // P
F = 2816
KF = F // P
HD = 64
TB = T // P
C = 64
NCH = T // C
EPS = 1e-6
GN_EPS = 64e-5
BIG = 1e30
CAUSAL_FILL = -3.0e38
TAKEN = -3.3e38
TOPK = min(256, T // 4)
RING = 4
WC = 256
SLOT = KD * WC

LEVELS = (1, 2, 4, 8, 16, 32)
CONST = {}
_at = 0
for _name, _n in (("ident", P), ("flip", P), ("ones", P), ("heads", P), ("first", P), ("first_t", P)) + tuple(
        (f"low{s}", P) for s in LEVELS[1:]) + (("strict", P), ("upto", C), ("causal", T),
                                           ("chunked", T), ("reset", T), ("eps", 4), ("freq", 2)):
    CONST[_name] = (_at, _at + _n)
    _at += _n
CONST_W = _at

ROWS_A = (("ada_b", 48), ("mix_pre_norm", 8), ("mix_post_norm", 8), ("ffn_pre_norm", 8), ("ffn_post_norm", 8),
          ("c", 8), ("q_norm", 2), ("kv_norm", 1), ("w0", 4), ("a0", 4), ("k_k", 4), ("k_a", 4), ("r_k", 4),
          ("ln_x_gain", 4), ("ln_x_bias", 4))
ROWS_B = (("norm_ffn_2", 32), ("norm_mix_2", 16), ("norm_final_2", 8), ("mla_q_norm_2", 2), ("mla_kv_norm_2", 1),
          ("pool_scale_2", 4), ("mu_rkv", 12), ("mu_wa", 1), ("mu_g", 1), ("mu_g2", 1), ("idx_k_norm", 1),
          ("ab_b_forget_2", 1))


def columns(rows, base):
    at, out = base, {}
    for name, n in rows:
        out[name] = at
        at += n
    return out, at


COL, _end = columns(ROWS_A, 0)
_colb, PAR_W = columns(ROWS_B, P)
COL.update(_colb)
N_A, N_B = sum(n for _, n in ROWS_A), sum(n for _, n in ROWS_B)

O_KV, O_IK, O_IW, O_R = 256, 384, 448, 456
O_WA = O_R + 3 * 512
O_G = O_WA + 128
IN_COLS = O_G + 160
AB_F = 2048
NEG_SQRT_E = -math.exp(-0.5)


class Plan:

    def __init__(self):
        self.segments, self.order, self.n, self.mark, self.splits = {}, [], 0, 0, 0

    def add(self, name, count, src, marks=2, split=True):
        s = {"name": name, "n0": self.n, "count": count, "src": src, "marks": marks, "mark0": self.mark,
             "split": split, "split0": self.splits}
        self.segments[name] = s
        self.order.append(s)
        self.n += count
        self.mark += marks * count
        self.splits += count * split

    def at(self, n):
        return [x for x in self.order if x["n0"] <= n][-1]

    def used(self, n):
        s = self.at(n)
        return s["mark0"] + s["marks"] * (n - s["n0"] + 1)

    def tile(self, name, c, k):
        s = self.segments[name]
        return s["mark0"] + k + 1 + s["marks"] * c

    def end(self, name):
        s = self.segments[name]
        return s["n0"] + s["count"]


class Core:

    def __init__(self, nc, ctx, io, plan):
        self.nc, self.ctx, self.io, self.plan = nc, ctx, io, plan
        sb = lambda name, shape, dt=F32: ctx.enter_context(nc.sbuf_tensor(name, shape, dt))
        sem = lambda name: ctx.enter_context(nc.semaphore(name))
        self.const = sb("const", [P, CONST_W])
        self.par = sb("par", [P, PAR_W])
        self.mod = sb("mod", [P, 48])
        self.coef = sb("coef", [P, 64])
        self.x = sb("x", [P, KD, T])
        self.h = sb("h", [P, KD, T])
        self.warm = sb("warm", [P, 1])
        self.ring = sb("ring", [P, RING, SLOT])
        self.bank = [ctx.enter_context(nc.psum_tensor(f"bank{i}", [P, 512], F32)) for i in range(8)]
        self.loaded = [sem(f"chunk_loaded{i}") for i in range(RING)]
        self.tiles_done, self.high_done, self.low_done = sem("tiles_done"), sem("high_done"), sem("low_done")
        self.dsa_bias_in, self.dsa_weights_in, self.mla_weights_in = sem("dsa_bias_in"), sem("dsa_weights_in"), sem("mla_weights_in")
        self.issued = 0
        self.sum_bank = None

    def k(self, name):
        a, b = CONST[name]
        return self.const[:, a:b]

    def p(self, name, i=0):
        return self.par[:, COL[name] + i:COL[name] + i + 1]

    def stream(self, sp, upto):
        for n in range(self.issued, min(upto, self.plan.n)):
            if n >= RING:
                o = self.plan.at(n - RING)
                if o["split"]:
                    sp.wait_ge(self.low_done, o["split0"] + n - RING - o["n0"] + 1)
                else:
                    sp.wait_ge(self.tiles_done, self.plan.used(n - RING))
            s = self.plan.at(n)
            self.load(sp, n, s["src"](n - s["n0"]))
        self.issued = max(self.issued, min(upto, self.plan.n))

    def load(self, sp, n, src):
        a, b = src.shape[1], src.shape[2]
        dst = self.ring[:, n % RING, 0:a * b].rearrange("p (a b) -> p a b", a=a)
        sp.dma_start(dst, src).then_inc(self.loaded[n % RING], 16)


class SumOfSquares:

    def __init__(self, K, st, tag, src, dst, bank):
        self.K, self.src, self.dst, self.bank = K, src, dst, bank
        self.s_sq, self.s_add, self.s_sum = st.sems(f"{tag}_squared", f"{tag}_added", f"{tag}_summed")

    def square(self, k):
        self.K.nc.scalar.activation(self.dst[k], self.src[k], ACT.Square).then_inc(self.s_sq, 1)

    def add(self, e, ops):
        d = self.dst
        for k in range(1, len(d) - 1):
            e.wait_ge(self.s_sq, k + 1)
            last = ops.tensor_tensor(d[0], d[0], d[k], ALU.add)
            if k < len(d) - 2:
                e.drain()
        if len(d) > 2:
            last.then_inc(self.s_add, 1)

    def columns(self, pe):
        K, d = self.K, self.dst
        if len(d) > 2:
            pe.wait_ge(self.s_add, 1)
        pe.wait_ge(self.s_sq, len(d))
        for b in range(TB):
            last = product(pe, K.bank[self.bank][:, b:b + 1],
                           [(x[:, b * P:(b + 1) * P], K.k("ones")[:, 0:1]) for x in ([d[0], d[-1]] if len(d) > 1 else [d[0]])])
        last.then_inc(self.s_sum, 1)

    def preload(self):
        K = self.K
        K.nc.scalar.activation(K.warm[:, :], K.k("eps")[:, 0:1], ACT.Sqrt)


class Rstd:

    def __init__(self, K, st, tag, bank, out, width, sums=None):
        self.K, self.bank, self.out, self.width, self.sums = K, bank, out, width, sums
        self.col = st.sb(f"{tag}_root", [P, TB])
        self.value = K.bank[out][:, :]
        self.s_root, self.s_inv, self.s_out = st.sems(f"{tag}_root", f"{tag}_inverse", f"{tag}_spread")

    def root(self, act):
        K = self.K
        if self.sums:
            act.wait_ge(self.sums.s_sum, 1)
        K.nc.scalar.activation(self.col[:, :], K.bank[self.bank][:, 0:TB], ACT.Sqrt, bias=K.k("eps")[:, 0:1],
                               scale=1.0 / self.width).then_inc(self.s_root, 1)

    def invert(self, dve):
        dve.wait_ge(self.s_root, 1)
        self.K.nc.vector.reciprocal(self.col[:, :], self.col[:, :]).then_inc(self.s_inv, 1)

    def spread(self, pe):
        K = self.K
        pe.wait_ge(self.s_inv, 1)
        for b in range(TB):
            last = pe.matmul(K.bank[self.out][:, b * P:(b + 1) * P], self.col[:, b:b + 1].broadcast_to([P, P]), K.k("ident"),
                             start=True, stop=True)
        last.then_inc(self.s_out, 1)


def tiles_of(x):
    return [x[:, k, :] for k in range(KD)]


class Split:
    PERIOD = 12

    def __init__(self, K, st, norm=None):
        self.K, self.nc, self.norm = K, K.nc, norm
        if norm:
            self.s_h, = st.sems("normed")
            bank, self.own = K.sum_bank, None
            if bank is None:
                bank = 7
                self.own = SumOfSquares(K, st, "own", tiles_of(K.x), tiles_of(K.h), bank)
            self.rstd = Rstd(K, st, "norm", bank, 7, D, self.own)
            K.sum_bank = None
        self.hh, self.hl = st.sb("feat_hi", [P, KD, T], F32R), st.sb("feat_lo", [P, KD, T], F32R)
        self.wh, self.wl = st.sb("wt_hi", [P, 2, SLOT], F32R), st.sb("wt_lo", [P, 2, SLOT], F32R)
        self.s_hh, self.s_hl, self.s_hl2 = st.sems("feat_high", "feat_low_even", "feat_low_odd")

    def high(self, act, name, r, t=0, words=SLOT):
        K, s = self.K, self.K.plan.segments[name]
        n = s["n0"] + r
        act.wait_ge(K.loaded[n % RING], 16 * (n // RING + 1) + 16 * (self.PERIOD // RING) * t)
        if not isinstance(t, int):
            act.wait_ge(K.tiles_done, s["mark0"] + s["marks"] * (r - 1) + s["marks"] * self.PERIOD * t)
        elif n + self.PERIOD * t >= 2:
            act.wait_ge(K.tiles_done, K.plan.used(n + self.PERIOD * t - 2))
        self.nc.scalar.copy(self.wh[:, n % 2, 0:words], K.ring[:, n % RING, 0:words]).then_inc(K.high_done, 1)

    def low(self, dve, name, r, t=0, words=SLOT):
        K, s = self.K, self.K.plan.segments[name]
        n = s["n0"] + r
        dve.wait_ge(K.high_done, s["split0"] + r + 1 + self.PERIOD * t)
        self.nc.vector.tensor_tensor(self.wl[:, n % 2, 0:words], K.ring[:, n % RING, 0:words],
                                     self.wh[:, n % 2, 0:words].bitcast(F32), ALU.subtract).then_inc(K.low_done, 1)

    def chunk(self, pe, name, r, width, t=0):
        K, s = self.K, self.K.plan.segments[name]
        n = s["n0"] + r
        pe.wait_ge(K.low_done, s["split0"] + r + 1 + self.PERIOD * t)
        k = SLOT // width
        return tuple(w[:, n % 2, 0:k * width].rearrange("p (k n) -> p k n", n=width) for w in (self.wh, self.wl))

    def squares(self, act):
        if self.norm:
            if self.own:
                for k in range(KD):
                    self.own.square(k)
            self.rstd.root(act)

    def sums(self, pe):
        if self.norm:
            if self.own:
                self.own.columns(pe)
            self.rstd.spread(pe)

    def invert(self, dve):
        if self.norm:
            if self.own:
                self.own.add(dve, self.nc.vector)
            self.rstd.invert(dve)

    def features_scalar(self, act):
        K = self.K
        if self.norm:
            for k in range(KD):
                act.wait_ge(self.s_h, k + 1)
                self.nc.scalar.copy(self.hh[:, k, :], K.h[:, k, :]).then_inc(self.s_hh, 1)

    def normed_vector(self, dve):
        K, v = self.K, self.nc.vector
        gain, shift = self.norm
        dve.wait_ge(self.rstd.s_out, 1)
        for k in range(KD):
            ins = v.scalar_tensor_tensor(K.h[:, k, :], K.x[:, k, :], gain(k), self.rstd.value, ALU.mult, ALU.mult)
            if shift:
                dve.drain()
                ins = v.tensor_scalar(K.h[:, k, :], K.h[:, k, :], shift(k), None, ALU.add)
            ins.then_inc(self.s_h, 1)
            if k % 2 == 1:
                dve.wait_ge(self.s_hh, k)
                v.tensor_tensor(self.hl[:, k - 1, :], K.h[:, k - 1, :], self.hh[:, k - 1, :].bitcast(F32), ALU.subtract).then_inc(self.s_hl, 1)
            if k == 1:
                self.first_low(dve)

    def features_vector(self, dve, src, first_low):
        self.first_low = first_low
        if self.norm:
            return self.normed_vector(dve)
        for k in range(KD):
            self.nc.vector.tensor_copy(self.hh[:, k, :], src(k)).then_inc(self.s_hh, 1)
            if k % 2 == 0:
                dve.drain()
                self.nc.vector.tensor_tensor(self.hl[:, k, :], src(k), self.hh[:, k, :].bitcast(F32), ALU.subtract).then_inc(self.s_hl, 1)
            if k == 1:
                first_low(dve)

    def features_pool(self, pool, src):
        for k in range(1, KD, 2):
            pool.wait_ge(self.s_hh, k + 1)
            self.nc.gpsimd.tensor_tensor(self.hl[:, k, :], src(k), self.hh[:, k, :].bitcast(F32), ALU.subtract).then_inc(self.s_hl2, 1)

    def feature(self, pe, k, wait, cols=slice(0, T)):
        if wait:
            pe.wait_ge(self.s_hl2 if k % 2 else self.s_hl, k // 2 + 1)
        return self.hh[:, k, cols], self.hl[:, k, cols]


def product3(pe, out, pairs, start=True, stop=True):
    last, n = None, 0
    pairs = iter(pairs)
    cur = next(pairs)
    while cur is not None:
        (ah, al), (bh, bl) = cur
        passes = ((ah, bh), (ah, bl), (al, bh))
        for m, (a, b) in enumerate(passes[:2]):
            pe.matmul(out, a, b, start=start and n == 0 and m == 0, stop=False)
        cur, n = next(pairs, None), n + 1
        last = pe.matmul(out, al, bh, start=False, stop=stop and cur is None)
    return last


def product(pe, out, pairs, start=True, stop=True):
    for n, (a, b) in enumerate(pairs):
        last = pe.matmul(out, a, b, start=start and n == 0, stop=stop and n == len(pairs) - 1)
    return last


def stage(K, name):
    st = ExitStack()
    nc = K.nc
    mine = []

    def sem(n):
        mine.append(nc.alloc_semaphore(f"{name}_{n}"))
        return mine[-1]

    def give_back():
        for x in mine:
            nc.gpsimd.sem_clear(x)
            nc.release_semaphore(x)

    st.callback(give_back)
    st.sem = sem
    st.sb = lambda n, shape, dt=F32: st.enter_context(nc.sbuf_tensor(f"{name}_{n}", shape, dt))
    st.sems = lambda *ns: [sem(n) for n in ns]
    return st


def start_stage(K, xin_rows):
    nc, io = K.nc, K.io
    with stage(K, "start") as st:
        rows = st.sb("rows", [P, 2, P])
        xin = st.sb("xin", [P, TB, D])
        s_const, s_x, s_zero, s_turned, s_copied = st.sems("const", "x", "zero", "turned", "copied")
        s_rows, st.n_rows = st.sems("rows_a", "rows_b"), [0, 0]
        def rows_in(e, which, group):
            e.wait_ge(s_zero, 1)
            at = n = 0
            for name, cnt in group:
                for dst, src in param_rows(io, name, cnt, rows, which, at):
                    e.dma_start(dst, src).then_inc(s_rows[which], 16)
                    n += 1
                at += cnt
            st.n_rows[which] = n

        with nc.Block() as block:
            @block.sync
            def _(sp):
                for t in range(TB):
                    sp.dma_start(xin[:, t, :], io["x"][0, t * P:(t + 1) * P, :]).then_inc(s_x, 16)
                rows_in(sp, 1, ROWS_B)
                sp.dma_start(K.const[:, :], io["const"]).then_inc(s_const, 16)
                K.stream(sp, RING)

            @block.scalar
            def _(act):
                rows_in(act, 0, ROWS_A)
                for k in range(1, KD, 2):
                    act.wait_ge(s_turned, 2 + k + 1)
                    nc.scalar.copy(K.x[:, k, :], K.bank[k][:, :])

            @block.vector
            def _(dve):
                nc.vector.memset(rows[:, :, :], 0.0).then_inc(s_zero, 1)
                dve.wait_ge(s_turned, 2)
                nc.vector.tensor_copy(K.par[:, 0:N_A], K.bank[0][:, 0:N_A])
                nc.vector.tensor_copy(K.par[:, P:P + N_B], K.bank[1][:, 0:N_B]).then_inc(s_copied, 1)
                for k in range(0, KD, 2):
                    dve.wait_ge(s_turned, 2 + k + 1)
                    nc.vector.tensor_copy(K.x[:, k, :], K.bank[k][:, :])

            @block.tensor
            def _(pe):
                pe.wait_ge(s_const, 16)
                pe.wait_ge(s_rows[0], 16 * st.n_rows[0])
                pe.transpose(K.bank[0][:, 0:N_A], rows[0:N_A, 0, :], K.k("ident")[0:N_A, 0:N_A]).then_inc(s_turned, 1)
                pe.wait_ge(s_rows[1], 16 * st.n_rows[1])
                pe.transpose(K.bank[1][:, 0:N_B], rows[0:N_B, 1, :], K.k("ident")[0:N_B, 0:N_B]).then_inc(s_turned, 1)
                pe.wait_ge(s_x, 16 * TB)
                for k in range(KD):
                    if k == 0:
                        pe.wait_ge(s_copied, 1)
                    for t in range(TB):
                        last = pe.transpose(K.bank[k][:, t * P:(t + 1) * P], xin[:, t, k * P:(k + 1) * P], K.k("ident"))
                    last.then_inc(s_turned, 1)


def param_rows(io, name, cnt, rows, which, at):
    dst = rows[at:at + cnt, which, :]
    mu = io["mu_shift"]
    if name == "mu_rkv":
        return [(dst, mu[0:1, 0:1536].rearrange("a (n p) -> (a n) p", p=P))]
    if name == "mu_wa":
        return [(dst, mu[0:1, 1536:1664])]
    if name == "mu_g":
        return [(dst, mu[0:1, 1664:1792])]
    if name == "mu_g2":
        return [(dst[:, 0:32], mu[0:1, 1792:1824])]
    if name == "idx_k_norm":
        return [(dst[:, 0:64], io[name]), (dst[:, 64:128], io[name])]
    if name == "ab_b_forget_2":
        return [(dst[:, 0:8], io[name])]
    ap = io[name]
    if name == "norm_ffn_2":
        return [(dst, ap.rearrange("a b (n p) -> (a b n) p", p=P))]
    if name == "r_k":
        return [(dst, ap.rearrange("a (n h) d -> (a n) (h d)", h=2))]
    if len(ap.shape) == 1:
        return [(dst, ap.rearrange("(n p) -> n p", p=P))]
    return [(dst, ap.rearrange("a (n p) -> (a n) p", p=P))]


class Modulation:

    def __init__(self, K, st, name, first):
        self.K, self.nc, self.name, self.first = K, K.nc, name, first
        self.seg = K.plan.segments[name]
        self.row = st.sb("row", [1, 2, WC])
        self.s_silu, self.s_row, self.s_turned = st.sems("silu_c", "row_out", "row_turned")

    def loop(self, e, body):
        n = self.seg["count"]
        for r in range(min(n, RING)):
            body(r, 0)
        if n > RING:
            with e.Fori(0, n // RING - 1) as i:
                for r in range(RING, 2 * RING):
                    body(r, i)

    def tensor(self, pe):
        K = self.K
        if self.first == 0:
            pe.wait_ge(self.s_silu, 1)

        def turn(r, i):
            pe.wait_ge(self.s_row, r + 1 + RING * i)
            for m in range(2):
                last = pe.matmul(K.bank[5][:, bass.ds(self.first + 2 * r + m + 2 * RING * i, 1)],
                                 self.row[:, r % 2, m * P:(m + 1) * P], K.k("ident")[0:1, 0:1], start=True, stop=True)
            last.then_inc(self.s_turned, 1)

        def body(r, i):
            n = self.seg["n0"] + r
            pe.wait_ge(K.loaded[n % RING], 16 * (n // RING + 1) + 16 * i)
            w = K.ring[:, n % RING, :].rearrange("p (k n) -> p k n", n=WC)
            product(pe, K.bank[6 + r % 2][0:1, 0:WC], [(K.coef[:, k:k + 1], w[:, k, :]) for k in range(KD)]).then_inc(K.tiles_done, 1)
            if r > 0:
                turn(r - 1, i)
        self.loop(pe, body)
        turn(self.seg["count"] - 1, 0)

    def silu(self):
        K = self.K
        self.nc.scalar.activation(K.coef[:, 0:8], K.par[:, COL["c"]:COL["c"] + 8], ACT.Silu).then_inc(self.s_silu, 1)

    def scalar(self, act):
        K = self.K

        def body(r, i):
            act.wait_ge(K.tiles_done, self.seg["mark0"] + r + 1 + RING * i)
            self.nc.scalar.activation(self.row[:, r % 2, :], K.bank[6 + r % 2][0:1, 0:WC], ACT.Copy).then_inc(self.s_row, 1)
        self.loop(act, body)

    def vector(self, dve):
        K, v, mod, coef = self.K, self.nc.vector, self.K.mod, self.K.coef
        par = lambda name: K.par[:, COL[name]:COL[name] + KD]
        dve.wait_ge(self.s_turned, self.seg["count"])
        a, b = self.first, self.first + 2 * self.seg["count"]
        v.tensor_tensor(mod[:, a:b], K.bank[5][:, a:b], K.par[:, a:b], ALU.add)
        dve.drain()
        if self.first == 0:
            v.scalar_tensor_tensor(coef[:, 8:16], mod[:, 8:16], 1.0, par("mix_pre_norm"), ALU.add, ALU.mult)
        elif b == 48:
            v.tensor_tensor(coef[:, 16:24], mod[:, 16:24], par("mix_post_norm"), ALU.mult)
            v.scalar_tensor_tensor(coef[:, 24:32], mod[:, 32:40], 1.0, par("ffn_pre_norm"), ALU.add, ALU.mult)
            v.tensor_tensor(coef[:, 32:40], mod[:, 40:48], par("ffn_post_norm"), ALU.mult)


def mod_stage(K):
    nc = K.nc
    with stage(K, "mod1") as st:
        M = Modulation(K, st, "mod1", 0)
        nxt = SumOfSquares(K, st, "next", tiles_of(K.x), tiles_of(K.h), 4)
        with nc.Block() as block:
            @block.sync
            def _(sp):
                K.stream(sp, K.plan.end("mod1") + RING)

            @block.tensor
            def _(pe):
                M.tensor(pe)
                nxt.columns(pe)

            @block.gpsimd
            def _(pool):
                nxt.add(pool, nc.gpsimd)

            @block.scalar
            def _(act):
                M.silu()
                for k in range(KD):
                    nxt.square(k)
                M.scalar(act)
                nxt.preload()

            @block.vector
            def _(dve):
                M.vector(dve)
        K.sum_bank = nxt.bank


def norm_stage(K, name, jobs, carry=False, loads=None):
    nc = K.nc
    with stage(K, name) as st:
        sq = st.sb("sq", [P, sum(len(job[0]) for job in jobs), T])
        s_w, = st.sems("written")
        sums, rstds, at = [], [], 0
        for j, (tiles, width, _) in enumerate(jobs):
            sums.append(SumOfSquares(K, st, f"job{j}", tiles, [sq[:, at + i, :] for i in range(len(tiles))], j))
            rstds.append(Rstd(K, st, f"job{j}", j, 7 - j, width, sums[-1]))
            at += len(tiles)
        nxt = SumOfSquares(K, st, "next", tiles_of(K.x), tiles_of(K.h), 3) if carry else None
        with nc.Block() as block:
            @block.sync
            def _(sp):
                if loads:
                    loads(sp)

            @block.scalar
            def _(act):
                for s in sums:
                    for i in range(len(s.src)):
                        s.square(i)
                for r in rstds:
                    r.root(act)
                if carry:
                    for k in range(KD):
                        act.wait_ge(s_w, k + 1)
                        nxt.square(k)
                    nxt.preload()

            @block.gpsimd
            def _(pool):
                if carry:
                    nxt.add(pool, nc.gpsimd)

            @block.tensor
            def _(pe):
                for s in sums:
                    s.columns(pe)
                for r in rstds:
                    r.spread(pe)
                if carry:
                    nxt.columns(pe)

            @block.vector
            def _(dve):
                for s in sums:
                    s.add(dve, nc.vector)
                for r in rstds:
                    r.invert(dve)
                for r, (tiles, _, write) in zip(rstds, jobs):
                    dve.wait_ge(r.s_out, 1)
                    for i in range(len(tiles)):
                        write(i, r.value, dve).then_inc(s_w, 1)
        if carry:
            K.sum_bank = nxt.bank


def residual_norm(K, name, coef):
    v = K.nc.vector

    def write(i, rstd, dve):
        v.scalar_tensor_tensor(K.h[:, i, :], K.h[:, i, :], coef(i), rstd, ALU.mult, ALU.mult)
        dve.drain()
        return v.tensor_tensor(K.x[:, i, :], K.x[:, i, :], K.h[:, i, :], ALU.add)

    norm_stage(K, name, [(tiles_of(K.h), D, write)], carry=True)


def small_job(K, tiles, gains, width):
    return tiles, width, lambda i, rstd, dve: K.nc.vector.scalar_tensor_tensor(
        tiles[i], tiles[i], gains[i], rstd, ALU.mult, ALU.mult)


THIRDS = (4, 4, 3)


def ffn_chunk(g, u, d, r, t=0):
    ups = 8 if isinstance(t, int) is False or t < 2 else 6
    if r >= Split.PERIOD:
        r, t = r - Split.PERIOD, t + 1
        ups = 8
    if r < ups:
        return (g, u)[r % 2][:, :, bass.ds((r // 2) * WC + 4 * WC * t, WC)]
    return d[:, bass.ds(8 * t, ups), (r - ups) * WC:(r - ups + 1) * WC]


def ffn_stage(K, name, residual, norm):
    nc, plan = K.nc, K.plan
    s = plan.segments[name]
    g_dram, u_dram, d_dram = s["parts"]
    with stage(K, name) as st:
        S = Split(K, st, norm)
        ah, al = st.sb("act_hi", [P, 8, T], F32R), st.sb("act_lo", [P, 8, T], F32R)
        g, a = st.sb("silu", [P, 2, T]), st.sb("act", [P, 2, T])
        s_silu, s_act, s_al, s_free = st.sems("silu", "act", "act_low", "out_read")
        nxt = SumOfSquares(K, st, "next", tiles_of(K.x), tiles_of(K.h), 0) if residual else None
        C_SILU, C_ACT, C_AL, C_FREE = 2, 2, 2, 4

        def thirds(e, body):
            with e.Fori(0, 2) as t:
                body(t, THIRDS[0], False)
            body(2, THIRDS[2], True)

        def words_of(r, t, steps, last):
            return 2 * steps * WC if last and r >= 2 * steps else SLOT

        with nc.Block() as block:
            @block.sync
            def _(sp):
                def load(r, t):
                    sp.wait_ge(K.low_done, s["split0"] + r - 3 + S.PERIOD * t)
                    K.load(sp, s["n0"] + r, ffn_chunk(g_dram, u_dram, d_dram, r, t))

                with sp.Fori(0, 2) as t:
                    for r in range(RING, RING + S.PERIOD):
                        load(r, t)
                for r in range(RING, 10):
                    load(r, 2)
                K.issued = plan.end(name)
                K.stream(sp, K.issued + RING)

            @block.tensor
            def _(pe):
                S.sums(pe)

                def body(t, steps, last):
                    for p in range(steps):
                        for which in range(2):
                            wh, wl = S.chunk(pe, name, 2 * p + which, WC, t)
                            for m in range(2):
                                pe.wait_ge((s_silu, s_act)[which], 2 * p + m + 1 + 8 * t)
                                c = slice(m * P, (m + 1) * P)
                                product3(pe, K.bank[2 * which + m][:, :],
                                         (((wh[:, k, c], wl[:, k, c]), S.feature(pe, k, p == which == m == 0)) for k in range(KD))
                                         ).then_inc(K.tiles_done, 1)
                    nf = 2 * steps

                    def hidden(f, wait):
                        if wait:
                            pe.wait_ge(s_al, f + 1 + C_AL + 8 * t)
                        return ah[:, f, :], al[:, f, :]

                    for d in range(4):
                        wh, wl = S.chunk(pe, name, nf + d, WC, t)
                        for m in range(2):
                            pe.wait_ge(s_free, 2 * d + m + 1 + 8 * t)
                            c = slice(m * P, (m + 1) * P)
                            product3(pe, K.bank[4 + 2 * (d % 2) + m][:, :],
                                     (((wh[:, f, c], wl[:, f, c]), hidden(f, d == m == 0)) for f in range(nf))
                                     ).then_inc(K.tiles_done, 1)
                    if last and nxt:
                        nxt.columns(pe)
                thirds(pe, body)

            @block.scalar
            def _(act):
                for _ in range(C_SILU):
                    act.sem_inc(s_silu, 1)
                S.squares(act)
                S.high(act, name, 0)
                S.features_scalar(act)

                def body(t, steps, last):
                    n = 2 * steps + 4
                    for r in range(n):
                        if not (last and r == n - 1):
                            S.high(act, name, r + 1, t, words_of(r + 1, t, steps, last))
                        if r < 2 * steps and r % 2 == 0:
                            for m in range(2):
                                act.wait_ge(K.tiles_done, plan.tile(name, r, m) + 2 * S.PERIOD * t)
                                act.wait_ge(s_act, r + m + 1 + 8 * t)
                                nc.scalar.activation(g[:, m, :], K.bank[m][:, :], ACT.Silu).then_inc(s_silu, 1)
                        if last and nxt and r >= 2 * steps:
                            for m in range(2):
                                k = 2 * (r - 2 * steps) + m
                                act.wait_ge(s_free, C_FREE + 8 * t + k + 1)
                                nxt.square(k)
                thirds(act, body)
                if nxt:
                    nxt.preload()

            @block.vector
            def _(dve):
                for _ in range(C_ACT):
                    dve.sem_inc(s_act, 1)
                for _ in range(C_FREE):
                    dve.sem_inc(s_free, 1)
                S.invert(dve)
                S.features_vector(dve, lambda k: K.h[:, k, :], lambda e: S.low(e, name, 0))
                if not residual:
                    dve.wait_ge(S.s_hl, KD // 2)
                    dve.wait_ge(S.s_hl2, KD // 2)
                    nc.vector.memset(K.h[:, :, :], 0.0)
                    dve.drain()

                def body(t, steps, last):
                    n = 2 * steps + 4
                    for r in range(n):
                        if not (last and r == n - 1):
                            S.low(dve, name, r + 1, t, words_of(r + 1, t, steps, last))
                        if r >= 2 * steps:
                            for m in range(2):
                                d = r - 2 * steps
                                to = (K.x if residual else K.h)[:, 2 * d + m, :]
                                dve.wait_ge(K.tiles_done, plan.tile(name, r, m) + 2 * S.PERIOD * t)
                                nc.vector.scalar_tensor_tensor(to, K.bank[4 + 2 * (d % 2) + m][:, :], 0.5 if residual else 1.0,
                                                               to, ALU.mult, ALU.add).then_inc(s_free, 1)
                        elif r % 2 == 1:
                            for m in range(2):
                                i = r - 1 + m
                                dve.wait_ge(K.tiles_done, plan.tile(name, r, m) + 2 * S.PERIOD * t)
                                dve.wait_ge(s_silu, i + 1 + C_SILU + 8 * t)
                                dve.wait_ge(s_al, i + 1 + 8 * t)
                                nc.vector.tensor_tensor(a[:, m, :], g[:, m, :], K.bank[2 + m][:, :], ALU.mult).then_inc(s_act, 1)
                thirds(dve, body)

            @block.gpsimd
            def _(pool):
                for _ in range(C_AL):
                    pool.sem_inc(s_al, 1)
                S.features_pool(pool, lambda k: K.h[:, k, :])

                def body(t, steps, last):
                    for i in range(2 * steps):
                        pool.wait_ge(s_act, i + 1 + C_ACT + 8 * t)
                        nc.gpsimd.tensor_tensor(ah[:, i, :], a[:, i % 2, :], K.k("ones")[:, 0:1].broadcast_to([P, T]), ALU.mult)
                        pool.drain()
                        nc.gpsimd.tensor_tensor(al[:, i, :], a[:, i % 2, :], ah[:, i, :].bitcast(F32), ALU.subtract).then_inc(s_al, 1)
                thirds(pool, body)
                if nxt:
                    nxt.add(pool, nc.gpsimd)
        if nxt:
            K.sum_bank = nxt.bank


def linear_stage(K, name, tiles, banks=8, scalar=lambda t: t % 2 == 1, extra=None, src=None, norm=None, carry=False):
    nc, plan = K.nc, K.plan
    extra = extra or {}
    src = src or (lambda k: K.h[:, k, :])
    with stage(K, name) as st:
        S = Split(K, st, norm)
        s_v, s_s = st.sems("vector_out", "scalar_out")
        nxt = SumOfSquares(K, st, "next", tiles_of(K.x), tiles_of(K.h), 7) if carry else None
        mine = [scalar(t) for t in range(len(tiles))]
        if "sems" in extra:
            extra["sems"](st)
        if "box" in extra:
            extra["box"]["read"] = s_v
        chunks = []
        for t, (seg, j, _, _, _, _, _, words) in enumerate(tiles):
            if not chunks or chunks[-1][:2] != (seg, j):
                chunks.append((seg, j, words, []))
            chunks[-1][3].append(t)

        with nc.Block() as block:
            @block.sync
            def _(sp):
                if "sync" in extra:
                    extra["sync"](sp)
                K.stream(sp, plan.end(tiles[-1][0]) + RING)

            @block.tensor
            def _(pe):
                S.sums(pe)
                for seg, j, _, members in chunks:
                    w = S.chunk(pe, seg, j, tiles[members[0]][3])
                    for t in members:
                        shape = tiles[t][5]
                        if t >= banks:
                            o = t - banks
                            pe.wait_ge(s_s if mine[o] else s_v, sum(x == mine[o] for x in mine[:o + 1]))
                        product3(pe, K.bank[t % banks][0:shape[0], 0:shape[1]], tiles[t][4](S, pe, w, t == 0)).then_inc(K.tiles_done, 1)
                if carry:
                    nxt.columns(pe)
                if "tensor" in extra:
                    extra["tensor"](pe)

            def evacuate(e, side, split):
                for n, (seg, j, words, members) in enumerate(chunks):
                    if n + 1 < len(chunks):
                        a, b, w, _ = chunks[n + 1]
                        split(e, a, b, 0, w)
                    for t in members:
                        if mine[t] == side:
                            e.wait_ge(K.tiles_done, plan.tile(seg, j, tiles[t][2]))
                            shape = tiles[t][5]
                            ins = tiles[t][6](K.bank[t % banks][0:shape[0], 0:shape[1]], "scalar" if side else "vector")
                            ins.then_inc(s_s if side else s_v, 1)
                        elif carry:
                            e.wait_ge(s_v, t + 1)
                            nxt.square(t)
                        elif "helper" in extra:
                            extra["helper"](e, t, K.bank[t % banks])

            @block.scalar
            def _(act):
                S.squares(act)
                S.high(act, chunks[0][0], chunks[0][1], 0, chunks[0][2])
                S.features_scalar(act)
                evacuate(act, True, S.high)
                if carry:
                    nxt.preload()
                if "scalar" in extra:
                    extra["scalar"](act)

            @block.vector
            def _(dve):
                S.invert(dve)
                S.features_vector(dve, src, lambda e: S.low(e, chunks[0][0], chunks[0][1], 0, chunks[0][2]))
                if "before" in extra:
                    extra["before"](dve)
                evacuate(dve, False, S.low)
                if "vector" in extra:
                    extra["vector"](dve)

            @block.gpsimd
            def _(pool):
                S.features_pool(pool, src)
                if carry:
                    nxt.add(pool, nc.gpsimd)
        if carry:
            K.sum_bank = nxt.bank


def copier(nc, dst, scale=None):
    def go(bank, engine):
        if engine == "scalar":
            return nc.scalar.copy(dst, bank) if scale is None else nc.scalar.activation(dst, bank, ACT.Copy, scale=scale)
        return nc.vector.tensor_copy(dst, bank) if scale is None else nc.vector.tensor_scalar(dst, bank, scale, None, ALU.mult)
    return go


def feature_pairs(c0, rows=P):
    return lambda S, pe, w, wait: (((w[0][:, k, c0:c0 + rows], w[1][:, k, c0:c0 + rows]), S.feature(pe, k, wait))
                                   for k in range(KD))


def token_pairs(b):
    return lambda S, pe, w, wait: ((S.feature(pe, k, wait, slice(b * P, (b + 1) * P)), (w[0][:, k, :], w[1][:, k, :]))
                                   for k in range(KD))


def out_stage(K, name, y, residual):
    nc = K.nc

    def evac(n):
        if residual:
            return lambda bank, engine: nc.vector.tensor_tensor(K.x[:, n, :], bank, K.x[:, n, :], ALU.add)
        return copier(nc, K.h[:, n, :])

    tiles = [(name, n // 2, n % 2, WC, feature_pairs((n % 2) * P), (P, T), evac(n), SLOT) for n in range(KD)]
    if residual:
        linear_stage(K, name, tiles, banks=7, scalar=lambda t: False, src=y, carry=True)
    else:
        linear_stage(K, name, tiles, src=y)


def finish_stage(K):
    nc = K.nc
    with stage(K, "finish") as st:
        out = st.sb("out", [P, TB, D])
        s_h, s_t, s_cv, s_ca, s_d = st.sems("normed", "turned", "copied_vector", "copied_scalar", "stored")
        R = Rstd(K, st, "norm", K.sum_bank, 7, D)
        with nc.Block() as block:
            @block.scalar
            def _(act):
                R.root(act)
                for half in range(2):
                    act.wait_ge(s_t, 4 * half + 4)
                    for t in (1, 3):
                        nc.scalar.copy(out[:, t, half * 512:half * 512 + 512], K.bank[2 * t + half][:, :]).then_inc(s_ca, 1)

            @block.vector
            def _(dve):
                R.invert(dve)
                dve.wait_ge(R.s_out, 1)
                for k in range(KD):
                    nc.vector.scalar_tensor_tensor(K.h[:, k, :], K.x[:, k, :], K.p("norm_final_2", k), R.value,
                                                   ALU.mult, ALU.mult).then_inc(s_h, 1)
                for half in range(2):
                    dve.wait_ge(s_t, 4 * half + 4)
                    for t in (0, 2):
                        nc.vector.tensor_copy(out[:, t, half * 512:half * 512 + 512], K.bank[2 * t + half][:, :]).then_inc(s_cv, 1)

            @block.tensor
            def _(pe):
                R.spread(pe)
                for k in range(KD):
                    pe.wait_ge(s_h, k + 1 if k < 4 else KD)
                    for t in range(TB):
                        last = pe.transpose(K.bank[2 * t + k // 4][:, (k % 4) * P:(k % 4) * P + P],
                                            K.h[:, k, t * P:(t + 1) * P], K.k("ident"))
                    last.then_inc(s_t, 1)

            @block.sync
            def _(sp):
                for half in range(2):
                    for t in range(TB):
                        sp.wait_ge(s_ca if t % 2 else s_cv, 2 * half + t // 2 + 1)
                        sp.dma_start(K.io["out"][0, t * P:(t + 1) * P, half * 512:half * 512 + 512],
                                     out[:, t, half * 512:half * 512 + 512]).then_inc(s_d, 16)
                sp.wait_ge(s_d, 16 * 2 * TB)


def in_proj_stage(K, M, norm):
    nc, plan, io = K.nc, K.plan, K.io
    w_in = io["w_in"][0].rearrange("(k p) n -> p k n", p=P)
    box = {}

    def shifted(t, rows, mu, dst):
        def go(bank, engine):
            nc.vector.wait_ge(box["part_done"], t - 2)
            return nc.vector.scalar_tensor_tensor(dst, bank, K.coef[0:rows, 40 + mu:41 + mu],
                                                  box["part"][0:rows, t % 2, 0:T], ALU.mult, ALU.add)
        return go

    tiles = [("in_q", 0, m, WC, feature_pairs(m * P), (P, T), copier(nc, M.cq[:, m, :]), SLOT) for m in range(2)]
    tiles.append(("in_kv", 0, 0, P, feature_pairs(0), (P, T), copier(nc, M.ckv[:, :]), KD * P))
    mus = [None] * 3
    for n in range(12):
        tiles.append(("in_rkv", n // 2, n % 2, WC, feature_pairs((n % 2) * P), (P, T), shifted(3 + n, P, n, M.rkv[:, n, :]), SLOT))
        mus.append(n)
    for n, (seg, m, width, rows, dst) in enumerate((("in_lora", 0, WC, P, M.wa), ("in_lora", 1, WC, P, M.g), ("in_lora2", 0, 32, 32, M.g2))):
        tiles.append((seg, 0, m, width, feature_pairs(m * P, rows), (rows, T), shifted(15 + n, rows, 12 + n, dst[0:rows, :]), KD * width))
        mus.append(12 + n)

    def sems(st):
        box["wik"], box["wiw"] = st.sb("wik", [P, KD, 2 * IDX_D]), st.sb("wiw", [P, KD, 8])
        box["part"] = st.sb("part", [P, 2, T + 1])
        box["w"], box["side"], box["part_done"], box["zero"] = st.sems("side_in", "side", "part", "zero")
        box["evac"] = None

    def sync(sp):
        for half in range(2):
            sp.dma_start(box["wik"][:, :, half * IDX_D:(half + 1) * IDX_D], w_in[:, :, O_IK:O_IW]).then_inc(box["w"], 16)
        sp.dma_start(box["wiw"][:, :, :], w_in[:, :, O_IW:O_R]).then_inc(box["w"], 16)

    def tensor(pe):
        pe.wait_ge(box["w"], 48)
        product(pe, K.bank[6][:, :], [(box["wik"][:, k, :], K.h[:, k, :]) for k in range(KD)]).then_inc(box["side"], 1)
        for b in range(TB):
            last = product(pe, K.bank[7][:, 8 * b:8 * b + 8],
                           [(K.h[:, k, b * P:(b + 1) * P], box["wiw"][:, k, :]) for k in range(KD)])
        last.then_inc(box["side"], 1)

    def before(dve):
        nc.vector.memset(box["part"][:, :, 0:1], 0.0).then_inc(box["zero"], 1)
        nc.vector.tensor_scalar(K.coef[:, 40:55], K.par[:, COL["mu_rkv"]:COL["mu_rkv"] + 15], -1.0, 1.0, ALU.mult, ALU.add)
        dve.drain()

    def helper(e, t, bank):
        seg, j, m, _, _, shape, _, _ = tiles[t]
        if mus[t] is None:
            return
        if t == 3:
            e.wait_ge(box["zero"], 1)
        e.wait_ge(K.tiles_done, plan.tile(seg, j, m))
        if t >= 5:
            e.wait_ge(box["read"], t - 1)
        nc.scalar.activation(box["part"][0:shape[0], t % 2, 1:T + 1], bank[0:shape[0], :], ACT.Copy,
                             scale=K.p("mu_rkv", mus[t])[0:shape[0], :]).then_inc(box["part_done"], 1)

    def vector(dve):
        dve.wait_ge(box["side"], 1)
        nc.vector.tensor_copy(M.ik[:, :], K.bank[6][:, :])
        dve.wait_ge(box["side"], 2)
        nc.vector.tensor_scalar(M.iw[:, :], K.bank[7][:, 0:32], (8 * IDX_D) ** -0.5, None, ALU.mult)

    linear_stage(K, "inproj", tiles, banks=6, scalar=lambda t: False,
                 extra={"sems": sems, "box": box, "sync": sync, "tensor": tensor, "before": before, "helper": helper, "vector": vector}, norm=norm)


IDX_D = 64


def dsa_loads(K, A, sp):
    io = K.io
    sp.dma_start(A.rb[:, :], io["rel_bias"]).then_inc(K.dsa_bias_in, 16)
    sp.dma_start(A.bucket[:, :], io["bucket"]).then_inc(K.dsa_bias_in, 16)
    for h in range(8):
        sp.dma_start(A.wuk[:, h * 64:(h + 1) * 64], io["w_uk"][0, h]).then_inc(K.dsa_weights_in, 16)
        sp.dma_start(A.wuv[:, h, :], io["w_uv"][0, h]).then_inc(K.dsa_weights_in, 16)
    sp.dma_start(A.wuq[:, :, :], io["w_uq"][0].rearrange("(k p) h d -> p k (h d)", p=P)).then_inc(K.dsa_weights_in, 16)
    sp.dma_start(A.wiq[:, :, :], io["w_idx_q"][0].rearrange("(k p) h d -> p k (h d)", p=P)).then_inc(K.dsa_weights_in, 16)


def dsa_prep_stage(K, A, M):
    nc, io = K.nc, K.io
    with stage(K, "dsaprep") as st:
        wuq, wiq, wuk, rb, bucket = A.wuq, A.wiq, A.wuk, A.rb, A.bucket
        wukt = st.sb("wukt", [P, 4, P])
        rev = st.sb("rev", [8, 640])
        shifted = A.o
        q = st.sb("q", [P, 4, T])
        far = nc.dram_tensor("bias_by_distance", (8, 640), F32, kind="Internal").ap()
        s_rev, s_far, s_sh, s_pe, s_ev = st.sems("rev", "far", "sh", "pe", "ev")
        steps = []

        def put(mms, evac):
            steps.append((mms, evac))

        idt = K.k("ident")
        put([(K.bank[0][0:8, :], rb[:, :], bucket[:, 0:512])], lambda: nc.scalar.copy(rev[:, 0:512], K.bank[0][0:8, :]))
        put([(K.bank[1][0:8, 0:128], rb[:, :], bucket[:, 512:640])],
            lambda: nc.scalar.activation(rev[:, 512:640], K.bank[1][0:8, 0:128], ACT.Copy, bias=-BIG, scale=0.0))
        n_rev = len(steps)
        put([(K.bank[2][:, n * P:(n + 1) * P], wuk[:, n * P:(n + 1) * P], None) for n in range(4)],
            lambda: nc.scalar.copy(wukt[:, :, :].rearrange("p a b -> p (a b)"), K.bank[2][:, :]))
        n_ukt = len(steps)
        put([(K.bank[3][:, b * P:(b + 1) * P], M.ckv[:, b * P:(b + 1) * P], None) for b in range(4)],
            lambda: nc.scalar.copy(A.ckvt[:, :, :].rearrange("p a b -> p (a b)"), K.bank[3][:, :]))
        for n in range(4):
            b = (4 + n) % 8
            put([(K.bank[b][:, :], wuq[:, k, n * P:(n + 1) * P], M.cq[:, k, :]) for k in range(2)],
                lambda n=n, b=b: nc.scalar.copy(q[:, n, :], K.bank[b][:, :]))
        n_q = len(steps)
        for n in range(4):
            put([(K.bank[n][:, :], wiq[:, k, n * P:(n + 1) * P], M.cq[:, k, :]) for k in range(2)],
                lambda n=n: nc.scalar.copy(A.iq[:, n, :], K.bank[n][:, :]))
        for h in range(8):
            r, b = slice((h % 2) * 64, (h % 2) * 64 + 64), (4 + h) % 8
            put([(K.bank[b][:, :], wukt[r, h // 2, :], q[r, h // 2, :])],
                lambda h=h, b=b: nc.scalar.mul(A.qa[:, h, :], K.bank[b][:, :], HD ** -0.5))
        n_flip = len(steps)
        for h in range(8):
            b = (4 + h) % 8
            put([(K.bank[b][:, :], K.k("flip"), shifted[:, h, :])],
                lambda h=h, b=b: nc.scalar.copy(A.bias[:, h, :], K.bank[b][:, :]))

        with nc.Block() as block:
            @block.sync
            def _(sp):
                sp.wait_ge(s_ev, n_rev)
                sp.dma_start(far, rev[:, :]).then_inc(s_far, 16)
                sp.wait_ge(s_far, 16)
                sp.dma_start(shifted[:, :, :], bass.AP(tensor=far.tensor, offset=0, ap=[[1, P], [640, 8], [1, T]])).then_inc(s_sh, 16)

            @block.tensor
            def _(pe):
                pe.wait_ge(K.dsa_bias_in, 32)
                for n, (mms, _) in enumerate(steps):
                    if n == n_rev:
                        pe.wait_ge(K.dsa_weights_in, 16 * 18)
                    if n == n_flip:
                        pe.wait_ge(s_sh, 16)
                    need = max(n_q if n >= n_q + 4 else 0, n - 3)
                    if need > 0:
                        pe.wait_ge(s_ev, need)
                    for m, (out, a, b) in enumerate(mms):
                        if b is None:
                            last = pe.transpose(out, a, idt)
                        else:
                            last = pe.matmul(out, a, b, start=m == 0, stop=m == len(mms) - 1)
                    last.then_inc(s_pe, 1)

            @block.scalar
            def _(act):
                for n, (_, evac) in enumerate(steps):
                    act.wait_ge(s_pe, n + 1)
                    evac().then_inc(s_ev, 1)


def topk_stage(K, A, M):
    nc = K.nc
    with stage(K, "topk") as st:
        relu = st.sb("relu", [P, 2, T])
        sc = st.sb("scores", [P, 3, T])
        top = st.sb("top", [P, 8])
        s_pe, s_relu, s_acc, s_done, s_mask = st.sems("dots", "relu", "acc", "scored", "masked")
        mod = Modulation(K, st, "mod3", 24)
        with nc.Block() as block:
            @block.sync
            def _(sp):
                K.stream(sp, K.plan.end("mod3") + RING)

            @block.tensor
            def _(pe):
                for i in range(1, TB):
                    n = (i + 1) * P
                    for h in range(8):
                        m = (i - 1) * 8 + h
                        r = slice((h % 2) * 64, (h % 2) * 64 + 64)
                        if m >= 4:
                            pe.wait_ge(s_relu, m - 3)
                        pe.matmul(K.bank[m % 4][:, 0:n], A.iq[r, h // 2, i * P:(i + 1) * P], M.ik[r, 0:n],
                                  start=True, stop=True).then_inc(s_pe, 1)
                mod.tensor(pe)

            @block.scalar
            def _(act):
                for m in range(24):
                    n = (m // 8 + 2) * P
                    act.wait_ge(s_pe, m + 1)
                    if m >= 2:
                        act.wait_ge(s_acc, m - 1)
                    nc.scalar.activation(relu[:, m % 2, 0:n], K.bank[m % 4][:, 0:n], ACT.Relu).then_inc(s_relu, 1)
                mod.scalar(act)

            @block.gpsimd
            def _(pool):
                for i in range(1, TB):
                    pool.wait_ge(s_done, i)
                    part = sc[:, i - 1, i * P:(i + 1) * P]
                    nc.gpsimd.affine_select(out=part, in_=part, compare_op=ALU.is_ge, fill=CAUSAL_FILL, base=0,
                                            pattern=[[-1, P]], channel_multiplier=1).then_inc(s_mask, 1)

            @block.vector
            def _(dve):
                for m in range(24):
                    i, h = m // 8 + 1, m % 8
                    n = (i + 1) * P
                    dve.wait_ge(s_relu, m + 1)
                    acc, w = sc[:, i - 1, 0:n], M.iw[:, 8 * i + h:8 * i + h + 1]
                    if h == 0:
                        ins = nc.vector.tensor_scalar(acc, relu[:, m % 2, 0:n], w, None, ALU.mult)
                    else:
                        ins = nc.vector.scalar_tensor_tensor(acc, relu[:, m % 2, 0:n], w, acc, ALU.mult, ALU.add)
                    ins.then_inc(s_acc, 1)
                    if h == 7:
                        dve.drain()
                        dve.sem_inc(s_done, 1)
                    else:
                        dve.drain()
                for i in range(1, TB):
                    n = (i + 1) * P
                    buf = sc[:, i - 1, 0:n]
                    dve.wait_ge(s_mask, i)
                    for _ in range(TOPK // 8):
                        nc.vector.max(top[:, :], buf)
                        dve.drain()
                        nc.vector.match_replace(buf, top[:, :], buf, TAKEN)
                        dve.drain()
                    nc.vector.tensor_scalar(A.mask[:, i - 1, 0:n], buf, TAKEN, -BIG, ALU.not_equal, ALU.mult)
                mod.vector(dve)


def attention_stage(K, name, H, rows, q, k, v, vw, dest, bias=None, prep=None):
    nc = K.nc
    items = [(h, i) for h in range(H) for i in range(TB)]
    N = len(items)
    with stage(K, name) as st:
        S = st.sb("S", [P, 4, T])
        pt = st.sb("pt", [P, 2, T])
        bm = st.sb("bm", [P, 2, T]) if prep else None
        stat = st.sb("stat", [P, 4, 4])
        s_score, s_bm, s_biased, s_exp, s_norm, s_turned, s_pt, s_pv, s_out = st.sems(
            "scored", "bias_made", "biased", "exp", "normed", "turned", "probs_out", "pv", "out")
        lo = lambda h: (h % 2) * 64 if vw == 64 else 0
        with nc.Block() as block:
            @block.sync
            def _(sp):
                pass

            @block.tensor
            def _(pe):
                for n in range(N + 4):
                    if n < N:
                        h, i = items[n]
                        if n >= 2:
                            pe.wait_ge(s_biased, n - 1)
                        w = (i + 1) * P
                        pe.matmul(K.bank[n % 2][:, 0:w], q(h, i), k(h, w), start=True, stop=True).then_inc(s_score, 1)
                    if 3 <= n <= N + 2:
                        m = n - 3
                        h, i = items[m]
                        pe.wait_ge(s_norm, m + 1)
                        if m >= 2:
                            pe.wait_ge(s_pt, m - 1)
                        for s in range(i + 1):
                            last = pe.transpose(K.bank[2 + m % 2][:, s * P:(s + 1) * P], S[:, m % 4, s * P:(s + 1) * P], K.k("ident"))
                        last.then_inc(s_turned, 1)
                    if n >= 4:
                        m = n - 4
                        h, i = items[m]
                        pe.wait_ge(s_pt, m + 1)
                        if m >= 2:
                            pe.wait_ge(s_out, m - 1)
                        product(pe, K.bank[4 + m % 2][lo(h):lo(h) + vw, 0:P],
                                [(v(h, s), pt[:, m % 2, s * P:(s + 1) * P]) for s in range(i + 1)]).then_inc(s_pv, 1)

            @block.gpsimd
            def _(pool):
                if prep:
                    for n, (h, i) in enumerate(items):
                        if n >= 2:
                            pool.wait_ge(s_biased, n - 1)
                        prep(pool, bm[:, n % 2, 0:(i + 1) * P], h, i).then_inc(s_bm, 1)

            @block.vector
            def _(dve):
                for n in range(N + 2):
                    if n < N:
                        h, i = items[n]
                        w = (i + 1) * P
                        dve.wait_ge(s_score, n + 1)
                        if prep:
                            dve.wait_ge(s_bm, n + 1)
                        if n >= 4:
                            dve.wait_ge(s_turned, n - 3)
                        table = bm[:, n % 2, 0:w] if prep else bias(h, i)
                        nc.vector.tensor_tensor_reduce(out=S[:, n % 4, 0:w], in0=K.bank[n % 2][:, 0:w], in1=table, scale=1.0,
                                                       scalar=-3.0e38, op0=ALU.add, op1=ALU.max, accum_out=stat[:, n % 4, 0:1])
                        dve.drain()
                        nc.vector.tensor_scalar(stat[:, n % 4, 1:2], stat[:, n % 4, 0:1], -1.0, None, ALU.mult).then_inc(s_biased, 1)
                    if n >= 2:
                        m = n - 2
                        w = (items[m][1] + 1) * P
                        dve.wait_ge(s_exp, m + 1)
                        nc.vector.reciprocal(stat[:, m % 4, 3:4], stat[:, m % 4, 2:3])
                        dve.drain()
                        nc.vector.tensor_scalar(S[:, m % 4, 0:w], S[:, m % 4, 0:w], stat[:, m % 4, 3:4], None, ALU.mult).then_inc(s_norm, 1)

            @block.scalar
            def _(act):
                for n in range(N + 4):
                    if n < N:
                        w = (items[n][1] + 1) * P
                        act.wait_ge(s_biased, n + 1)
                        nc.scalar.activation(S[:, n % 4, 0:w], S[:, n % 4, 0:w], ACT.Exp, bias=stat[:, n % 4, 1:2], scale=1.0,
                                             accum_out=stat[:, n % 4, 2:3]).then_inc(s_exp, 1)
                    if 3 <= n <= N + 2:
                        m = n - 3
                        w = (items[m][1] + 1) * P
                        act.wait_ge(s_turned, m + 1)
                        if m >= 2:
                            act.wait_ge(s_pv, m - 1)
                        nc.scalar.copy(pt[:, m % 2, 0:w], K.bank[2 + m % 2][:, 0:w]).then_inc(s_pt, 1)
                    if n >= 4:
                        m = n - 4
                        h, i = items[m]
                        act.wait_ge(s_pv, m + 1)
                        nc.scalar.copy(dest(h, i), K.bank[4 + m % 2][lo(h):lo(h) + vw, 0:P]).then_inc(s_out, 1)


def value_stage(K, A, y):
    nc = K.nc
    with stage(K, "value") as st:
        s_pe, = st.sems("pe")
        with nc.Block() as block:
            @block.tensor
            def _(pe):
                for h in range(8):
                    pe.matmul(K.bank[h // 2][(h % 2) * 64:(h % 2) * 64 + 64, :], A.wuv[:, h, :], A.o[:, h, :],
                              start=True, stop=True).then_inc(s_pe, 1)

            @block.vector
            def _(dve):
                for n in range(4):
                    dve.wait_ge(s_pe, 2 * n + 2)
                    nc.vector.tensor_copy(y[:, n, :], K.bank[n][:, :])


class Bag:
    pass


def mixer1(K, norm):
    nc = K.nc
    with ExitStack() as st:
        sb = lambda n, shape: st.enter_context(nc.sbuf_tensor(n, shape, F32))
        M = Bag()
        y = sb("y", [P, KD, T])
        M.cq, M.ckv, M.ik, M.iw = sb("cq", [P, 2, T]), sb("ckv", [P, T]), sb("ik", [P, T]), sb("iw", [P, 32])
        with ExitStack() as rs:
            rb = lambda n, shape: rs.enter_context(nc.sbuf_tensor(n, shape, F32))
            M.rkv, M.wa, M.g, M.g2 = rb("rkv", [P, 12, T]), rb("wa", [P, T]), rb("g", [P, T]), rb("g2", [32, T])
            in_proj_stage(K, M, norm)
            rwkv(K, M, y)
        with ExitStack() as as_:
            ab = lambda n, shape: as_.enter_context(nc.sbuf_tensor(n, shape, F32))
            A = Bag()
            A.qa = K.h
            A.iq, A.ckvt, A.bias = ab("iq", [P, 4, T]), ab("ckvt", [P, TB, P]), ab("bias", [P, 8, T])
            A.o, A.wuv, A.mask = ab("o", [P, 8, T]), ab("wuv", [P, 8, 64]), ab("mask", [P, 3, T])
            A.wuq, A.wiq, A.wuk = ab("wuq", [P, 2, 512]), ab("wiq", [P, 2, 512]), ab("wuk", [P, 512])
            A.rb, A.bucket = ab("rb", [32, 8]), ab("bucket", [32, 640])
            norm_stage(K, "norm_dsa", loads=lambda sp: dsa_loads(K, A, sp), jobs=[small_job(K, [M.cq[:, 0, :], M.cq[:, 1, :]], [K.p("q_norm", 0), K.p("q_norm", 1)], 256),
                                       small_job(K, [M.ckv[:, :]], [K.p("kv_norm")], 128),
                                       small_job(K, [M.ik[:, :]], [K.p("idx_k_norm")], 128)])
            dsa_prep_stage(K, A, M)
            topk_stage(K, A, M)

            def prep(pool, out, h, i):
                w = (i + 1) * P
                table = A.bias[:, h, 384 - i * P:384 - i * P + w]
                if i == 0:
                    return nc.gpsimd.tensor_copy(out, table)
                return nc.gpsimd.tensor_tensor(out, table, A.mask[:, i - 1, 0:w], ALU.add)

            attention_stage(K, "dsa", 8, P, lambda h, i: A.qa[:, h, i * P:(i + 1) * P], lambda h, w: M.ckv[:, 0:w],
                            lambda h, s: A.ckvt[:, s, :], P, lambda h, i: A.o[:, h, i * P:(i + 1) * P], prep=prep)
            value_stage(K, A, y)
        out_stage(K, "out1", lambda k: y[:, k, :], False)


def rwkv_prep_stage(K, M, R, p):
    nc, io = K.nc, K.io
    r, k, v = M.rkv[:, p, :], M.rkv[:, 4 + p, :], M.rkv[:, 8 + p, :]
    tmp = lambda i: K.h[:, i, :]
    lw, L, a, kk, t0, eN, eA, eC = (tmp(i) for i in range(8))
    chunks = lambda ap: ap.rearrange("p (c t) -> p c t", t=C)
    with stage(K, f"rprep{p}") as st:
        s_w, s_lora, s_dots, s_sig, s_kk, s_sq, s_norm, s_root, s_l, s_exp, s_bd, s_zero = st.sems(
            "w", "lora", "dots", "sigmoid", "kk", "square", "norm", "root", "logs", "exp", "scaled", "zero")
        mod = Modulation(K, st, f"mod2_{p}", 16 + 2 * p)
        with nc.Block() as block:
            @block.sync
            def _(sp):
                if p == 0:
                    sp.dma_start(R.wl[0:64, :], io["w_decay_up"][0]).then_inc(s_w, 16)
                    sp.dma_start(R.wl[64:128, :], io["w_aaa_up"][0]).then_inc(s_w, 16)
                K.stream(sp, K.plan.end(f"mod2_{p}") + RING)

            @block.tensor
            def _(pe):
                if p == 0:
                    pe.wait_ge(s_w, 32)
                    pe.wait_ge(s_lora, 1)
                pe.matmul(K.bank[0][:, :], R.wl[0:64, p * P:(p + 1) * P], M.wa[0:64, :], start=True, stop=True).then_inc(s_dots, 1)
                pe.matmul(K.bank[1][:, :], R.wl[64:128, p * P:(p + 1) * P], M.wa[64:128, :], start=True, stop=True).then_inc(s_dots, 1)
                pe.wait_ge(s_sq, 1)
                pe.matmul(K.bank[2][:, :], K.k("heads"), t0, start=True, stop=True).then_inc(s_norm, 1)
                mod.tensor(pe)

            @block.scalar
            def _(act):
                if p == 0:
                    nc.scalar.activation(M.wa[0:64, :], M.wa[0:64, :], ACT.Tanh).then_inc(s_lora, 1)
                    nc.scalar.activation(M.g[:, :], M.g[:, :], ACT.Sigmoid)
                    nc.scalar.activation(M.g2[:, :], M.g2[:, :], ACT.Sigmoid)
                act.wait_ge(s_dots, 1)
                nc.scalar.activation(lw, K.bank[0][:, :], ACT.Sigmoid, bias=K.p("w0", p)).then_inc(s_sig, 1)
                act.wait_ge(s_dots, 2)
                nc.scalar.activation(a, K.bank[1][:, :], ACT.Sigmoid, bias=K.p("a0", p)).then_inc(s_sig, 1)
                act.wait_ge(s_kk, 1)
                nc.scalar.activation(t0, kk, ACT.Square).then_inc(s_sq, 1)
                act.wait_ge(s_norm, 1)
                nc.scalar.activation(t0, K.bank[2][:, :], ACT.Sqrt).then_inc(s_root, 1)
                act.wait_ge(s_l, 1)
                nc.scalar.activation(eA, eA, ACT.Exp).then_inc(s_exp, 1)
                nc.scalar.activation(eN, L, ACT.Exp, scale=-1.0).then_inc(s_exp, 1)
                nc.scalar.activation(eC, eC, ACT.Exp).then_inc(s_exp, 1)
                nc.scalar.activation(R.eP[:, :], L, ACT.Exp).then_inc(s_exp, 1)
                mod.scalar(act)

            @block.gpsimd
            def _(pool):
                if p == 0:
                    for n in range(6):
                        nc.gpsimd.memset(R.bd[:, n, :, :], 0.0)
                    pool.drain().then_inc(s_zero, 1)
                    pool.wait_ge(s_zero, 1)
                for hh in range(2):
                    q = slice(64 * hh, 64 * hh + 64)
                    nc.gpsimd.tensor_copy(R.bd[q, 5, :, q], chunks(v)[q])
                pool.wait_ge(s_bd, 1)
                pool.wait_ge(s_exp, 3)
                for hh in range(2):
                    q = slice(64 * hh, 64 * hh + 64)
                    nc.gpsimd.tensor_tensor(R.bd[q, 3, :, q], chunks(k)[q], chunks(eC)[q], ALU.mult)
                    nc.gpsimd.tensor_tensor(R.bd[q, 4, :, q], chunks(a)[q], chunks(eC)[q], ALU.mult)

            @block.vector
            def _(dve):
                nc.vector.tensor_scalar(kk, k, K.p("k_k", p), None, ALU.mult).then_inc(s_kk, 1)
                nc.vector.tensor_scalar(R.oka[:, :], K.p("k_a", p), -1.0, 1.0, ALU.mult, ALU.add)
                dve.wait_ge(s_sig, 1)
                nc.vector.tensor_scalar(lw, lw, NEG_SQRT_E, None, ALU.mult)
                dve.drain()
                nc.vector.tensor_tensor_scan(L, K.k("reset"), lw, 0.0, ALU.mult, ALU.add)
                dve.drain()
                nc.vector.tensor_tensor(eA, L, lw, ALU.subtract)
                end = chunks(L)[:, :, C - 1:C].broadcast_to([P, NCH, C])
                nc.vector.tensor_tensor(chunks(eC), end, chunks(L), ALU.subtract).then_inc(s_l, 1)
                dve.wait_ge(s_root, 1)
                nc.vector.tensor_scalar(t0, t0, 1e-12, None, ALU.max)
                dve.drain()
                nc.vector.reciprocal(t0, t0)
                dve.drain()
                nc.vector.scalar_tensor_tensor(kk, kk, -1.0, t0, ALU.mult, ALU.mult)
                dve.drain()
                dve.wait_ge(s_sig, 2)
                nc.vector.tensor_scalar(t0, a, K.p("k_a", p), R.oka[:, :], ALU.mult, ALU.add)
                dve.drain()
                nc.vector.tensor_tensor(k, k, t0, ALU.mult)
                nc.vector.scalar_tensor_tensor(a, kk, -1.0, a, ALU.mult, ALU.mult)
                dve.drain().then_inc(s_bd, 1)
                if p == 0:
                    dve.wait_ge(s_zero, 1)
                dve.wait_ge(s_exp, 1)
                for n, (x, e) in enumerate(((kk, eA), (a, eN), (k, eN))):
                    if n == 1:
                        dve.wait_ge(s_exp, 2)
                    for hh in range(2):
                        q = slice(64 * hh, 64 * hh + 64)
                        nc.vector.tensor_tensor(R.bd[q, n, :, q], chunks(x)[q], chunks(e)[q], ALU.mult)
                dve.wait_ge(s_exp, 4)
                nc.vector.tensor_tensor(R.rt[:, :], r, R.eP[:, :], ALU.mult)
                mod.vector(dve)


def rwkv_chunk_stage(K, R, p, yout):
    nc = K.nc
    BD_A, BD_B, BD_K, BD_KH, BD_BH, BD_V = range(6)
    idt = K.k("ident")
    wide = lambda ap: ap.unsqueeze(1).broadcast_to([P, 4, P])
    with stage(K, f"rchunk{p}") as st:
        G = []
        for g in range(2):
            B = Bag()
            B.vt, B.kht, B.bht = (K.h[:, 2 + 3 * g + n, :].rearrange("p (c t) -> p c t", t=P) for n in range(3))
            B.at, B.akt, B.nt, B.T, B.TT, B.X, B.rbk = (
                st.sb(f"{n}{g}", [P, 4, P]) for n in ("at", "akt", "nt", "t", "tt", "x", "rbk"))
            G.append(B)
        S = st.sb("state", [P, 2, P])
        s_pe, s_dve, s_act, s_sp, s_sv = st.sems("products", "vector_out", "scalar_out", "state_product", "state")
        steps = []

        def flat(t):
            return t[:, :, :].rearrange("p a b -> p (a b)")

        def add(g, mms, evacs):
            steps.append((g, mms, evacs))

        def group_steps(g):
            B = G[g]
            b0 = 4 * g
            bd = lambda n, c: R.bd[:, n, 4 * g + c, :]
            rt = lambda c: R.rt[:, (4 * g + c) * C:(4 * g + c + 1) * C]
            out = []

            def put(mms, evacs):
                out.append((g, mms, evacs))

            def full(lhs, rhs, bank, w=P, at=0, more=None):
                ms = []
                for c in range(4):
                    o = K.bank[bank][:, c * P + at:c * P + at + w]
                    ms.append((o, lhs(c), rhs(c), True, more is None))
                    if more:
                        ms.append((o, more[0](c), more[1](c), False, True))
                return ms

            def turn(n, bank):
                return [(K.bank[bank][:, c * P:(c + 1) * P], bd(n, c), None, True, True) for c in range(4)]

            v = nc.vector
            a = nc.scalar
            bank = lambda n: K.bank[b0 + n][:, :]
            bank3 = lambda n: K.bank[b0 + n][:, :].rearrange("p (c t) -> p c t", t=P)
            sl = lambda t: (lambda c: t[:, c, :])
            put(full(lambda c: bd(BD_B, c), lambda c: bd(BD_A, c), b0),
                [("dve", lambda: v.tensor_tensor(B.nt[:, :, :], bank3(0), wide(K.k("strict")), ALU.mult)),
                 ("dve", lambda: v.tensor_tensor(B.TT[:, :, :], bank3(0), wide(K.k("first_t")), ALU.mult))])
            put(full(lambda c: bd(BD_A, c), lambda c: bd(BD_B, c), b0 + 1),
                [("dve", lambda: v.tensor_tensor(B.T[:, :, :], bank3(1), wide(K.k("first")), ALU.mult)),
                 ("dve", lambda: v.tensor_tensor(B.TT[:, :, :], B.TT[:, :, :], wide(idt), ALU.add)),
                 ("drain", None),
                 ("dve", lambda: v.tensor_tensor(B.T[:, :, :], B.T[:, :, :], wide(idt), ALU.add))])
            turns = [(BD_V, B.vt), (BD_KH, B.kht), (BD_BH, B.bht), (BD_A, B.at)]
            extra = []
            for m, (n, dst) in enumerate(turns):
                extra.append((g, turn(n, b0 + 3), [("act", lambda dst=dst: a.copy(flat(dst), bank(3)))]))
            extra.append((g, full(lambda c: bd(BD_K, c), lambda c: bd(BD_A, c), b0 + 3),
                [("dve", lambda: v.tensor_tensor(B.akt[:, :, :], bank3(3), wide(K.k("strict")), ALU.mult))]))
            up = K.k("upto").unsqueeze(1).broadcast_to([P, 8, C])
            extra.append((g, full(lambda c: bd(BD_B, c), rt, b0 + 3, C) + full(lambda c: bd(BD_K, c), rt, b0 + 3, C, C),
                [("dve", lambda: v.tensor_tensor(B.rbk[:, :, :].rearrange("p a (b t) -> p (a b) t", t=C),
                                                 K.bank[b0 + 3][:, :].rearrange("p (c t) -> p c t", t=C), up, ALU.mult))]))
            extra.append((g, full(sl(B.akt), sl(B.vt), b0 + 3), [("act", lambda: a.copy(flat(B.akt), bank(3)))]))
            for s in LEVELS[1:]:
                put(full(sl(B.nt), sl(B.T), b0),
                    [("dve", lambda s=s: v.tensor_tensor(B.X[:, :, :], bank3(0), wide(K.k(f"low{s}")), ALU.mult))])
                if extra:
                    out.append(extra.pop(0))
                last = s == LEVELS[-1]
                mms = full(sl(B.X), sl(B.TT), b0 + 2)
                ev = [("dve", lambda: v.tensor_tensor(B.TT[:, :, :], bank3(2), B.TT[:, :, :], ALU.add))]
                if not last:
                    mms = full(sl(B.TT), sl(B.X), b0 + 1) + mms
                    ev = [("dve", lambda: v.tensor_tensor(B.T[:, :, :], bank3(1), B.T[:, :, :], ALU.add))] + ev
                put(mms, ev)
                if extra:
                    out.append(extra.pop(0))
            assert not extra
            put(full(sl(B.TT), sl(B.at), b0), [("act", lambda: a.copy(flat(B.X), bank(0)))])
            put(full(sl(B.TT), sl(B.akt), b0 + 1), [("act", lambda: a.copy(flat(B.T), bank(1)))])
            ta, takv = B.X, B.T
            rb = lambda c: B.rbk[:, c, 0:C]
            rk = lambda c: B.rbk[:, c, C:P]

            def m_out(c):
                end = R.eP[:, (4 * g + c + 1) * C - 1:(4 * g + c + 1) * C]
                return lambda: v.scalar_tensor_tensor(R.M[:, 4 * g + c, :], idt, end, K.bank[b0 + 2][:, c * P:(c + 1) * P], ALU.mult, ALU.add)

            put(full(sl(ta), sl(B.bht), b0 + 2), [("dve", m_out(c)) for c in range(4)])
            sp4 = lambda t: t[:, 4 * g * C:4 * (g + 1) * C].rearrange("p (c t) -> p c t", t=C)
            put(full(sl(ta), rb, b0 + 3, C),
                [("dve", lambda: v.tensor_tensor(sp4(R.Q), bank3(3)[:, :, 0:C], sp4(R.rt), ALU.add))])
            put(full(sl(B.bht), sl(takv), b0, P, 0, (sl(B.kht), sl(B.vt))),
                [("act", lambda: a.copy(R.Z[:, 4 * g:4 * g + 4, :].rearrange("p a b -> p (a b)"), bank(0)))])
            put(full(sl(takv), rb, b0 + 1, C, 0, (sl(B.vt), rk)),
                [("act", lambda: a.copy(sp4(R.Y), bank3(1)[:, :, 0:C]))])
            return out

        one, two = group_steps(0), group_steps(1)
        for x, z in zip(one, two):
            steps += [x, z]
        n_dve = [sum(e == "dve" for e, _ in ev) for _, _, ev in steps]
        n_act = [sum(e == "act" for e, _ in ev) for _, _, ev in steps]
        N = len(steps)

        with nc.Block() as block:
            @block.sync
            def _(sp):
                pass

            @block.tensor
            def _(pe):
                for n, (g, mms, _) in enumerate(steps):
                    if n >= 2:
                        d, a = sum(n_dve[:n - 1]), sum(n_act[:n - 1])
                        if d:
                            pe.wait_ge(s_dve, d)
                        if a:
                            pe.wait_ge(s_act, a)
                    for out, l, r, start, stop in mms:
                        if r is None:
                            last = pe.transpose(out, l, idt)
                        else:
                            last = pe.matmul(out, l, r, start=start, stop=stop)
                    last.then_inc(s_pe, 1)
                pe.wait_ge(s_dve, sum(n_dve))
                pe.wait_ge(s_act, sum(n_act))
                for c in range(1, NCH):
                    pe.wait_ge(s_sv, c)
                    if c < NCH - 1:
                        pe.matmul(K.bank[c % 2][:, 0:P], R.M[:, c, :], S[:, (c - 1) % 2, :], start=True, stop=True).then_inc(s_sp, 1)
                    last = pe.matmul(K.bank[2][:, c * C:(c + 1) * C], S[:, (c - 1) % 2, :], R.Q[:, c * C:(c + 1) * C], start=True, stop=True)
                last.then_inc(s_sp, 1)

            @block.vector
            def _(dve):
                for n, (g, _, evacs) in enumerate(steps):
                    if n_dve[n]:
                        dve.wait_ge(s_pe, n + 1)
                        dve.drain()
                    for e, f in evacs:
                        if e == "dve":
                            f().then_inc(s_dve, 1)
                        elif e == "drain":
                            dve.drain()
                dve.wait_ge(s_act, sum(n_act))
                nc.vector.tensor_copy(S[:, 0, :], R.Z[:, 0, :]).then_inc(s_sv, 1)
                for c in range(1, NCH - 1):
                    dve.wait_ge(s_sp, c)
                    nc.vector.tensor_tensor(S[:, c % 2, :], K.bank[c % 2][:, 0:P], R.Z[:, c, :], ALU.add).then_inc(s_sv, 1)
                dve.wait_ge(s_sp, NCH - 1)
                nc.vector.tensor_copy(yout[:, 0:C], R.Y[:, 0:C])
                nc.vector.tensor_tensor(yout[:, C:T], K.bank[2][:, C:T], R.Y[:, C:T], ALU.add)

            @block.scalar
            def _(act):
                for n, (g, _, evacs) in enumerate(steps):
                    if n_act[n]:
                        act.wait_ge(s_pe, n + 1)
                    for e, f in evacs:
                        if e == "act":
                            f().then_inc(s_act, 1)


def rwkv_finish_stage(K, M, y):
    nc, io = K.nc, K.io
    with stage(K, "rfin") as st:
        wg = st.sb("wg", [P, 512])
        wg2 = st.sb("wg2", [32, 512])
        sq = st.sb("sq", [P, 2, T])
        rs = st.sb("rs", [P, 2, T])
        s_w, s_mean, s_yc, s_sq, s_var, s_root, s_rk, s_bonus, s_done = st.sems(
            "w", "mean", "centred", "square", "var", "root", "rk", "bonus", "done")
        with nc.Block() as block:
            @block.sync
            def _(sp):
                sp.dma_start(wg[:, :], io["w_gate_up"][0, 0:P, :]).then_inc(s_w, 16)
                sp.dma_start(wg2[:, :], io["w_gate_up"][0, P:P + 32, :]).then_inc(s_w, 16)

            @block.tensor
            def _(pe):
                pe.wait_ge(s_w, 32)
                for p in range(4):
                    b = 4 * (p % 2)
                    if p >= 2:
                        pe.wait_ge(s_done, p - 1)
                    pe.matmul(K.bank[b][:, :], K.k("heads"), y[:, 4 + p, :], start=True, stop=True).then_inc(s_mean, 1)
                    pe.wait_ge(s_rk, p + 1)
                    pe.matmul(K.bank[b + 1][:, :], K.k("heads"), K.h[:, p, :], start=True, stop=True)
                    pe.matmul(K.bank[b + 2][:, :], wg[:, p * P:(p + 1) * P], M.g[:, :], start=True, stop=False)
                    pe.matmul(K.bank[b + 2][:, :], wg2[:, p * P:(p + 1) * P], M.g2[:, :], start=False, stop=True).then_inc(s_bonus, 1)
                    pe.wait_ge(s_sq, p + 1)
                    pe.matmul(K.bank[b + 3][:, :], K.k("heads"), sq[:, p % 2, :], start=True, stop=True).then_inc(s_var, 1)

            @block.scalar
            def _(act):
                for p in range(4):
                    act.wait_ge(s_yc, p + 1)
                    if p >= 2:
                        act.wait_ge(s_var, p - 1)
                        act.wait_ge(s_done, p - 1)
                    nc.scalar.activation(sq[:, p % 2, :], y[:, 4 + p, :], ACT.Square).then_inc(s_sq, 1)
                    act.wait_ge(s_var, p + 1)
                    nc.scalar.activation(rs[:, p % 2, :], K.bank[4 * (p % 2) + 3][:, :], ACT.Sqrt, bias=K.k("eps")[:, 1:2],
                                         scale=1.0 / HD).then_inc(s_root, 1)

            @block.vector
            def _(dve):
                for p in range(4):
                    nc.vector.scalar_tensor_tensor(K.h[:, p, :], M.rkv[:, p, :], K.p("r_k", p), M.rkv[:, 4 + p, :],
                                                   ALU.mult, ALU.mult).then_inc(s_rk, 1)
                for p in range(4):
                    b = 4 * (p % 2)
                    yt = y[:, 4 + p, :]
                    dve.wait_ge(s_mean, p + 1)
                    nc.vector.scalar_tensor_tensor(yt, K.bank[b][:, :], -1.0 / HD, yt, ALU.mult, ALU.add).then_inc(s_yc, 1)
                    dve.wait_ge(s_bonus, p + 1)
                    nc.vector.tensor_tensor(M.rkv[:, p, :], K.bank[b + 1][:, :], M.rkv[:, 8 + p, :], ALU.mult)
                    dve.wait_ge(s_root, p + 1)
                    nc.vector.reciprocal(rs[:, p % 2, :], rs[:, p % 2, :])
                    dve.drain()
                    nc.vector.scalar_tensor_tensor(yt, yt, K.p("ln_x_gain", p), rs[:, p % 2, :], ALU.mult, ALU.mult)
                    dve.drain()
                    nc.vector.scalar_tensor_tensor(yt, yt, K.p("ln_x_bias", p), M.rkv[:, p, :], ALU.add, ALU.add)
                    dve.drain()
                    nc.vector.tensor_tensor(yt, yt, K.bank[b + 2][:, :], ALU.mult).then_inc(s_done, 1)


def rwkv(K, M, y):
    nc = K.nc
    with ExitStack() as st:
        sb = lambda n, shape: st.enter_context(nc.sbuf_tensor(n, shape, F32))
        R = Bag()
        with ExitStack() as inner:
            isb = lambda n, shape: inner.enter_context(nc.sbuf_tensor(n, shape, F32))
            R.wl, R.oka, R.eP, R.rt = isb("wl", [P, 512]), isb("oka", [P, 1]), isb("eP", [P, T]), isb("rt", [P, T])
            R.bd = isb("bd", [P, 6, NCH, P])
            R.M = y[:, 0:2, :].rearrange("p a (c j) -> p (a c) j", j=P)
            R.Z = y[:, 2:4, :].rearrange("p a (c j) -> p (a c) j", j=P)
            R.Q, R.Y = K.h[:, 0, :], K.h[:, 1, :]
            for p in range(4):
                rwkv_prep_stage(K, M, R, p)
                rwkv_chunk_stage(K, R, p, y[:, 4 + p, :])
        rwkv_finish_stage(K, M, y)


PAD = 16


def ab_in_stage(K, B, norm):
    nc, io = K.nc, K.io
    tiles = []
    for n in range(12):
        dst = B.u[:, n, PAD:] if n < 4 else (B.q if n < 8 else B.k)[:, n % 4, :]
        tiles.append(("ab_in", n // 2, n % 2, WC, feature_pairs((n % 2) * P), (P, T),
                      copier(nc, dst, HD ** -0.5 if n // 4 == 1 else None), SLOT))
    for j in range(2):
        for b in range(TB):
            tiles.append(("ab_v", j, b, WC, token_pairs(b), (P, WC), copier(nc, B.v[:, b, j * WC:(j + 1) * WC]), SLOT))
    wf = B.wf
    box = {}

    def sems(st):
        box["w"], box["pe"] = st.sems("wf", "f")

    def sync(sp):
        sp.dma_start(wf[:, :, :], io["ab_w_in_2"][0].rearrange("(k p) n -> p k n", p=P)[:, :, AB_F:AB_F + 8]).then_inc(box["w"], 16)

    def tensor(pe):
        pe.wait_ge(box["w"], 16)
        product(pe, K.bank[7][0:8, :], [(wf[:, k, :], K.h[:, k, :]) for k in range(KD)]).then_inc(box["pe"], 1)

    def vector(dve):
        dve.wait_ge(box["pe"], 1)
        nc.vector.tensor_scalar(B.z[:, :], K.bank[7][0:8, :], K.p("ab_b_forget_2")[0:8, :], None, ALU.add)

    linear_stage(K, "abin", tiles, banks=7, extra={"sems": sems, "sync": sync, "tensor": tensor, "vector": vector}, norm=norm)


def fox_prep_stage(K, B, y):
    nc, io = K.nc, K.io
    with stage(K, "foxprep") as st:
        e, l, one = st.sb("e", [8, T]), st.sb("l", [8, T]), st.sb("one", [8, T])
        inv = st.sb("inv", [P, 4, T])
        wp = st.sb("wp", [P, 4, P])
        acc = st.sb("acc", [P, 2, T + PAD])
        dif = st.sb("dif", [P, 4, T])
        s_w, s_z, s_exp, s_e1, s_ln, s_F, s_pe, s_ev, s_dif, s_pool, s_pp = st.sems(
            "w", "z", "exp", "e1", "ln", "F", "turned", "out", "dif", "pool", "pooled")
        with nc.Block() as block:
            @block.sync
            def _(sp):
                for g in range(4):
                    sp.dma_start(inv[:, g, :], io["window"][g].partition_broadcast(P)).then_inc(s_w, 16)
                sp.dma_start(wp[:, :, :], io["pool_w_2"][0].rearrange("g k n -> k g n")).then_inc(s_w, 16)

            @block.gpsimd
            def _(pool):
                nc.gpsimd.memset(B.u[:, :, 0:PAD], 0.0)
                nc.gpsimd.memset(acc[:, :, 0:PAD], 0.0)
                pool.drain()
                pool.wait_ge(s_w, 80)
                for g in range(4):
                    cur = B.u[:, g, :]
                    for n in range(g + 1):
                        d = 1 << n
                        nc.gpsimd.tensor_tensor(acc[:, n % 2, PAD:], cur[:, PAD:], cur[:, PAD - d:T + PAD - d], ALU.add)
                        pool.drain()
                        cur = acc[:, n % 2, :]
                    nc.gpsimd.tensor_tensor(dif[:, g, :], cur[:, PAD:], inv[:, g, :], ALU.mult)
                    pool.drain()
                    nc.gpsimd.tensor_tensor(dif[:, g, :], dif[:, g, :], B.u[:, g, PAD:], ALU.subtract).then_inc(s_pool, 1)

            @block.scalar
            def _(act):
                act.wait_ge(s_z, 1)
                nc.scalar.activation(e[:, :], e[:, :], ACT.Exp).then_inc(s_exp, 1)
                act.wait_ge(s_e1, 1)
                nc.scalar.activation(l[:, :], e[:, :], ACT.Ln).then_inc(s_ln, 1)
                act.wait_ge(s_pe, 1)
                nc.scalar.copy(B.F[:, :], K.bank[0][:, 0:32])
                for h in range(8):
                    act.wait_ge(s_pe, 2 + h)
                    nc.scalar.copy(B.nF[:, h, :], K.bank[1 + h % 2][:, :]).then_inc(s_ev, 1)

            @block.vector
            def _(dve):
                nc.vector.tensor_scalar(e[:, :], B.z[:, :], -1.0, None, ALU.mult)
                nc.vector.memset(one[:, :], 1.0)
                dve.drain()
                nc.vector.tensor_tensor(e[:, :], e[:, :], B.z[:, :], ALU.min).then_inc(s_z, 1)
                dve.wait_ge(s_exp, 1)
                nc.vector.tensor_scalar(e[:, :], e[:, :], 1.0, None, ALU.add).then_inc(s_e1, 1)
                dve.wait_ge(s_ln, 1)
                nc.vector.scalar_tensor_tensor(l[:, :], B.z[:, :], 0.0, l[:, :], ALU.min, ALU.subtract)
                dve.drain()
                nc.vector.tensor_tensor_scan(B.z[:, :], one[:, :], l[:, :], 0.0, ALU.mult, ALU.add)
                dve.drain()
                nc.vector.tensor_scalar(e[:, :], B.z[:, :], -1.0, None, ALU.mult).then_inc(s_F, 1)
                for g in range(4):
                    dve.wait_ge(s_pp, g + 1)
                    nc.vector.tensor_scalar(y[:, g, :], K.bank[4 + g][:, :], K.p("pool_scale_2", g), None, ALU.mult)

            @block.tensor
            def _(pe):
                pe.wait_ge(s_F, 1)
                for b in range(TB):
                    last = pe.transpose(K.bank[0][:, 8 * b:8 * b + 8], B.z[:, b * P:(b + 1) * P], K.k("ident")[0:8, 0:8])
                last.then_inc(s_pe, 1)
                for h in range(8):
                    if h >= 2:
                        pe.wait_ge(s_ev, h - 1)
                    pe.matmul(K.bank[1 + h % 2][:, :], K.k("ident")[0:8, h:h + 1].broadcast_to([8, P]), e[:, :],
                              start=True, stop=True).then_inc(s_pe, 1)
                for g in range(4):
                    pe.wait_ge(s_pool, g + 1)
                    pe.matmul(K.bank[4 + g][:, :], wp[:, g, :], dif[:, g, :], start=True, stop=True).then_inc(s_pp, 1)


def mixer2(K, norm):
    nc = K.nc
    with ExitStack() as st:
        sb = lambda n, shape: st.enter_context(nc.sbuf_tensor(n, shape, F32))
        B = Bag()
        B.q, B.k, B.v, B.F = sb("fq", [P, 4, T]), sb("fk", [P, 4, T]), sb("fv", [P, TB, 512]), sb("fF", [P, 32])
        B.nF = sb("fnF", [P, 8, T])
        y = K.h
        with ExitStack() as inner:
            isb = lambda n, shape: inner.enter_context(nc.sbuf_tensor(n, shape, F32))
            B.u, B.wf, B.z = isb("fu", [P, 4, T + PAD]), isb("fwf", [P, KD, 8]), isb("fz", [8, T])
            ab_in_stage(K, B, norm)
            fox_prep_stage(K, B, y)

        def prep(pool, out, h, i):
            w = (i + 1) * P
            nc.gpsimd.tensor_scalar(out, B.nF[:, h, 0:w], B.F[:, 8 * i + h:8 * i + h + 1], None, ALU.add)
            pool.drain()
            return nc.gpsimd.tensor_tensor(out[:, w - P:w], out[:, w - P:w], K.k("causal")[:, T - P:T], ALU.add)

        r = lambda h: slice((h % 2) * 64, (h % 2) * 64 + 64)
        attention_stage(K, "fox", 8, HD, lambda h, i: B.q[r(h), h // 2, i * P:(i + 1) * P], lambda h, w: B.k[r(h), h // 2, 0:w],
                        lambda h, s: B.v[:, s, h * 64:(h + 1) * 64], 64, lambda h, i: y[r(h), 4 + h // 2, i * P:(i + 1) * P], prep=prep)
        out_stage(K, "ab_out", lambda k: y[:, k, :], True)


ROPE = 32
QK = 96
MH = 16
TWO_PI_HI = 6.28125
TWO_PI_MID = float(np.float32(int((2 * math.pi - 6.28125) * 2 ** 20) / 2 ** 20))
TWO_PI_LO = 2 * math.pi - TWO_PI_HI - TWO_PI_MID
ROUND = 12582912.0


def mla_in_stage(K, B, norm):
    nc, io = K.nc, K.io
    w_in = io["mla_w_in_2"][0].rearrange("(k p) n -> p k n", p=P)
    tiles = [("mla_q", 0, m, WC, feature_pairs(m * P), (P, T), copier(nc, B.cq[:, m, :]), SLOT) for m in range(2)]
    tiles.append(("mla_kv", 0, 0, P, feature_pairs(0), (P, T), copier(nc, B.ckv[:, :]), KD * P))
    box = {}
    R = slice(64, 96)

    def sems(st):
        box["w"], box["pe"], box["pos"], box["ang"], box["sin"], box["rope"] = st.sems("wr", "rope", "pos", "angle", "sin", "rotated")
        box["wr"] = st.sb("wr", [P, KD, 2 * ROPE])
        box["pos_i"] = st.sb("pos_i", [P, T], I32)
        box["ang_t"], box["turn"] = st.sb("ang", [P, T]), st.sb("turn", [P, T])

    def sync(sp):
        for a, b in ((0, 384), (16, 400), (32, 400), (48, 384)):
            sp.dma_start(box["wr"][:, :, a:a + 16], w_in[:, :, b:b + 16]).then_inc(box["w"], 16)
        sp.dma_start(box["pos_i"][:, :], io["positions_2"][0].partition_broadcast(P)).then_inc(box["pos"], 16)

    def tensor(pe):
        pe.wait_ge(box["w"], 64)
        for n in range(2):
            product(pe, K.bank[5 + n][R, :], [(box["wr"][:, k, n * ROPE:(n + 1) * ROPE], K.h[:, k, :]) for k in range(KD)]
                    ).then_inc(box["pe"], 1)

    def before(dve):
        ang, turn = box["ang_t"], box["turn"]
        dve.wait_ge(box["pos"], 16)
        nc.vector.tensor_copy(ang[:, :], box["pos_i"][:, :])
        dve.drain()
        nc.vector.tensor_scalar(ang[:, :], ang[:, :], K.k("freq")[:, 0:1], None, ALU.mult)
        dve.drain()
        nc.vector.tensor_scalar(turn[:, :], ang[:, :], 1.0 / (2 * math.pi), ROUND, ALU.mult, ALU.add)
        dve.drain()
        nc.vector.tensor_scalar(turn[:, :], turn[:, :], ROUND, None, ALU.subtract)
        dve.drain()
        for part in (TWO_PI_HI, TWO_PI_MID, TWO_PI_LO):
            nc.vector.scalar_tensor_tensor(ang[:, :], turn[:, :], -part, ang[:, :], ALU.mult, ALU.add)
            dve.drain()
        nc.vector.tensor_scalar(ang[:, :], ang[:, :], 3.1415925, -3.1415925, ALU.min, ALU.max).then_inc(box["ang"], 1)

    def scalar(act):
        act.wait_ge(box["ang"], 1)
        nc.scalar.activation(B.sin[:, :], box["ang_t"][:, :], ACT.Sin)
        nc.scalar.activation(B.cos[:, :], box["ang_t"][:, :], ACT.Sin, scale=0.5).then_inc(box["sin"], 1)

    def vector(dve):
        dve.wait_ge(box["sin"], 1)
        nc.vector.tensor_tensor(B.cos[:, :], B.cos[:, :], B.cos[:, :], ALU.mult)
        nc.vector.tensor_scalar(B.sin[:, :], B.sin[:, :], K.k("freq")[:, 1:2], None, ALU.mult)
        dve.drain()
        nc.vector.tensor_scalar(B.cos[:, :], B.cos[:, :], -2.0, 1.0, ALU.mult, ALU.add)
        dve.drain()
        dve.wait_ge(box["pe"], 2)
        nc.vector.tensor_tensor(B.kr[R, :], K.bank[5][R, :], B.cos[R, :], ALU.mult)
        nc.vector.tensor_tensor(box["turn"][R, :], K.bank[6][R, :], B.sin[R, :], ALU.mult)
        dve.drain()
        nc.vector.tensor_tensor(B.kr[R, :], B.kr[R, :], box["turn"][R, :], ALU.add)

    linear_stage(K, "mlain", tiles, banks=4, scalar=lambda t: True,
                 extra={"sems": sems, "sync": sync, "tensor": tensor, "scalar": scalar, "before": before, "vector": vector}, norm=norm)


def mla_loads(K, B, sp):
    io = K.io
    sp.dma_start(B.wq[:, :, :], io["mla_w_q_b_2"][0].rearrange("(k p) n -> p k n", p=P)).then_inc(K.mla_weights_in, 16)
    for part in range(2):
        sp.dma_start(B.wkv[:, part * 1024:(part + 1) * 1024].rearrange("p (h d) -> p h d", d=64),
                     io["mla_w_kv_b_2"][0].rearrange("p (h two d) -> p two h d", two=2, d=64)[:, part]).then_inc(K.mla_weights_in, 16)


def mla_prep_stage(K, B):
    nc, io = K.nc, K.io
    R = slice(64, 96)
    swap = K.h
    with stage(K, "mlaprep") as st:
        wq, wkv = B.wq, B.wkv
        s_pe, s_v, s_s, s_swap, s_q, s_rot, s_cos = st.sems("pe", "vector_out", "scalar_out", "swapped", "q", "rotated", "cos_part")
        steps = []
        for h in range(MH):
            steps.append((QK, T, [(wq[:, k, h * QK:(h + 1) * QK], B.cq[:, k, :]) for k in range(2)], B.Q[0:QK, h, :], QK ** -0.5))
        for h in range(0, MH, 2):
            steps.append((P, T, [(wkv[:, h * 64:(h + 2) * 64], B.ckv[:, :])], (B.K[0:64, h, :], B.K[0:64, h + 1, :]), None))
        for b in range(TB):
            for half in range(2):
                steps.append((P, T, [(B.ckv[:, b * P:(b + 1) * P], wkv[:, 1024 + half * 512:1536 + half * 512])],
                              B.V[:, b, half * 512:(half + 1) * 512], None))
        with nc.Block() as block:
            @block.sync
            def _(sp):
                for g in range(4):
                    sp.wait_ge(s_v, 2 * g + 2)
                    sp.wait_ge(s_s, 2 * g + 2)
                    if g >= 2:
                        sp.wait_ge(s_rot, g - 1)
                    o = 4 * (g % 2)
                    sp.dma_start(swap[64:80, o:o + 4, :], B.Q[80:96, 4 * g:4 * g + 4, :]).then_inc(s_swap, 16)
                    sp.dma_start(swap[80:96, o:o + 4, :], B.Q[64:80, 4 * g:4 * g + 4, :]).then_inc(s_swap, 16)
                    sp.wait_ge(s_swap, 32 * g + 32)
                    sp.sem_inc(s_q, 1)

            @block.tensor
            def _(pe):
                pe.wait_ge(K.mla_weights_in, 48)
                for t, (rows, _, pairs, _, _) in enumerate(steps):
                    if t >= 8:
                        pe.wait_ge(s_s if t % 2 else s_v, (t - 8) // 2 + 1)
                    product(pe, K.bank[t % 8][0:rows, :], pairs).then_inc(s_pe, 1)

            wide = lambda ap: ap[R, :].unsqueeze(1).broadcast_to([ROPE, 4, T])
            turned = lambda g: (B.Q[R, 4 * g:4 * g + 4, :], swap[R, 4 * (g % 2):4 * (g % 2) + 4, :])

            def rotate(g):
                q, w = turned(g)
                nc.vector.wait_ge(s_q, g + 1)
                nc.vector.tensor_tensor(w, w, wide(B.sin), ALU.mult)
                nc.vector.drain()
                nc.vector.wait_ge(s_cos, g + 1)
                nc.vector.tensor_tensor(q, q, w, ALU.add).then_inc(s_rot, 1)

            def evacuate(e, side):
                for t, (rows, _, _, dst, scale) in enumerate(steps):
                    if side == 0 and t >= 12 and t % 4 == 0 and t // 4 - 3 < 4:
                        rotate(t // 4 - 3)
                    if t % 2 == side:
                        e.wait_ge(s_pe, t + 1)
                        if isinstance(dst, tuple):
                            copier(nc, dst[0])(K.bank[t % 8][0:64, :], "scalar" if side else "vector")
                            dst, rows = dst[1], slice(64, P)
                        else:
                            rows = slice(0, rows)
                        copier(nc, dst, scale)(K.bank[t % 8][rows, :], "scalar" if side else "vector").then_inc(s_s if side else s_v, 1)

            @block.scalar
            def _(act):
                nc.scalar.copy(B.K[R, :, :], B.kr[R, :].unsqueeze(1).broadcast_to([ROPE, MH, T]))
                evacuate(act, 1)

            @block.vector
            def _(dve):
                evacuate(dve, 0)

            @block.gpsimd
            def _(pool):
                for g in range(4):
                    pool.wait_ge(s_q, g + 1)
                    q, _ = turned(g)
                    nc.gpsimd.tensor_tensor(q, q, wide(B.cos), ALU.mult).then_inc(s_cos, 1)


def mixer3(K, norm):
    nc = K.nc
    with ExitStack() as st:
        sb = lambda n, shape: st.enter_context(nc.sbuf_tensor(n, shape, F32))
        B = Bag()
        B.cq, B.ckv, B.sin, B.cos, B.kr = sb("mcq", [P, 2, T]), sb("mckv", [P, T]), sb("msin", [P, T]), sb("mcos", [P, T]), sb("mkr", [P, T])
        mla_in_stage(K, B, norm)
        with ExitStack() as inner:
            isb = lambda n, shape: inner.enter_context(nc.sbuf_tensor(n, shape, F32))
            B.V = isb("mV", [P, TB, 1024])
            B.Q, B.K = isb("mQ", [QK, MH, T]), isb("mK", [QK, MH, T])
            mla_body(K, B)
        out_stage(K, "mla_out", lambda k: K.h[:, k, :], True)


def mla_body(K, B):
    nc = K.nc
    with ExitStack() as st:
        with ExitStack() as inner:
            isb = lambda n, shape: inner.enter_context(nc.sbuf_tensor(n, shape, F32))
            B.wq, B.wkv = isb("mwq", [P, 2, MH * QK]), isb("mwkv", [P, MH * P])
            norm_stage(K, "norm_mla", loads=lambda sp: mla_loads(K, B, sp), jobs=[small_job(K, [B.cq[:, 0, :], B.cq[:, 1, :]], [K.p("mla_q_norm_2", 0), K.p("mla_q_norm_2", 1)], 256),
                                       small_job(K, [B.ckv[:, :]], [K.p("mla_kv_norm_2")], 128)])
            mla_prep_stage(K, B)
        y = K.h
        r = lambda h: slice((h % 2) * 64, (h % 2) * 64 + 64)
        attention_stage(K, "mla", MH, QK, lambda h, i: B.Q[:, h, i * P:(i + 1) * P], lambda h, w: B.K[:, h, 0:w],
                        lambda h, s: B.V[:, s, h * 64:(h + 1) * 64], 64, lambda h, i: y[r(h), h // 2, i * P:(i + 1) * P],
                        bias=lambda h, i: K.k("chunked")[:, 384 - i * P:384 - i * P + (i + 1) * P])


def build(nc, io):
    plan = Plan()

    def cols(w, a, width):
        v = w.rearrange("(k p) n -> p k n", p=P)
        return lambda c: v[:, :, a + width * c:a + width * (c + 1)]

    def ffn(name, *weights):
        parts = [w.rearrange("(k p) n -> p k n", p=P) for w in weights]
        plan.add(name, 34, lambda c: ffn_chunk(*parts, c))
        if name in plan.segments:
            plan.segments[name]["parts"] = parts

    w_in = io["w_in"][0]
    plan.add("mod1", 8, cols(io["ada_w"][0], 0, WC), marks=1, split=False)
    plan.add("in_q", 1, cols(w_in, 0, WC))
    plan.add("in_kv", 1, cols(w_in, O_KV, P), marks=1)
    plan.add("in_rkv", 6, cols(w_in, O_R, WC))
    plan.add("in_lora", 1, cols(w_in, O_WA, WC))
    plan.add("in_lora2", 1, cols(w_in, O_WA + WC, 32), marks=1)
    for p in range(4):
        plan.add(f"mod2_{p}", 1, cols(io["ada_w"][0], 2048 + p * WC, WC), marks=1, split=False)
    plan.add("mod3", 12, cols(io["ada_w"][0], 2048 + 4 * WC, WC), marks=1, split=False)
    plan.add("out1", 4, cols(io["w_out"][0], 0, WC))
    ffn("ffn1", io["w_ffn_gate"][0], io["w_ffn_up"][0], io["w_ffn_down"][0])

    def ffn2(name, l, i):
        ffn(name, io["ffn_w_gate_2"][l, i], io["ffn_w_up_2"][l, i], io["ffn_w_down_2"][l, i])

    ffn2("ffn2", 0, 0)
    plan.add("ab_in", 6, cols(io["ab_w_in_2"][0], 0, WC))
    plan.add("ab_v", 2, cols(io["ab_w_in_2"][0], 1536, WC), marks=4)
    plan.add("ab_out", 4, cols(io["ab_w_out_2"][0], 0, WC))
    ffn2("ffn3", 0, 1)
    ffn2("ffn4", 1, 0)
    plan.add("mla_q", 1, cols(io["mla_w_in_2"][0], 0, WC))
    plan.add("mla_kv", 1, cols(io["mla_w_in_2"][0], 256, P), marks=1)
    plan.add("mla_out", 4, cols(io["mla_w_out_2"][0], 0, WC))
    ffn2("ffn5", 1, 1)

    with ExitStack() as ctx:
        K = Core(nc, ctx, io, plan)
        par, coef, mod = K.p, K.coef, K.mod
        gain = lambda name, at=0: (lambda i: par(name, at + i), None)
        steps = [
            ("mod1", lambda: mod_stage(K)),
            ("mix1", lambda: mixer1(K, (lambda i: coef[:, 8 + i:9 + i], lambda i: mod[:, i:i + 1]))),
            ("x1", lambda: residual_norm(K, "post1", lambda i: coef[:, 16 + i:17 + i])),
            ("f1", lambda: ffn_stage(K, "ffn1", False, (lambda i: coef[:, 24 + i:25 + i], lambda i: mod[:, 24 + i:25 + i]))),
            ("x2", lambda: residual_norm(K, "post2", lambda i: coef[:, 32 + i:33 + i])),
            ("x3", lambda: ffn_stage(K, "ffn2", True, gain("norm_ffn_2"))),
            ("x4", lambda: mixer2(K, gain("norm_mix_2"))),
            ("x5", lambda: ffn_stage(K, "ffn3", True, gain("norm_ffn_2", 8))),
            ("x6", lambda: ffn_stage(K, "ffn4", True, gain("norm_ffn_2", 16))),
            ("x7", lambda: mixer3(K, gain("norm_mix_2", 8))),
            ("x8", lambda: ffn_stage(K, "ffn5", True, gain("norm_ffn_2", 24))),
            ("out", lambda: finish_stage(K)),
        ]
        start_stage(K, None)
        for _, step in steps:
            step()


def const_table():
    t = np.zeros((P, CONST_W), np.float32)

    def put(name, v):
        a, b = CONST[name]
        t[:, a:b] = v

    i, j = np.arange(P)[:, None], np.arange(P)[None, :]
    same = (i // C) == (j // C)
    ii, jj = i % C, j % C
    put("ident", i == j)
    put("flip", i + j == P - 1)
    put("ones", 1.0)
    put("heads", same)
    for s in LEVELS:
        low = same & (ii // (2 * s) == jj // (2 * s)) & (ii // s > jj // s)
        put("first" if s == 1 else f"low{s}", low)
        if s == 1:
            put("first_t", low.T)
    put("strict", same & (ii < jj))
    put("upto", np.arange(P)[:, None] % C <= np.arange(C)[None, :])
    x = np.arange(T)[None, :]
    put("causal", np.where(x - 384 > i, -BIG, 0.0))
    put("chunked", np.where((x - 384) // C > i // C, -BIG, 0.0))
    put("reset", x % C != 0)
    put("eps", np.array([EPS, GN_EPS, 0.0, 0.0], np.float32)[None, :])
    inv = (np.float32(10000.0) ** (-np.arange(0, 32, 2, dtype=np.float32) / np.float32(32))).astype(np.float32)
    put("freq", np.stack([np.tile(inv, 8), np.where(np.arange(P) % 32 < 16, -1.0, 1.0)], 1))
    return t


def bucket_table():
    d = np.arange(T)
    nf = np.maximum(d, 1).astype(np.float32)
    large = 16 + (np.log(nf / np.float32(16)) / np.float32(math.log(8.0)) * np.float32(16)).astype(np.int32)
    b = np.where(d < 16, d, np.minimum(large, 31))
    t = (b[None, ::-1] == np.arange(32)[:, None]).astype(np.float32)
    return np.concatenate([t, np.zeros((32, P), np.float32)], 1)


def window_table():
    n = np.arange(T) + 1
    return np.stack([(np.float32(1.0) / np.minimum(n, w).astype(np.float32)) for w in (2, 4, 8, 16)]).astype(np.float32)


TABLES = {"const": const_table, "bucket": bucket_table, "window": window_table}
INS = ["x", "c", "rel_bias", "ada_w", "ada_b", "mix_pre_norm", "mix_post_norm", "ffn_pre_norm", "ffn_post_norm",
       "w_in", "q_norm", "w_uq", "w_idx_q", "kv_norm", "idx_k_norm", "w_uk", "w_uv", "mu_shift", "w0", "w_decay_up",
       "a0", "w_aaa_up", "w_gate_up", "k_k", "k_a", "r_k", "ln_x_gain", "ln_x_bias", "w_out", "w_ffn_gate",
       "w_ffn_up", "w_ffn_down", "positions_2", "norm_ffn_2", "norm_mix_2", "norm_final_2", "ffn_w_gate_2",
       "ffn_w_up_2", "ffn_w_down_2", "ab_w_in_2", "ab_b_forget_2", "pool_w_2", "pool_scale_2", "ab_w_out_2",
       "mla_w_in_2", "mla_q_norm_2", "mla_kv_norm_2", "mla_w_q_b_2", "mla_w_kv_b_2", "mla_w_out_2"]


def kernel(**inputs):
    import concourse.bacc as bacc
    from concourse.bass_utils import run_bass_kernel_spmd

    nc = bacc.Bacc("TRN2", target_bir_lowering=False, num_devices=1)
    arrays, io = {}, {}
    for name in INS + list(TABLES):
        a = np.ascontiguousarray(inputs[name] if name in inputs else TABLES[name]())
        arrays[f"in_{name}"] = a
        io[name] = nc.dram_tensor(f"in_{name}", a.shape, mybir.dt.from_np(a.dtype), kind="ExternalInput").ap()
    io["out"] = nc.dram_tensor("out", (1, T, D), F32, kind="ExternalOutput").ap()
    build(nc, io)
    r = run_bass_kernel_spmd(nc, [arrays], core_ids=[0])
    return r.results[0]["out"]
```
